# Optimizing a Trainium2 kernel written in Bass

```python
import functools
import jax
import jax.numpy as jnp
from jax import lax
import numpy as np

D_MODEL = 1024
BATCH = 1
SEQ = 512
DEPTH = 1
DEC_BATCH = 8
DEC_SEQ = 8
PAST_LEN = 4096
PAGE_SIZE = 128

HEAD_DIM = 64
N_HEADS_A = 8
WIDTH_A = N_HEADS_A * HEAD_DIM
MOBA_BLOCK = 256
MOBA_TOPK = 3
Q_CHUNK = 128
N_HEADS_B = 8
WIDTH_B = N_HEADS_B * HEAD_DIM
D_DECAY_LORA = 64
D_AAA_LORA = 64
D_GATE_LORA = 128
RWKV_PROJ = 3 * WIDTH_B + D_DECAY_LORA + D_AAA_LORA + D_GATE_LORA
PROJ_W = 3 * WIDTH_A + RWKV_PROJ + 2 * D_MODEL
D_FF = 2816
CONV_W = 3
RMS_EPS = 1e-6
GN_EPS = 64e-5
SPLIT_IN = (WIDTH_A, 2 * WIDTH_A, 3 * WIDTH_A, 3 * WIDTH_A + RWKV_PROJ)
SPLIT_B = (WIDTH_B, 2 * WIDTH_B, 3 * WIDTH_B, 3 * WIDTH_B + D_DECAY_LORA, 3 * WIDTH_B + D_DECAY_LORA + D_AAA_LORA)

kernel_name = 'hybrid_moba_rwkv7_convffn_step'

def rmsnorm(x, g):
    xf = x.astype(jnp.float32)
    y = xf * lax.rsqrt(jnp.mean(xf * xf, axis=-1, keepdims=True) + RMS_EPS)
    return (y * g.astype(jnp.float32)).astype(x.dtype)

def moba_prompt(q, k, v):
    B, S, H, Dh = q.shape
    f32 = jnp.float32
    scale = Dh ** -0.5
    nb = -(-S // MOBA_BLOCK)
    pad = ((0, 0), (0, nb * MOBA_BLOCK - S), (0, 0), (0, 0))
    kb = jnp.pad(k, pad).reshape(B, nb, MOBA_BLOCK, H, Dh)
    vb = jnp.pad(v, pad).reshape(B, nb, MOBA_BLOCK, H, Dh)
    n_sel = min(MOBA_TOPK, nb - 1)
    n_chunk = S // Q_CHUNK
    hix = jnp.arange(H)[:, None, None]
    if n_sel > 0:
        kmean = jnp.mean(kb.astype(f32), axis=2)
        gate = jnp.einsum('bshd,bjhd->bhsj', q.astype(f32), kmean)
        past = jnp.arange(nb)[None, :] < (jnp.arange(S) // MOBA_BLOCK)[:, None]
        _, sel = lax.top_k(jnp.where(past, gate, -jnp.inf), n_sel)

    def chunk_fn(bc):
        b = bc // n_chunk
        q0 = (bc % n_chunk) * Q_CHUNK
        blk = q0 // MOBA_BLOCK
        qc = lax.dynamic_slice_in_dim(q[b], q0, Q_CHUNK, axis=0)
        k_own = kb[b, blk]
        v_own = vb[b, blk]
        qpos = q0 % MOBA_BLOCK + jnp.arange(Q_CHUNK)
        causal = jnp.arange(MOBA_BLOCK)[None, :] <= qpos[:, None]
        l_own = jnp.einsum('qhd,khd->hqk', qc, k_own).astype(f32) * scale
        l_own = jnp.where(causal[None], l_own, -jnp.inf)
        if n_sel == 0:
            p = jax.nn.softmax(l_own, axis=-1)
            o = jnp.einsum('hqk,khd->qhd', p, v_own.astype(f32))
        else:
            sel_c = lax.dynamic_slice_in_dim(sel[b], q0, Q_CHUNK, axis=1)
            k_g = kb[b][sel_c, :, hix]
            v_g = vb[b][sel_c, :, hix]
            l_sel = jnp.einsum('qhd,hqjkd->hqjk', qc, k_g).astype(f32) * scale
            valid = jnp.arange(n_sel) < blk
            l_sel = jnp.where(valid[None, None, :, None], l_sel, -jnp.inf)
            n_g = n_sel * MOBA_BLOCK
            p = jax.nn.softmax(jnp.concatenate([l_sel.reshape(H, Q_CHUNK, n_g), l_own], axis=-1), axis=-1)
            o = (jnp.einsum('hqjk,hqjkd->qhd', p[..., :n_g].reshape(H, Q_CHUNK, n_sel, MOBA_BLOCK), v_g.astype(f32))
                 + jnp.einsum('hqk,khd->qhd', p[..., n_g:], v_own.astype(f32)))
        return o.astype(q.dtype)

    out = lax.map(chunk_fn, jnp.arange(B * n_chunk))
    return out.reshape(B, S, H, Dh)

def moba_sample(q, k, v, cache_k, cache_v, page_table):
    DB, T, H, Dh = q.shape
    f32 = jnp.float32
    scale = Dh ** -0.5
    past_len = page_table.shape[1] * PAGE_SIZE
    ppb = MOBA_BLOCK // PAGE_SIZE
    c = past_len // MOBA_BLOCK
    n_sel = min(MOBA_TOPK, c)
    own_start = c * MOBA_BLOCK
    n_oc = past_len - own_start
    qf = q.astype(f32)
    parts = []
    if n_sel > 0:
        k_full = cache_k[page_table[:, :c * ppb]].astype(f32).reshape(DB, c, MOBA_BLOCK, H, Dh)
        kmean = jnp.mean(k_full, axis=2)
        gate = jnp.einsum('bthd,bjhd->bhtj', qf, kmean)
        _, sel = lax.top_k(gate, n_sel)
        logical = sel[..., None] * ppb + jnp.arange(ppb)
        phys = page_table[jnp.arange(DB)[:, None, None, None, None], logical]
        hix = jnp.arange(H)[None, :, None, None, None]
        k_g = cache_k[phys, :, hix].reshape(DB, H, T, n_sel * MOBA_BLOCK, Dh)
        v_g = cache_v[phys, :, hix].reshape(DB, H, T, n_sel * MOBA_BLOCK, Dh)
        parts.append((jnp.einsum('bthd,bhtkd->bhtk', qf, k_g.astype(f32)), v_g, 'bhtk,bhtkd->bthd'))
    if n_oc > 0:
        pages = page_table[:, own_start // PAGE_SIZE:]
        k_oc = cache_k[pages].reshape(DB, n_oc, H, Dh)
        v_oc = cache_v[pages].reshape(DB, n_oc, H, Dh)
        parts.append((jnp.einsum('bthd,bkhd->bhtk', qf, k_oc.astype(f32)), v_oc, 'bhtk,bkhd->bthd'))
    causal = jnp.tril(jnp.ones((T, T), dtype=bool))
    l_new = jnp.where(causal, jnp.einsum('bthd,bshd->bhts', qf, k.astype(f32)), -jnp.inf)
    parts.append((l_new, v, 'bhts,bshd->bthd'))
    probs = jax.nn.softmax(jnp.concatenate([lp for lp, _, _ in parts], axis=-1) * scale, axis=-1)
    cuts = [int(s) for s in np.cumsum([lp.shape[-1] for lp, _, _ in parts])[:-1]]
    out = jnp.zeros((DB, T, H, Dh), f32)
    for pr, (_, vals, spec) in zip(jnp.split(probs, cuts, axis=-1), parts):
        out = out + jnp.einsum(spec, pr, vals.astype(f32))
    return out.astype(q.dtype)

def rwkv7_branch(pb, prev_row, s0, mu, w0, w2, a0, a2, g2, k_k, k_a, r_k, lnx_g, lnx_b):
    B, T, _ = pb.shape
    f32 = jnp.float32
    H, N = N_HEADS_B, HEAD_DIM
    prev = jnp.concatenate([prev_row[:, None, :].astype(pb.dtype), pb[:, :-1]], axis=1)
    xm = pb + (prev - pb) * mu
    r, k, v, wd, ad, gd = jnp.split(xm, SPLIT_B, axis=-1)
    logw = -jax.nn.softplus(-(w0 + jnp.tanh(wd) @ w2).astype(f32)) - 0.5
    decay = jnp.exp(-jnp.exp(logw))
    a = jax.nn.sigmoid((a0 + ad @ a2).astype(f32))
    g = jax.nn.sigmoid(gd) @ g2
    hd = lambda t: t.astype(f32).reshape(B, T, H, N)
    r, k, v, decay, a = hd(r), hd(k), hd(v), hd(decay), hd(a)
    kk = k * k_k.astype(f32).reshape(H, N)
    kk = kk / jnp.maximum(jnp.linalg.norm(kk, axis=-1, keepdims=True), 1e-12)
    k = k * (1.0 + (a - 1.0) * k_a.astype(f32).reshape(H, N))

    def step(S, inp):
        r_t, w_t, k_t, v_t, a_t, b_t = inp
        sa = jnp.einsum('bhij,bhj->bhi', S, a_t)
        S = S * w_t[:, :, None, :] + sa[..., None] * b_t[:, :, None, :] + v_t[..., None] * k_t[:, :, None, :]
        return S, jnp.einsum('bhij,bhj->bhi', S, r_t)

    tm = lambda t: jnp.swapaxes(t, 0, 1)
    s_fin, y = lax.scan(step, s0.astype(f32), (tm(r), tm(decay), tm(k), tm(v), tm(-kk), tm(kk * a)))
    y = tm(y)
    mean = jnp.mean(y, axis=-1, keepdims=True)
    var = jnp.mean(jnp.square(y - mean), axis=-1, keepdims=True)
    yn = (y - mean) * lax.rsqrt(var + GN_EPS) * lnx_g.astype(f32).reshape(H, N) + lnx_b.astype(f32).reshape(H, N)
    bonus = jnp.sum(r * k * r_k.astype(f32), axis=-1, keepdims=True) * v
    out = (yn + bonus).reshape(B, T, WIDTH_B).astype(pb.dtype) * g
    return out, s_fin, pb[:, -1]

def trunk_layer(x, attend, shift_prev, wkv0, conv_prev, ln1_g, w_in, w_br_a, mu, w0, w2, a0, a2, g2,
                k_k, k_a, r_k, lnx_g, lnx_b, w_br_b, w_o, ln2_g, w_up, conv_w, conv_b, w_down):
    B, T, _ = x.shape
    xn = rmsnorm(x, ln1_g)
    qa, ka, va, pb, gates = jnp.split(xn @ w_in, SPLIT_IN, axis=-1)
    heads = lambda t: t.reshape(B, T, N_HEADS_A, HEAD_DIM)
    qa, ka, va = heads(qa), heads(ka), heads(va)
    y_a = attend(qa, ka, va).reshape(B, T, WIDTH_A) @ w_br_a
    y_b, wkv_new, shift_new = rwkv7_branch(pb, shift_prev, wkv0, mu, w0, w2, a0, a2, g2, k_k, k_a, r_k, lnx_g, lnx_b)
    y_b = y_b @ w_br_b
    g_a, g_b = jnp.split(jax.nn.sigmoid(gates), 2, axis=-1)
    h = x + (g_a * y_a + g_b * y_b) @ w_o
    u = rmsnorm(h, ln2_g) @ w_up
    uc = jnp.concatenate([conv_prev.astype(u.dtype), u], axis=1)
    cv = conv_b
    for i in range(CONV_W):
        cv = cv + uc[:, i:i + T] * conv_w[i]
    val, gt = jnp.split(cv, 2, axis=-1)
    out = h + (jax.nn.silu(gt) * val) @ w_down
    return out, (ka, va, wkv_new, shift_new, uc[:, -(CONV_W - 1):])

def setup_inputs(seed: int = 0) -> dict:
    key = jax.random.key(seed)
    ks = jax.random.split(key, 32)
    f32 = jnp.float32
    nrm = lambda k, shape, s: jax.random.normal(k, shape, f32) * s
    L = DEPTH
    n_pages = PAST_LEN // PAGE_SIZE
    n_used = DEC_BATCH * n_pages
    n_pool = n_used + max(1, n_used // 4)
    page_table = jax.random.permutation(ks[4], n_pool)[:n_used].reshape(DEC_BATCH, n_pages).astype(jnp.int32)
    return {
        'x_prompt': nrm(ks[0], (BATCH, SEQ, D_MODEL), 1.0),
        'x_sample': nrm(ks[1], (DEC_BATCH, DEC_SEQ, D_MODEL), 1.0),
        'cache_k': nrm(ks[2], (L, n_pool, PAGE_SIZE, N_HEADS_A, HEAD_DIM), 1.0),
        'cache_v': nrm(ks[3], (L, n_pool, PAGE_SIZE, N_HEADS_A, HEAD_DIM), 1.0),
        'page_table': page_table,
        'state_wkv': nrm(ks[5], (L, DEC_BATCH, N_HEADS_B, HEAD_DIM, HEAD_DIM), 0.3),
        'state_tshift': nrm(ks[6], (L, DEC_BATCH, RWKV_PROJ), 1.0),
        'state_conv': nrm(ks[7], (L, DEC_BATCH, CONV_W - 1, 2 * D_FF), 1.0),
        'ln1_g': 1.0 + nrm(ks[8], (L, D_MODEL), 0.02),
        'w_in': nrm(ks[9], (L, D_MODEL, PROJ_W), D_MODEL ** -0.5),
        'w_br_a': nrm(ks[10], (L, WIDTH_A, D_MODEL), WIDTH_A ** -0.5),
        'mu': jax.random.uniform(ks[11], (L, RWKV_PROJ), f32),
        'w0': jax.random.uniform(ks[12], (L, WIDTH_B), f32, -5.0, 1.0),
        'w2': nrm(ks[13], (L, D_DECAY_LORA, WIDTH_B), 0.1),
        'a0': nrm(ks[14], (L, WIDTH_B), 0.1),
        'a2': nrm(ks[15], (L, D_AAA_LORA, WIDTH_B), D_AAA_LORA ** -0.5),
        'g2': nrm(ks[16], (L, D_GATE_LORA, WIDTH_B), D_GATE_LORA ** -0.5),
        'k_k': 0.85 + nrm(ks[17], (L, WIDTH_B), 0.05),
        'k_a': 1.0 + nrm(ks[18], (L, WIDTH_B), 0.05),
        'r_k': nrm(ks[19], (L, N_HEADS_B, HEAD_DIM), 0.1),
        'lnx_g': 1.0 + nrm(ks[20], (L, WIDTH_B), 0.02),
        'lnx_b': nrm(ks[21], (L, WIDTH_B), 0.01),
        'w_br_b': nrm(ks[22], (L, WIDTH_B, D_MODEL), WIDTH_B ** -0.5),
        'w_o': nrm(ks[23], (L, D_MODEL, D_MODEL), D_MODEL ** -0.5),
        'ln2_g': 1.0 + nrm(ks[24], (L, D_MODEL), 0.02),
        'w_up': nrm(ks[25], (L, D_MODEL, 2 * D_FF), D_MODEL ** -0.5),
        'conv_w': nrm(ks[26], (L, CONV_W, 2 * D_FF), CONV_W ** -0.5),
        'conv_b': nrm(ks[27], (L, 2 * D_FF), 0.01),
        'w_down': nrm(ks[28], (L, D_FF, D_MODEL), D_FF ** -0.5),
        'lnf_g': 1.0 + nrm(ks[29], (D_MODEL,), 0.02),
    }

def reference(x_prompt, x_sample, cache_k, cache_v, page_table, state_wkv, state_tshift, state_conv,
              ln1_g, w_in, w_br_a, mu, w0, w2, a0, a2, g2, k_k, k_a, r_k, lnx_g, lnx_b, w_br_b, w_o,
              ln2_g, w_up, conv_w, conv_b, w_down, lnf_g):
    bp = x_prompt.shape[0]
    hp, hs = x_prompt, x_sample
    new_p, new_s = [], []
    for l in range(DEPTH):
        lw = (ln1_g[l], w_in[l], w_br_a[l], mu[l], w0[l], w2[l], a0[l], a2[l], g2[l], k_k[l], k_a[l],
              r_k[l], lnx_g[l], lnx_b[l], w_br_b[l], w_o[l], ln2_g[l], w_up[l], conv_w[l], conv_b[l], w_down[l])
        zero_shift = jnp.zeros((bp, RWKV_PROJ), x_prompt.dtype)
        zero_wkv = jnp.zeros((bp, N_HEADS_B, HEAD_DIM, HEAD_DIM), jnp.float32)
        zero_conv = jnp.zeros((bp, CONV_W - 1, 2 * D_FF), x_prompt.dtype)
        hp, st_p = trunk_layer(hp, moba_prompt, zero_shift, zero_wkv, zero_conv, *lw)
        attend_s = functools.partial(moba_sample, cache_k=cache_k[l], cache_v=cache_v[l], page_table=page_table)
        hs, st_s = trunk_layer(hs, attend_s, state_tshift[l], state_wkv[l], state_conv[l], *lw)
        new_p.append(st_p)
        new_s.append(st_s)
    y_prompt = rmsnorm(hp, lnf_g)
    y_sample = rmsnorm(hs, lnf_g)
    k_prompt, v_prompt, wkv_prompt, tshift_prompt, conv_prompt = [jnp.stack(z) for z in zip(*new_p)]
    k_sample, v_sample, wkv_sample, tshift_sample, conv_sample = [jnp.stack(z) for z in zip(*new_s)]
    return (y_prompt, y_sample, k_prompt, v_prompt, wkv_prompt, tshift_prompt, conv_prompt,
            k_sample, v_sample, wkv_sample, tshift_sample, conv_sample)


_drawn_inputs = setup_inputs


def setup_inputs(seed=0):
    import zlib

    import numpy as np

    out = dict(_drawn_inputs(seed))
    spreads = {}
    factors = {'lnx_g': 8.0,
     'lnx_b': 37.854,
     'ln2_g': 2.866,
     'conv_b': 7.903,
     'lnf_g': 8.538,
     'cache_k': 3.331,
     'cache_v': 3.204}
    for name, (base, spread) in spreads.items():
        noise = np.random.default_rng([zlib.crc32(name.encode()), seed]).standard_normal(out[name].shape)
        drawn = base * np.exp(spread * noise) if base else spread * noise
        out[name] = jnp.asarray(drawn.astype(out[name].dtype))
    for name, factor in factors.items():
        out[name] = (out[name] * factor).astype(out[name].dtype)
    return out
```

```python
from contextlib import ExitStack

import numpy as np

import concourse.bass as bass
from concourse import mybir

F32 = mybir.dt.float32
I32 = mybir.dt.int32
ALU = mybir.AluOpType
ACT = mybir.ActivationFunctionType
AX = mybir.AxisListType

P = 128
D = 1024
KT = D // P
SEQ = 512
DB, DT = 8, 8
NS = DB * DT
T = SEQ + NS
HALF = T // 2
HD = 64
HP = 4
WA = 512
NPB = 1792 // P
NG = D // P
DFF = 2816
NF = DFF // P
PAST = 4096
PAGE = 128
NPG = PAST // PAGE
GP = 4
NGRP = NPG // GP
BLK = 256
NBLK = PAST // BLK
TOPK = 3
C = 64
NCH = SEQ // C
SCALE = HD ** -0.5
NEG = -1e30
EPS = 1e-6
GN_EPS = 64e-5
EM05 = float(np.exp(-0.5))
LEVELS = 6
ARENA = 52800

PV = {}
_at = 0
for _n, _w in (("ln1", 8), ("mu", 14), ("w0", 4), ("a0", 4), ("kk", 4), ("ka", 4), ("rk", 4), ("lg", 4),
               ("lb", 4), ("ln2", 8), ("lnf", 8), ("cw0", 44), ("cw1", 44), ("cw2", 44), ("cb", 44)):
    PV[_n] = _at
    _at += _w
NPV = _at

CV = {}
_at = 0
for _n, _w in (("ident", 128), ("ones", 128), ("bones", 128), ("causal", 128), ("eye2", 128),
               ("mp0", 128), ("mp1", 128), ("ms0", 128), ("ms1", 128), ("lvl", LEVELS * 128),
               ("colm", DB * 64), ("rowm", DB), ("newm", DB * 64), ("tri", 256), ("reset", T)):
    CV[_n] = _at
    _at += _w
NCV = _at


def constants():
    c = np.zeros((P, NCV), np.float32)
    p = np.arange(P)
    f = np.arange(P)
    s = (p % 64)[:, None]
    t = np.arange(64)[None, :]

    def put(name, a):
        a = np.asarray(a, np.float32).reshape(P, -1)
        c[:, CV[name]:CV[name] + a.shape[1]] = a

    put("ident", np.eye(P))
    put("ones", np.ones((P, P)))
    put("bones", (p[:, None] // 64) == (f[None, :] // 64))
    put("causal", np.where(f[None, :] <= p[:, None], 0.0, NEG))
    eye = s == t
    put("eye2", np.concatenate([eye, eye], 1))
    same = (s // DT) == (t // DT)
    put("mp0", np.concatenate([t < s, s < t], 1))
    put("mp1", np.concatenate([s < t, s <= t], 1))
    put("ms0", np.concatenate([(t < s) & same, (s < t) & same], 1))
    put("ms1", np.concatenate([(s < t) & same, (s <= t) & same], 1))
    lv = []
    for l in range(LEVELS):
        m = 1 << l
        low = (s // (2 * m) == t // (2 * m)) & ((s // m) % 2 == 1) & ((t // m) % 2 == 0)
        up = (s // (2 * m) == t // (2 * m)) & ((t // m) % 2 == 1) & ((s // m) % 2 == 0)
        lv.append(np.concatenate([low, up], 1))
    put("lvl", np.concatenate(lv, 1))
    b = np.arange(DB)
    put("colm", np.broadcast_to((np.arange(64)[None, :] // DT == b[:, None])[None], (P, DB, 64)))
    put("rowm", ((p % 64) // DT)[:, None] == b[None, :])
    tt = (p % DT)[:, None, None]
    key = np.arange(64)[None, None, :]
    ok = (key // DT == b[None, :, None]) & (key % DT <= tt)
    put("newm", np.where(ok, 0.0, NEG))
    i = np.arange(NBLK)
    put("tri", np.broadcast_to((i[None, :] < i[:, None])[None], (P, NBLK, NBLK)))
    start = np.ones(T)
    start[np.arange(0, SEQ, C)] = 0
    start[np.arange(SEQ, T, DT)] = 0
    put("reset", np.broadcast_to(start[None], (P, T)))
    return c


class Line:

    def __init__(self, eng, sem, base=0):
        self.eng, self.sem, self.base, self.n = eng, sem, base, 0

    def did(self, ins):
        ins.then_inc(self.sem, 1)
        self.n += 1
        return ins

    def settle(self):
        self.eng.wait_ge(self.sem, self.base + self.n)


def build(nc, xin, kcache, vcache, pages, s0t, sshift, sconv, pvec, consts, lora, w_in, w_br, w_o, w_up, w_down,
          yT, kT_out, v_out, vs_out, wkvp, tsh_out, conv_out, wkvs):
    ctx = ExitStack()
    with ctx:
        arena = ctx.enter_context(nc.sbuf_tensor("arena", [P, ARENA], F32))
        ptab = ctx.enter_context(nc.sbuf_tensor("ptab", [1, DB * NPG], I32))
        ps = ctx.enter_context(nc.psum_tensor("ps", [P, 8, 512], F32))

        def sem(name):
            return ctx.enter_context(nc.semaphore(name))

        def sems(name, n):
            return [sem(f"{name}{i}") for i in range(n)]

        def view(at, *shape):
            v = arena[:, at:at + int(np.prod(shape))]
            if len(shape) == 2:
                return v.rearrange("p (a b) -> p a b", a=shape[0])
            if len(shape) == 3:
                return v.rearrange("p (a b c) -> p a b c", a=shape[0], b=shape[1])
            return v

        x = view(0, KT, T)
        xn = view(4608, KT, T)
        wr = [view(9216 + 1024 * i, KT, P) for i in range(4)]
        kring = [view(4608 + 2048 * i, GP, HP, PAGE) for i in range(4)]
        vring = [view(4608 + 2048 * i, GP, WA) for i in range(4)]
        oa = view(13312, HP, T)
        yb = view(15616, HP, T)
        sqb = [view(13312 + T * i, T) for i in range(2)]
        ub = [view(15616 + 600 * i, 600) for i in range(2)]
        df = view(15616 + 1200, 600)
        qk = view(17920, 2 * HP, T)
        tmp = [view(17920 + T * i, T) for i in range(8)]
        s0 = view(17920, HP, DB, 64)
        ex = [view(17920 + 2048 + 512 * i, DB, 64) for i in range(4)]
        lg = view(17920, PAST + NS)
        vp = view(22528, HP, WA)
        vsm = view(22528 + 2048, WA)
        rw = view(25088, 20, T)
        R, K, V, AL, BE = (rw[:, 4 * i:4 * i + 4, :] for i in range(5))
        wad = view(36608, T)
        gd = view(36608 + T, T)
        stg = view(37760, 20, C)
        sR, sK, sV, sA, sB = (stg[:, 4 * i:4 * i + 4, :] for i in range(5))
        aa = view(39040, 2, HP, C)
        mm1 = view(39552, 2, HP, C)
        mkv = view(40064, 2, HP, C)
        bk = view(40576, 2, HP, C)
        tt = view(41088, 2, HP, C)
        amt = view(41600, LEVELS - 1, HP, C)
        xx = view(42880, HP, C)
        ww = view(43136, HP, C)
        uu = view(43392, HP, C)
        st = view(43648, HP, C)
        pr = [view(37760 + 512 * i, SEQ) for i in range(2)]
        prT = [view(37760 + 1024 + 512 * i, HP, P) for i in range(2)]
        at = [43904]

        def take(*shape):
            v = view(at[0], *shape)
            at[0] += int(np.prod(shape))
            return v

        cst = take(NCV)
        pv = take(NPV)
        omka = take(HP)
        shs = take(NPB, DB)
        lo = take(2 * WA)
        w2a2, g2 = lo[:, 0:WA], lo[:, WA:2 * WA]
        qks = take(2 * HP, NS)
        tsh = take(NPB, 9)
        qbd = take(HP, 32)
        lc = take(HP, 16)
        gs = take(16)
        bm = take(17)
        mb = take(17)
        bi = take(17)
        psm = take(17)
        sc = take(8)
        cmp1 = take(16, 16)
        cmp2 = take(16, 16)
        mx = take(8)
        nmx = take(8)
        rsm = take(8)
        rin = take(8)
        pT = [take(GP, P) for _ in range(2)]
        ob = take(P)
        rs = take(T)
        assert at[0] <= ARENA, at[0]
        m = view(25088, KT, T)
        g0 = view(17920, T)
        g1 = view(17920 + T, T)
        hh = view(13312, NF, T)
        wd = [view(25984 + 2816 * i, NF, P) for i in range(2)]
        cu = [view(31616 + 604 * i, 604) for i in range(4)]
        cc = [view(34032 + 592 * i, 592) for i in range(4)]
        scv = view(36400, 2 * NF, DB * 2)
        cvo = view(37104, 2 * NF, 18)

        ident, ones, bones, causal = (cst[:, CV[n]:CV[n] + P] for n in ("ident", "ones", "bones", "causal"))
        reset = cst[:, CV["reset"]:CV["reset"] + T]
        tri = cst[:, CV["tri"]:CV["tri"] + 256].rearrange("p (a b) -> p a b", a=16)
        colm = cst[:, CV["colm"]:CV["colm"] + 512].rearrange("p (a b) -> p a b", a=DB)
        rowm = cst[:, CV["rowm"]:CV["rowm"] + DB]

        def mpair(name, at=0):
            a = CV[name] + at
            return cst[:, a:a + 128].rearrange("p (a o b) -> p a o b", a=2, o=1).to_broadcast([P, 2, HP, C])

        def mone(name, at=0):
            a = CV[name] + at
            return cst[:, a:a + 64].rearrange("p (o b) -> p o b", o=1).to_broadcast([P, HP, C])

        def pcol(name, i):
            if isinstance(i, int):
                return pv[:, PV[name] + i:PV[name] + i + 1]
            return pv[:, bass.ds(i + PV[name], 1)]

        def tile_of(w, i):
            if isinstance(i, int):
                return w[i]
            return w[bass.ds(i, 1)].rearrange("o p k n -> p (o k) n")

        def pair(b):
            return ps[:, 2 * b:2 * b + 2, 0:HALF]

        def lin(a):
            return a.rearrange("p (h n) -> p h n", h=2)

        def lin3(a):
            return a.rearrange("p o (h n) -> p (o h) n", h=2)

        def q4(bank, j=0):
            return ps[:, bank, 256 * j:256 * j + 256].rearrange("p (a b) -> p a b", a=HP)

        def q8(bank):
            return ps[:, bank, :].rearrange("p (c a b) -> p c a b", c=2, a=HP)

        def heads():
            for hp in range(HP):
                for half in range(2):
                    yield hp, slice(64 * half, 64 * half + 64)

        s_c0, s_c1, s_pv, s_pt, s_lora, s_s0, s_sc = (sem(n) for n in (
            "ones_in", "const_in", "params_in", "pages_in", "lora_in", "states_in", "conv_in"))
        s_x = sems("x_in", 4)
        w_a, w_g, w_ob, w_u, w_d = sems("w_in", 4), sems("w_gate", 3), sems("w_o", 4), sems("w_up", 4), sems("w_down", 2)
        kv_in = sems("kv_in", 4)
        sq_ready, sq_used, ms_ready, rt_ready, xn_ready = (sem(n) for n in ("sq_ready", "sq_used", "ms_ready", "rt_ready", "xn_ready"))
        qk_tile, qk_out, v_tile, v_evac, rw_tile, u_ready, xm_done, tsh_done, qks_done = (sem(n) for n in (
            "qk_tile", "qk_out", "v_tile", "v_evac", "rw_tile", "u_ready", "xm_done", "tsh_done", "qks_done"))
        own = {n: sem("own_" + n) for n in ("setup", "shift", "attn", "prep", "chunk0", "loop", "gn", "gate", "up", "norm", "ch0", "chl")}
        init_done = sem("init_done")
        at_lg, at_mx, at_ex, at_pn, at_tp, at_tc, at_pv, at_oe = (sem(n) for n in (
            "at_logits", "at_max", "at_exp", "at_norm", "at_transposed", "at_pt", "at_pv", "at_out"))
        pr_sq, pr_ss, pr_mx, pr_rt, pr_kk, pr_lin, pr_w, pr_sig, pr_exc, pr_exp, pr_b, pr_bp, pr_done = (sem(n) for n in (
            "kk_sq", "kk_ss", "kk_ms", "kk_rt", "kk_done", "lora_act", "lora_mm", "lora_sig", "excl", "decays", "bonus_in", "bonus_mm", "prep_done"))
        ch_stg, ch_g, ch_ev, ch_amt, ch_x, ch_xe, ch_d, ch_te, ch_w, ch_we, ch_u, ch_ue, ch_y, ch_ye, ch_s, st_ready = (sem(n) for n in (
            "c_staged", "c_gram", "c_gram_out", "c_levels", "c_x", "c_x_out", "c_d", "c_t", "c_w", "c_w_out", "c_u", "c_u_out",
            "c_y", "c_y_out", "c_s", "state_ready"))
        ss_ex, ss_w, ss_we, ss_u, ss_ue, ss_y, ss_s, ss_st = (sem(n) for n in (
            "ss_exp", "ss_w", "ss_w_out", "ss_u", "ss_u_out", "ss_y", "ss_s", "ss_state"))
        sa_q, kv_used, sa_ev, sa_lg, sa_bi, sa_ex, sa_tp, sa_tc, sa_nw, sa_ob, sa_ot, sa_oo = (sem(n) for n in (
            "s_q", "kv_used", "s_logits_out", "s_new_logits", "s_bias", "s_exp", "s_transposed", "s_pt", "s_pv_new",
            "s_o", "s_ot", "s_oa"))
        gn_mm, gn_sq, gn_v, gn_rt, gn_out = (sem(n) for n in ("gn_mm", "gn_sq", "gn_var", "gn_rt", "gn_out"))
        ga_mm, ga_sig, m_done = sem("gate_mm"), sem("gate_sig"), sem("m_done")
        ga_free = sems("gate_free", 4)
        o_mm, h_done = sem("o_mm"), sem("h_done")
        up_mm, up_ev, up_st, up_c0, up_cv, up_si, up_h, up_cp, up_z = (sem(n) for n in (
            "up_mm", "up_u", "up_state", "up_c0", "up_cv", "up_silu", "up_h", "up_conv_out", "up_zero"))
        dn_mm, y_done = sem("down_mm"), sem("y_done")
        stored = sem("stored")
        k_stored, ws_stored = sem("k_stored"), sem("wkvs_stored")
        waited = sem("waited")
        N_STORES = 7

        block = ctx.enter_context(nc.Block())

        @block.sync
        def _(e):
            e.dma_start(cst[:, 0:256], consts[:, 0:256]).then_inc(s_c0, 16)
            for i in range(4):
                e.dma_start(x[:, 2 * i:2 * i + 2, :], xin[:, 2 * i:2 * i + 2, :]).then_inc(s_x[i], 16)
            e.dma_start(pv[:, :], pvec).then_inc(s_pv, 16)
            for s in range(4):
                e.dma_start(wr[s], w_in[s]).then_inc(w_a[s], 16)
            e.dma_start(cst[:, 256:NCV], consts[:, 256:NCV]).then_inc(s_c1, 16)
            e.dma_start(shs[:, :, :], sshift).then_inc(s_c1, 16)
            e.dma_start(lo[:, :], lora).then_inc(s_lora, 16)
            e.dma_start(ptab[:, :], pages).then_inc(s_pt, 16)

            def w_tile(i, s, used, n):
                e.wait_ge(used, n)
                e.dma_start(wr[s], tile_of(w_in, i)).then_inc(w_a[s], 16)

            for s in range(4):
                w_tile(4 + s, s, qk_tile, s + 1)
            for s in range(4):
                w_tile(8 + s, s, qk_tile, 4 + s + 1)
            for s in range(4):
                w_tile(12 + s, s, v_tile, s + 1)
            with e.Fori(0, 2) as it:
                for s in range(4):
                    w_tile(it * 4 + (16 + s), s, rw_tile, it * 4 + (s + 1))
            for s in range(2):
                w_tile(24 + s, s, rw_tile, 8 + s + 1)

            e.wait_ge(qk_out, 2 * HP)
            e.dma_start(kT_out, qk[:, HP:2 * HP, :]).then_inc(k_stored, 16)
            e.wait_ge(v_evac, 2 * HP)
            e.dma_start(v_out, vp[:, :, :]).then_inc(stored, 16)
            e.dma_start(vs_out, vsm[0:NS, :]).then_inc(stored, 16)
            e.wait_ge(tsh_done, NPB)
            e.dma_start(tsh_out, tsh[:, :, :]).then_inc(stored, 16)

            e.wait_ge(s_pt, 16)
            e.wait_ge(rw_tile, NPB)

            def page_group(b, g, value, n):
                pgs = [e.value_load(ptab[0:1, bass.ds(b * NPG + (g * GP + q), 1)], min_val=0, max_val=kcache.shape[0] - 1)
                       for q in range(GP)]
                if n is not None:
                    e.wait_ge(kv_used, n)
                for q, pg in enumerate(pgs):
                    slot = (vring if value else kring)[g % 4][:, q:q + 1]
                    slot = slot.rearrange("p o a -> p (o a)") if value else slot.rearrange("p o a b -> p (o a b)")
                    cache = vcache if value else kcache
                    e.dma_start(slot, cache[bass.ds(pg, 1)].rearrange("o p n -> p (o n)")).then_inc(kv_in[g % 4], 16)

            for g in range(4):
                page_group(0, g, False, None)
            e.wait_ge(pr_done, 1)
            e.dma_start(s0[:, :, :, :].rearrange("p a b c -> p (a b c)"), s0t).then_inc(s_s0, 16)
            e.wait_ge(ss_st, HP)
            e.dma_start(wkvs, s0[:, :, :, :].rearrange("p a b c -> p (a b c)")).then_inc(ws_stored, 16)
            for g in range(4, NGRP):
                page_group(0, g, False, g - 3)
            for g in range(NGRP):
                page_group(0, g, True, NGRP + g - 3)
            with e.Fori(1, DB) as b:
                for g in range(NGRP):
                    page_group(b, g, False, b * (2 * NGRP) + (g - 3))
                for g in range(NGRP):
                    page_group(b, g, True, b * (2 * NGRP) + (NGRP + g - 3))

            e.wait_ge(st_ready, NCH + 1)
            e.dma_start(wkvp, st[:, :, :].rearrange("p a b -> p (a b)")).then_inc(stored, 16)
            e.wait_ge(kv_used, 2 * DB * NGRP)
            for s in range(2):
                e.dma_start(wr[s], w_in[26 + 8 * s]).then_inc(w_g[s], 16)
            e.dma_start(wr[2], w_br[0]).then_inc(w_g[2], 16)
            with e.Fori(1, NG) as c:
                for s in range(2):
                    e.wait_ge(ga_mm, c * 4 + (s - 3))
                    e.dma_start(wr[s], tile_of(w_in, c + (26 + 8 * s))).then_inc(w_g[s], 16)
                e.wait_ge(ga_mm, c * 4)
                e.dma_start(wr[2], tile_of(w_br, c)).then_inc(w_g[2], 16)
            e.wait_ge(ga_mm, 4 * NG)
            for s in range(4):
                e.dma_start(wr[s], w_o[s]).then_inc(w_ob[s], 16)
            for s in range(4):
                e.wait_ge(o_mm, s + 1)
                e.dma_start(wr[s], w_o[4 + s]).then_inc(w_ob[s], 16)
            e.wait_ge(o_mm, KT)
            e.dma_start(scv[:, :, :], sconv).then_inc(s_sc, 16)

            def up_tiles(it):
                for s in range(4):
                    if not isinstance(it, int):
                        e.wait_ge(up_mm, it * 4 + (s - 3))
                    e.dma_start(wr[s], tile_of(w_up, it * 2 + (s // 2 + NF * (s % 2)))).then_inc(w_u[s], 16)

            up_tiles(0)
            for s in range(2):
                e.dma_start(wd[s], w_down[s]).then_inc(w_d[s], 16)
            with e.Fori(1, NF // 2) as it:
                up_tiles(it)
            with e.Fori(1, KT // 2) as it:
                for s in range(2):
                    e.wait_ge(dn_mm, it * 2 + (s - 1))
                    e.dma_start(wd[s], tile_of(w_down, it * 2 + s)).then_inc(w_d[s], 16)
            e.wait_ge(up_cp, 2 * NF)
            e.dma_start(conv_out, cvo[:, :, :]).then_inc(stored, 16)
            for i in range(2):
                e.wait_ge(xn_ready, 3 * KT + 4 * (i + 1))
                e.dma_start(yT[:, 4 * i:4 * i + 4, :], xn[:, 4 * i:4 * i + 4, :]).then_inc(stored, 16)
            e.wait_ge(k_stored, 16)
            e.wait_ge(ws_stored, 16)
            e.wait_ge(stored, 16 * N_STORES)

        @block.tensor
        def _(e):
            def wait(s, n):
                e.wait_ge(s, n)
                e.sem_inc(waited, 1)

            def sumsq(n):
                for k in range(KT):
                    e.wait_ge(sq_ready, n * KT + k + 1)
                    for h in range(2):
                        i = e.matmul(ps[:, h, 0:HALF], ones, sqb[k % 2][:, h * HALF:(h + 1) * HALF],
                                     start=(k == 0), stop=(k == KT - 1))
                    i.then_inc(sq_used, 1)

            def project(b, w, act, nk, done, k0=0):
                for k in range(nk):
                    for h in range(2):
                        i = e.matmul(ps[:, 2 * b + h, 0:HALF], w[:, k0 + k, :], act[:, k, h * HALF:(h + 1) * HALF],
                                     start=(k == 0), stop=(k == nk - 1))
                i.then_inc(done, 1)

            def project_split(s, done):
                for k in range(KT):
                    e.matmul(ps[:, 2 * s, 0:256], wr[s][:, k, :], xn[:, k, 0:256], start=(k == 0), stop=(k == KT - 1))
                    i = e.matmul(ps[:, 2 * s + 1, 0:320], wr[s][:, k, :], xn[:, k, 256:T], start=(k == 0), stop=(k == KT - 1))
                i.then_inc(done, 1)

            e.wait_ge(s_c0, 16)
            sumsq(0)
            e.wait_ge(xn_ready, KT)
            for r in range(2):
                for s in range(4):
                    e.wait_ge(w_a[s], 16 * (r + 1))
                    if r:
                        e.wait_ge(qk_out, s + 1)
                    project(s, wr[s], xn, KT, qk_tile)
            for s in range(4):
                e.wait_ge(w_a[s], 48)
                e.wait_ge(qk_out, 4 + s + 1)
                for t4 in range(5):
                    n = P if t4 < 4 else NS
                    dst = ps[0:n, 2 * s, t4 * P:(t4 + 1) * P] if t4 < 4 else ps[0:n, 2 * s + 1, 0:P]
                    for k in range(KT):
                        i = e.matmul(dst, xn[:, k, t4 * P:t4 * P + n], wr[s][:, k, :], start=(k == 0), stop=(k == KT - 1))
                i.then_inc(v_tile, 1)
            for s in range(4):
                e.wait_ge(w_a[s], 64)
                e.wait_ge(v_evac, 2 * s + 2)
                project_split(s, rw_tile)

            def rw_proj(it, s):
                e.wait_ge(w_a[s], it * 16 + 64)
                e.wait_ge(u_ready, it * 4 + (s - 3))
                project_split(s, rw_tile)

            with e.Fori(1, 3) as it:
                for s in range(4):
                    rw_proj(it, s)
            for s in range(2):
                rw_proj(3, s)

            units = [(h, qt) for h in range(8) for qt in range(4)]
            e.wait_ge(u_ready, NPB)
            e.wait_ge(s_c1, 32)

            def logits(u):
                h, qt = units[u]
                hp, r = h // 2, slice(64 * (h % 2), 64 * (h % 2) + 64)
                if u >= 4:
                    e.wait_ge(at_ex, u - 3)
                e.matmul(ps[:, u % 4, 0:P * (qt + 1)], qk[r, hp, qt * P:(qt + 1) * P], qk[r, HP + hp, 0:P * (qt + 1)],
                         start=True, stop=True).then_inc(at_lg, 1)

            def turn(u):
                h, qt = units[u]
                e.wait_ge(at_pn, u + 1)
                if u >= 2:
                    e.wait_ge(at_tc, u - 1)
                for k in range(qt + 1):
                    i = e.transpose(ps[:, 4 + u % 2, k * P:(k + 1) * P], pr[u % 2][:, k * P:(k + 1) * P], ident)
                i.then_inc(at_tp, 1)

            def values(u):
                h, qt = units[u]
                hp, r = h // 2, slice(64 * (h % 2), 64 * (h % 2) + 64)
                e.wait_ge(at_tc, u + 1)
                if u % 8 == 0 and hp >= 2:
                    e.wait_ge(at_oe, hp - 1)
                for k in range(qt + 1):
                    i = e.matmul(ps[r, 6 + hp % 2, qt * P:(qt + 1) * P], vp[:, k, h * HD:(h + 1) * HD], prT[u % 2][:, k, :],
                                 start=(k == 0), stop=(k == qt))
                i.then_inc(at_pv, 1)

            n = len(units)
            for u in range(n + 2):
                if u < n:
                    logits(u)
                if 1 <= u <= n:
                    turn(u - 1)
                if u >= 2:
                    values(u - 2)

            e.wait_ge(at_oe, HP)
            for hp in range(HP):
                e.wait_ge(pr_sq, hp + 1)
                for h in range(2):
                    i = e.matmul(ps[:, 2 * hp + h, 0:HALF], bones, tmp[hp][:, h * HALF:(h + 1) * HALF], start=True, stop=True)
                i.then_inc(pr_ss, 1)
            e.wait_ge(pr_mx, HP)
            e.wait_ge(s_lora, 16)
            e.wait_ge(pr_lin, 1)
            for hp in range(HP):
                if hp >= 2:
                    e.wait_ge(pr_sig, 2 * (hp - 1))
                for w in range(2):
                    r = slice(64 * w, 64 * w + 64)
                    for h in range(2):
                        i = e.matmul(ps[:, 4 * (hp % 2) + 2 * w + h, 0:HALF], w2a2[r, hp * P:(hp + 1) * P],
                                     wad[r, h * HALF:(h + 1) * HALF], start=True, stop=True)
                    i.then_inc(pr_w, 1)
            e.wait_ge(pr_sig, 2 * HP)
            for hp in range(HP):
                e.wait_ge(pr_b, hp + 1)
                for h in range(2):
                    i = e.matmul(ps[:, h, 0:HALF], bones, tmp[5][:, h * HALF:(h + 1) * HALF], start=True, stop=True)
                i.then_inc(pr_bp, 1)

            def gram(n, bank):
                if bank == 0:
                    wait(ch_stg, n + 1)
                ops = (((sA, sB), (sB, sA)), ((sK, sA), (sB, sR)), ((sK, sR), (sV, None)), ((sB, None), (sK, None)))[bank]
                for j, (lhs, rhs) in enumerate(ops):
                    for hp, r in heads():
                        right = rhs[r, hp, :] if rhs is not None else ident[r, r]
                        i = e.matmul(ps[r, bank, j * 256 + hp * C:j * 256 + (hp + 1) * C], lhs[r, hp, :], right,
                                     start=True, stop=True)
                i.then_inc(ch_g, 1)

            def level_x(n, l):
                if l == 0:
                    wait(ch_amt, n + 1)
                wait(ch_te, n * LEVELS + (l + 1))
                for hp, r in heads():
                    i = e.matmul(ps[r, 0, hp * C:(hp + 1) * C], amt[r, l, hp, :], tt[r, 0, hp, :], start=True, stop=True)
                i.then_inc(ch_x, 1)

            def level_d(n, l):
                if l == 0:
                    wait(ch_ev, n * 5 + 5)
                wait(ch_xe, n * (LEVELS - 1) + (l + 1))
                for hp, r in heads():
                    e.matmul(ps[r, 1, hp * C:(hp + 1) * C], tt[r, 1, hp, :], xx[r, hp, :], start=True, stop=True)
                for hp, r in heads():
                    i = e.matmul(ps[r, 1, 256 + hp * C:256 + (hp + 1) * C], xx[r, hp, :], tt[r, 1, hp, :],
                                 start=True, stop=True)
                i.then_inc(ch_d, 1)

            def chunk_w(c):
                wait(st_ready, c + 1)
                for hp, r in heads():
                    e.matmul(ps[r, 2, hp * C:(hp + 1) * C], sA[r, hp, :], st[r, hp, :], start=True, stop=False)
                    i = e.matmul(ps[r, 2, hp * C:(hp + 1) * C], mm1[r, 0, hp, :], mkv[r, 1, hp, :], start=False, stop=True)
                i.then_inc(ch_w, 1)

            def chunk_u(c):
                wait(ch_we, c + 1)
                wait(ch_te, c * LEVELS + 2 * LEVELS)
                for hp, r in heads():
                    i = e.matmul(ps[r, 3, hp * C:(hp + 1) * C], tt[r, 1, hp, :], ww[r, hp, :], start=True, stop=True)
                i.then_inc(ch_u, 1)

            def chunk_y(c):
                wait(ch_ue, c + 1)
                for hp, r in heads():
                    d = ps[r, 2, hp * C:(hp + 1) * C]
                    e.matmul(d, st[r, hp, :], sR[r, hp, :], start=True, stop=False)
                    e.matmul(d, uu[r, hp, :], mm1[r, 1, hp, :], start=False, stop=False)
                    i = e.matmul(d, mkv[r, 1, hp, :], mkv[r, 0, hp, :], start=False, stop=True)
                i.then_inc(ch_y, 1)
                for hp, r in heads():
                    d = ps[r, 0, hp * C:(hp + 1) * C]
                    e.matmul(d, bk[r, 0, hp, :], uu[r, hp, :], start=True, stop=False)
                    i = e.matmul(d, bk[r, 1, hp, :], mkv[r, 1, hp, :], start=False, stop=True)
                i.then_inc(ch_s, 1)

            e.wait_ge(pr_done, 1)
            for bank in range(4):
                gram(0, bank)
            for l in range(LEVELS - 1):
                level_x(0, l)
                level_d(0, l)
            wait(ch_te, LEVELS)
            e.wait_ge(s_s0, 16)
            halves = [slice(0, 64), slice(64, 128)]
            for hp in range(HP):
                cols = slice(hp * C, (hp + 1) * C)
                e.wait_ge(ss_ex, 2 * hp + 1)
                for r in halves:
                    for b in range(DB):
                        e.matmul(ps[r, 2, cols], ex[0][r, b, :], s0[r, hp, b, :], start=(b == 0), stop=False)
                    i = e.matmul(ps[r, 2, cols], mm1[r, 0, hp, :], mkv[r, 1, hp, :], start=False, stop=True)
                i.then_inc(ss_w, 1)
                e.wait_ge(ss_we, hp + 1)
                for r in halves:
                    i = e.matmul(ps[r, 3, cols], tt[r, 1, hp, :], ww[r, hp, :], start=True, stop=True)
                i.then_inc(ss_u, 1)
                e.wait_ge(ss_ue, hp + 1)
                for r in halves:
                    for b in range(DB):
                        e.matmul(ps[r, 4, cols], s0[r, hp, b, :], ex[1][r, b, :], start=(b == 0), stop=False)
                    e.matmul(ps[r, 4, cols], mkv[r, 1, hp, :], mkv[r, 0, hp, :], start=False, stop=False)
                    i = e.matmul(ps[r, 4, cols], uu[r, hp, :], mm1[r, 1, hp, :], start=False, stop=True)
                i.then_inc(ss_y, 1)
                e.wait_ge(ss_ex, 2 * hp + 2)
                if hp:
                    e.wait_ge(ss_st, hp)
                for r in halves:
                    e.matmul(ps[r, 6, :], bk[r, 0, hp, :], ex[2][r, :, :], start=True, stop=False)
                    i = e.matmul(ps[r, 6, :], bk[r, 1, hp, :], ex[3][r, :, :], start=False, stop=True)
                i.then_inc(ss_s if hp < HP - 1 else ch_s, 1)
            e.wait_ge(ss_st, HP)

            PER = 2 * NGRP

            def qk_group(b, g):
                wait(kv_in[g % 4], b * 256 + 64 * (g // 4 + 1))
                if g >= 2:
                    wait(sa_ev, b * PER + 2 * (g - 1))
                for hp in range(HP):
                    i = e.matmul(ps[32 * hp:32 * hp + 32, 4 + g % 2, :], qbd[:, hp, :], kring[g % 4][:, :, hp, :],
                                 start=True, stop=True)
                i.then_inc(kv_used, 1)

            def pv_turn(b, g):
                if g >= 2:
                    wait(sa_tc, b * (NGRP + 1) + (g - 1))
                if g < NGRP:
                    for q in range(GP):
                        i = e.transpose(ps[:, 4 + g % 2, q * P:(q + 1) * P], lg[:, (g * GP + q) * P:(g * GP + q + 1) * P], ident)
                else:
                    i = e.transpose(ps[0:NS, 4 + g % 2, 0:P], lg[:, PAST:PAST + NS], ident)
                i.then_inc(sa_tp, 1)

            def pv_group(b, g):
                wait(sa_tc, b * (NGRP + 1) + (g + 1))
                if g < NGRP:
                    wait(kv_in[g % 4], b * 256 + 64 * (g // 4 + 3))
                    for q in range(GP):
                        for hp in range(HP):
                            i = e.matmul(ps[32 * hp:32 * hp + 32, 7, 0:P], pT[g % 2][:, q, 32 * hp:32 * hp + 32],
                                         vring[g % 4][:, q, hp * P:(hp + 1) * P], start=(g == 0 and q == 0), stop=False)
                    i.then_inc(kv_used, 1)
                else:
                    for hp in range(HP):
                        i = e.matmul(ps[32 * hp:32 * hp + 32, 7, 0:P], pT[g % 2][0:NS, 0, 32 * hp:32 * hp + 32],
                                     vsm[0:NS, hp * P:(hp + 1) * P], start=False, stop=True)
                    i.then_inc(sa_nw, 1)

            e.sem_inc(sa_lg, 1)
            with e.Fori(0, DB) as b:
                wait(sa_q, b * 2 + 2)
                for g in range(NGRP):
                    qk_group(b, g)
                    if g < 2:
                        gram(b + 1, 2 * g)
                        gram(b + 1, 2 * g + 1)
                    elif g % 2 == 0:
                        level_x(b + 1, g // 2 - 1)
                    else:
                        level_d(b + 1, g // 2 - 1)
                wait(sa_ev, b * PER + 2 * (NGRP - 1))
                for hp in range(HP):
                    i = e.matmul(ps[32 * hp:32 * hp + 32, 4, 0:NS], qbd[:, hp, :], qks[:, HP + hp, :], start=True, stop=True)
                i.then_inc(sa_lg, 1)
                for l in range(3, LEVELS - 1):
                    level_x(b + 1, l)
                    level_d(b + 1, l)
                chunk_w(b)
                wait(sa_ex, b + 1)
                for g in range(NGRP + 2):
                    if g <= NGRP:
                        pv_turn(b, g)
                    if g >= 1:
                        pv_group(b, g - 1)
                    if g == 1:
                        chunk_u(b)
                    if g == 3:
                        chunk_y(b)
                e.wait_ge(sa_ob, b + 1)
                e.wait_ge(sa_oo, b + 1)
                e.transpose(ps[:, 6, 0:P], ob, ident).then_inc(sa_ot, 1)

            e.wait_ge(ch_ye, NCH)
            e.wait_ge(sa_oo, DB + 1)
            for hp in range(HP):
                if hp:
                    e.wait_ge(gn_out, hp)
                for h in range(2):
                    e.matmul(ps[:, 4 + h, 0:HALF], g2[:, hp * P:(hp + 1) * P], gd[:, h * HALF:(h + 1) * HALF], start=True, stop=True)
                for h in range(2):
                    i = e.matmul(ps[:, h, 0:HALF], bones, R[:, hp, h * HALF:(h + 1) * HALF], start=True, stop=True)
                i.then_inc(gn_mm, 1)
                e.wait_ge(gn_sq, hp + 1)
                for h in range(2):
                    i = e.matmul(ps[:, 2 + h, 0:HALF], bones, tmp[1][:, h * HALF:(h + 1) * HALF], start=True, stop=True)
                i.then_inc(gn_mm, 1)

            e.wait_ge(gn_out, HP)
            e.wait_ge(xn_ready, 2 * KT)
            with e.Fori(0, NG) as c:
                for s in range(2):
                    e.wait_ge(w_g[s], c * 16 + 16)
                    e.wait_ge(ga_free[s], c + 1)
                    project(s, wr[s], xn, KT, ga_mm)
                e.wait_ge(w_g[2], c * 16 + 16)
                for s, act in ((2, oa), (3, yb)):
                    e.wait_ge(ga_free[s], c + 1)
                    project(s, wr[2], act, HP, ga_mm, k0=HP * (s - 2))
            e.wait_ge(m_done, NG + 1)
            for r in range(2):
                for s in range(4):
                    e.wait_ge(w_ob[s], 16 * (r + 1))
                    if r:
                        e.wait_ge(h_done, s + 1)
                    project(s, wr[s], m, KT, o_mm)
            e.wait_ge(h_done, KT)
            sumsq(1)
            e.wait_ge(xn_ready, 3 * KT)

            def up(it):
                for s in range(4):
                    e.wait_ge(w_u[s], it * 16 + 16)
                    if not isinstance(it, int):
                        e.wait_ge(up_ev, it * 4 + (s - 3))
                    project_split(s, up_mm)

            up(0)
            with e.Fori(1, NF // 2) as it:
                up(it)
            e.wait_ge(up_h, NF)

            def down(it):
                for s in range(2):
                    e.wait_ge(w_d[s], it * 16 + 16)
                    if not isinstance(it, int):
                        e.wait_ge(y_done, it * 2 + (s - 1))
                    project(s, wd[s], hh, NF, dn_mm)

            down(0)
            with e.Fori(1, KT // 2) as it:
                down(it)
            e.wait_ge(y_done, KT)
            sumsq(2)

        @block.scalar
        def _(e):
            def squares(n):
                for k in range(KT):
                    if n == 0:
                        e.wait_ge(s_x[k // 2], 16)
                    if k >= 2:
                        e.wait_ge(sq_used, n * KT + k - 1)
                    e.activation(sqb[k % 2], x[:, k, :], ACT.Square).then_inc(sq_ready, 1)

            def root(n):
                e.wait_ge(ms_ready, n + 1)
                e.activation(rs, rs, ACT.Sqrt).then_inc(rt_ready, 1)

            squares(0)
            root(0)
            for c in range(2 * HP):
                e.wait_ge(qk_tile, c + 1)
                e.activation(lin(qk[:, c, :]), pair(c % 4), ACT.Copy).then_inc(qk_out, 1)

            def shift_in(it, s):
                u = ub[s % 2]
                e.wait_ge(rw_tile, it * 4 + (s + 1))
                if s >= 2 or not (isinstance(it, int) and it == 0):
                    e.wait_ge(xm_done, it * 4 + (s - 1))
                    e.wait_ge(tsh_done, it * 4 + (s - 1))
                e.activation(u[:, 1:513].rearrange("p (h n) -> p h n", h=2), ps[:, 2 * s:2 * s + 2, 0:256], ACT.Copy)
                e.activation(u[:, 513:585].rearrange("p (b n) -> p b n", b=DB)[:, :, 1:9],
                             ps[:, 2 * s + 1, 256:320].rearrange("p (b n) -> p b n", b=DB), ACT.Copy).then_inc(u_ready, 1)

            e.wait_ge(init_done, 1)
            for s in range(4):
                shift_in(0, s)
            with e.Fori(1, 3) as it:
                for s in range(4):
                    shift_in(it, s)
            for s in range(2):
                shift_in(3, s)

            units = [(h, qt) for h in range(8) for qt in range(4)]
            n = len(units)
            for u in range(n + 1):
                if u < n:
                    w = P * (units[u][1] + 1)
                    e.wait_ge(at_mx, u + 1)
                    if u >= 2:
                        e.wait_ge(at_tp, u - 1)
                    e.activation(pr[u % 2][:, 0:w], ps[:, u % 4, 0:w], ACT.Exp, bias=nmx[:, u % 8:u % 8 + 1], scale=SCALE,
                                 accum_out=rsm[:, u % 8:u % 8 + 1]).then_inc(at_ex, 1)
                if u >= 1:
                    v = u - 1
                    w = P * (units[v][1] + 1)
                    e.wait_ge(at_tp, v + 1)
                    if v >= 2:
                        e.wait_ge(at_pv, v - 1)
                    e.activation(prT[v % 2][:, :, :].rearrange("p a b -> p (a b)")[:, 0:w], ps[:, 4 + v % 2, 0:w],
                                 ACT.Copy).then_inc(at_tc, 1)

            for hp in range(HP):
                e.wait_ge(pr_mx, hp + 1)
                e.activation(tmp[4 + hp], tmp[4 + hp], ACT.Sqrt).then_inc(pr_rt, 1)
            e.wait_ge(xm_done, NPB)
            e.activation(wad[0:64, :], wad[0:64, :], ACT.Tanh).then_inc(pr_lin, 1)
            e.activation(gd, gd, ACT.Sigmoid)
            for hp in range(HP):
                for w, (dst, name) in enumerate(((AL, "w0"), (BE, "a0"))):
                    e.wait_ge(pr_w, 2 * hp + w + 1)
                    e.activation(lin(dst[:, hp, :]), pair(2 * (hp % 2) + w), ACT.Sigmoid, bias=pcol(name, hp)).then_inc(pr_sig, 1)
            for hp in range(HP):
                e.wait_ge(pr_exc, hp + 1)
                e.activation(tmp[3], tmp[1], ACT.Exp)
                e.activation(tmp[4], tmp[1], ACT.Exp, scale=-1.0)
                e.activation(tmp[2], tmp[2], ACT.Exp).then_inc(pr_exp, 1)

            e.wait_ge(ws_stored, 16)
            with e.Fori(0, DB) as b:
                for g in range(NGRP):
                    e.wait_ge(kv_used, b * (2 * NGRP) + (g + 1))
                    for j in range(2):
                        blk = 2 * g + j
                        e.activation(lg[:, blk * BLK:(blk + 1) * BLK], ps[:, 4 + g % 2, j * BLK:(j + 1) * BLK], ACT.Identity,
                                     accum_out=gs[:, blk:blk + 1]).then_inc(sa_ev, 1)
                e.wait_ge(sa_bi, b + 1)
                for k in range(NBLK):
                    e.activation(lg[:, k * BLK:(k + 1) * BLK], lg[:, k * BLK:(k + 1) * BLK], ACT.Exp, bias=bi[:, k:k + 1],
                                 scale=SCALE, accum_out=psm[:, k:k + 1])
                e.activation(lg[:, PAST:PAST + NS], lg[:, PAST:PAST + NS], ACT.Exp, bias=bi[:, NBLK:NBLK + 1], scale=SCALE,
                             accum_out=psm[:, NBLK:NBLK + 1]).then_inc(sa_ex, 1)
                for g in range(NGRP + 1):
                    e.wait_ge(sa_tp, b * (NGRP + 1) + (g + 1))
                    if g >= 2:
                        e.wait_ge(kv_used, b * (2 * NGRP) + (NGRP + g - 1))
                    if g < NGRP:
                        e.activation(pT[g % 2][:, :, :].rearrange("p a b -> p (a b)"), ps[:, 4 + g % 2, :], ACT.Copy).then_inc(sa_tc, 1)
                    else:
                        e.activation(pT[g % 2][0:NS, 0, :], ps[0:NS, 4 + g % 2, 0:P], ACT.Copy).then_inc(sa_tc, 1)

            for hp in range(HP):
                e.wait_ge(gn_v, hp + 1)
                e.activation(tmp[2], tmp[2], ACT.Sqrt).then_inc(gn_rt, 1)

            for s in range(2):
                e.sem_inc(ga_free[s], 1)
            with e.Fori(0, NG) as c:
                e.wait_ge(m_done, c + 1)
                for s, g in ((0, g0), (1, g1)):
                    e.wait_ge(ga_mm, c * 4 + (s + 1))
                    e.activation(lin(g), pair(s), ACT.Sigmoid).then_inc(ga_free[s], 1)

            e.wait_ge(h_done, KT)
            squares(1)
            root(1)

            def up(it):
                later = not isinstance(it, int)
                for s in range(4):
                    col = it * 2 + (s // 2 + NF * (s % 2))
                    e.wait_ge(up_mm, it * 4 + (s + 1))
                    if later:
                        e.wait_ge(up_cp, it * 4 + (s - 3))
                        e.wait_ge(up_h, it * 2 + (s // 2 - 1))
                    e.activation(cu[s][:, 2:514].rearrange("p (h n) -> p h n", h=2), ps[:, 2 * s:2 * s + 2, 0:256], ACT.Copy)
                    e.activation(cu[s][:, 514:594].rearrange("p (b n) -> p b n", b=DB)[:, :, 2:10],
                                 ps[:, 2 * s + 1, 256:320].rearrange("p (b n) -> p b n", b=DB), ACT.Copy).then_inc(up_ev, 1)
                    e.wait_ge(up_ev, it * 4 + (s + 1))
                    e.wait_ge(up_st, it * 4 + (s + 1))
                    e.activation(cc[s], cu[s][:, 2:594], ACT.Identity, bias=pcol("cb", col), scale=pcol("cw2", col)).then_inc(up_c0, 1)
                for s in (1, 3):
                    e.wait_ge(up_cv, it * 4 + (s + 1))
                    e.activation(cc[s], cc[s], ACT.Silu).then_inc(up_si, 1)

            up(0)
            with e.Fori(1, NF // 2) as it:
                up(it)
            e.wait_ge(y_done, KT)
            squares(2)
            root(2)

        @block.gpsimd
        def _(e):
            e.wait_ge(qk_out, 2 * HP)
            e.tensor_copy(qks[:, :, :], qk[:, :, SEQ:T]).then_inc(qks_done, 1)

            def last_rows(g, s):
                e.wait_ge(u_ready, g + 1)
                dst = tsh[:, g:g + 1, :] if isinstance(g, int) else tsh[:, bass.ds(g, 1), :]
                e.tensor_copy(dst, ub[s % 2][:, 512:593].rearrange("p (o b n) -> p o b n", o=1, n=9)[:, :, :, 0]).then_inc(tsh_done, 1)

            with e.Fori(0, 3) as it:
                for s in range(4):
                    last_rows(it * 4 + s, s)
            for s in range(2):
                last_rows(12 + s, s)

            def stage(n, cols):
                if not (isinstance(n, int) and n == 0):
                    e.wait_ge(ch_s, n)
                e.tensor_copy(stg[:, :, :], rw[:, :, cols]).then_inc(ch_stg, 1)
                e.wait_ge(ch_ev, n * 5 + 1)
                for l in range(LEVELS - 1):
                    i = e.tensor_tensor(amt[:, l, :, :], aa[:, 1, :, :], mone("lvl", 128 * (l + 1) + 64), ALU.mult)
                i.then_inc(ch_amt, 1)

            e.wait_ge(pr_done, 1)
            stage(0, slice(SEQ, T))
            with e.Fori(0, DB) as b:
                e.wait_ge(sa_lg, b + 1)
                e.tensor_copy(qbd[0:64, :, 0:8], qks[0:64, 0:HP, bass.ds(b * DT, DT)]).then_inc(sa_q, 1)
                e.wait_ge(sa_q, b * 2 + 1)
                e.tensor_copy(qbd[64:128, :, 8:16], qks[64:128, 0:HP, bass.ds(b * DT, DT)]).then_inc(sa_q, 1)
                e.wait_ge(sa_q, b * 2 + 2)
                stage(b + 1, bass.ds(b * C, C))

            e.wait_ge(o_mm, KT)
            for s in range(4):
                i = e.memset(cu[s][:, 0:2], 0.0)
            i.then_inc(up_z, 1)
            e.wait_ge(s_sc, 16)

            def conv_rows(it):
                for s in range(4):
                    col = it * 2 + (s // 2 + NF * (s % 2))
                    at_ = bass.ds(col, 1)
                    if isinstance(it, int):
                        at_ = slice(col, col + 1)
                    else:
                        e.wait_ge(up_cv, it * 4 + (s - 3))
                    e.tensor_copy(cu[s][:, 514:594].rearrange("p (b n) -> p b n", b=DB)[:, :, 0:2],
                                  scv[:, at_, :].rearrange("p o (b n) -> p (o b) n", b=DB)).then_inc(up_st, 1)
                    e.wait_ge(up_ev, it * 4 + (s + 1))
                    e.tensor_copy(cvo[:, at_, :].rearrange("p o (b n) -> p (o b) n", b=9),
                                  cu[s][:, 512:602].rearrange("p (b n) -> p b n", b=9)[:, :, 0:2]).then_inc(up_cp, 1)

            conv_rows(0)
            with e.Fori(1, NF // 2) as it:
                conv_rows(it)

        @block.vector
        def _(e):
            def rstd(n):
                own_ = Line(e, own["norm"], 2 * n)
                e.wait_ge(sq_used, (n + 1) * KT)
                own_.did(e.tensor_scalar(lin(rs), pair(0), 1.0 / D, EPS, ALU.mult, ALU.add))
                own_.settle()
                e.sem_inc(ms_ready, 1)
                e.wait_ge(rt_ready, n + 1)
                own_.did(e.reciprocal(rs, rs))
                own_.settle()

            def normed(gain):
                for k in range(KT):
                    e.scalar_tensor_tensor(out=xn[:, k, :], in0=x[:, k, :], scalar=pcol(gain, k), in1=rs,
                                           op0=ALU.mult, op1=ALU.mult).then_inc(xn_ready, 1)

            ln = Line(e, own["setup"])
            for u in ub:
                ln.did(e.memset(u[:, :], 0.0))
            ln.did(e.memset(qbd[:, :, :], 0.0))
            ln.did(e.memset(mb[:, :], 0.0))
            ln.settle()
            e.sem_inc(init_done, 1)
            e.wait_ge(s_pv, 16)
            rstd(0)
            normed("ln1")
            e.tensor_scalar(omka, pv[:, PV["ka"]:PV["ka"] + HP], -1.0, 1.0, ALU.mult, ALU.add)
            for s in range(4):
                e.wait_ge(v_tile, s + 1)
                e.tensor_copy(vp[:, :, s * P:(s + 1) * P], ps[:, 2 * s, :].rearrange("p (a b) -> p a b", a=4)).then_inc(v_evac, 1)
                e.tensor_copy(vsm[0:NS, s * P:(s + 1) * P], ps[0:NS, 2 * s + 1, 0:P]).then_inc(v_evac, 1)

            SH = 2
            e.wait_ge(s_c1, 32)

            def shift(g, s, base, dst):
                ln = Line(e, own["shift"], base)
                u = ub[s % 2]
                e.wait_ge(u_ready, g + 1)
                src = shs[:, g, :] if isinstance(g, int) else shs[:, bass.ds(g, 1), :].rearrange("p o b -> p (o b)")
                ln.did(e.tensor_scalar(u[:, 513:585].rearrange("p (b n) -> p b n", b=DB)[:, :, 0], src, 1.0, None, ALU.mult))
                ln.settle()
                ln.did(e.tensor_tensor(df[:, 0:584], u[:, 0:584], u[:, 1:585], ALU.subtract))
                ln.settle()
                mu = pcol("mu", g)
                e.scalar_tensor_tensor(out=dst[:, 0:SEQ], in0=df[:, 0:SEQ], scalar=mu, in1=u[:, 1:513],
                                       op0=ALU.mult, op1=ALU.add)
                e.scalar_tensor_tensor(out=dst[:, SEQ:T].rearrange("p (b n) -> p b n", b=DB),
                                       in0=df[:, 513:585].rearrange("p (b n) -> p b n", b=DB)[:, :, 0:8], scalar=mu,
                                       in1=u[:, 514:586].rearrange("p (b n) -> p b n", b=DB)[:, :, 0:8],
                                       op0=ALU.mult, op1=ALU.add).then_inc(xm_done, 1)
                assert ln.n == SH

            with e.Fori(0, 3) as it:
                for s in range(4):
                    shift(it * 4 + s, s, it * (4 * SH) + SH * s, rw[:, bass.ds(it * 4 + s, 1), :].rearrange("p o n -> p (o n)"))
            for s, dst in enumerate((wad, gd)):
                shift(12 + s, s, SH * (12 + s), dst)

            ln = Line(e, own["attn"])
            units = [(h, qt) for h in range(8) for qt in range(4)]
            n = len(units)
            for u in range(n + 2):
                if u < n:
                    qt = units[u][1]
                    w, j = P * (qt + 1), u % 8
                    e.wait_ge(at_lg, u + 1)
                    diag = ps[:, u % 4, w - P:w]
                    ln.did(e.tensor_tensor(diag, diag, causal, ALU.add))
                    ln.settle()
                    ln.did(e.tensor_reduce(mx[:, j:j + 1], ps[:, u % 4, 0:w], AX.X, ALU.max))
                    ln.settle()
                    e.tensor_scalar(nmx[:, j:j + 1], mx[:, j:j + 1], -SCALE, None, ALU.mult).then_inc(at_mx, 1)
                if 1 <= u <= n:
                    v = u - 1
                    w, j = P * (units[v][1] + 1), v % 8
                    e.wait_ge(at_ex, v + 1)
                    ln.did(e.reciprocal(rin[:, j:j + 1], rsm[:, j:j + 1]))
                    ln.settle()
                    e.tensor_scalar(pr[v % 2][:, 0:w], pr[v % 2][:, 0:w], rin[:, j:j + 1], None, ALU.mult).then_inc(at_pn, 1)
                if u >= 9 and (u - 9) % 8 == 0:
                    hp = (u - 9) // 8
                    e.wait_ge(at_pv, 8 * hp + 8)
                    e.tensor_copy(oa[:, hp, 0:SEQ], ps[:, 6 + hp % 2, :]).then_inc(at_oe, 1)

            ln = Line(e, own["prep"])
            e.wait_ge(qks_done, 1)
            e.wait_ge(tsh_done, NPB)
            e.wait_ge(k_stored, 16)
            for hp in range(HP):
                ln.did(e.tensor_scalar(yb[:, hp, :], K[:, hp, :], pcol("kk", hp), None, ALU.mult))
                ln.settle()
                e.tensor_tensor(tmp[hp], yb[:, hp, :], yb[:, hp, :], ALU.mult).then_inc(pr_sq, 1)
            for hp in range(HP):
                e.wait_ge(pr_ss, hp + 1)
                e.tensor_scalar(lin(tmp[4 + hp]), pair(hp), 1e-24, None, ALU.max).then_inc(pr_mx, 1)
            for hp in range(HP):
                e.wait_ge(pr_rt, hp + 1)
                ln.did(e.reciprocal(tmp[4 + hp], tmp[4 + hp]))
                ln.settle()
                ln.did(e.tensor_tensor(yb[:, hp, :], yb[:, hp, :], tmp[4 + hp], ALU.mult))
            ln.settle()
            for hp in range(HP):
                r_, k_, v_, al, be, kk = (a[:, hp, :] for a in (R, K, V, AL, BE, yb))
                e.wait_ge(pr_sig, 2 * hp + 2)
                ln.did(e.tensor_scalar(tmp[0], al, -EM05, None, ALU.mult))
                ln.settle()
                ln.did(e.tensor_tensor_scan(tmp[1], reset, tmp[0], 0.0, ALU.mult, ALU.add))
                ln.settle()
                e.tensor_tensor(tmp[2], tmp[1], tmp[0], ALU.subtract).then_inc(pr_exc, 1)
                ln.did(e.tensor_scalar(tmp[5], be, pcol("ka", hp), omka[:, hp:hp + 1], ALU.mult, ALU.add))
                ln.settle()
                ln.did(e.tensor_tensor(k_, k_, tmp[5], ALU.mult))
                ln.settle()
                e.scalar_tensor_tensor(out=tmp[5], in0=r_, scalar=pcol("rk", hp), in1=k_, op0=ALU.mult, op1=ALU.mult).then_inc(pr_b, 1)
                ln.did(e.tensor_tensor(be, be, kk, ALU.mult))
                ln.settle()
                e.wait_ge(pr_exp, hp + 1)
                ln.did(e.scalar_tensor_tensor(out=al, in0=kk, scalar=-1.0, in1=tmp[2], op0=ALU.mult, op1=ALU.mult))
                ln.did(e.tensor_tensor(be, be, tmp[4], ALU.mult))
                e.wait_ge(pr_b, hp + 1)
                ln.did(e.tensor_tensor(k_, k_, tmp[4], ALU.mult))
                ln.did(e.tensor_tensor(r_, r_, tmp[3], ALU.mult))
                ln.did(e.tensor_copy(lc[:, hp, 0:8], tmp[3][:, 0:SEQ].rearrange("p (c n) -> p c n", n=C)[:, :, C - 1]))
                ln.did(e.tensor_copy(lc[:, hp, 8:16], tmp[3][:, SEQ:T].rearrange("p (c n) -> p c n", n=DT)[:, :, DT - 1]))
                ln.settle()
                e.wait_ge(pr_bp, hp + 1)
                ln.did(e.tensor_tensor(lin(kk), lin(v_), pair(0), ALU.mult))
                ln.settle()
            ln.did(e.memset(st[:, :, :], 0.0))
            ln.settle()
            e.sem_inc(st_ready, 1)
            e.sem_inc(pr_done, 1)

            TI = 2

            def gram_out(n, bank, base, own_sem, masks):
                e.wait_ge(ch_g, n * 4 + (bank + 1))
                if bank == 0:
                    ln = Line(e, own_sem, base)
                    e.tensor_tensor(aa[:, :, :, :], q8(0), mpair(masks[0]), ALU.mult).then_inc(ch_ev, 1)
                    e.wait_ge(ch_ev, n * 5 + 1)
                    ln.did(e.tensor_tensor(tt[:, :, :, :], aa[:, :, :, :], mpair("lvl"), ALU.mult))
                    ln.settle()
                    e.tensor_tensor(tt[:, :, :, :], tt[:, :, :, :], mpair("eye2"), ALU.add).then_inc(ch_te, 1)
                elif bank == 1:
                    e.tensor_tensor(mm1[:, :, :, :], q8(1), mpair(masks[1]), ALU.mult).then_inc(ch_ev, 1)
                elif bank == 2:
                    e.tensor_tensor(mkv[:, 0, :, :], q4(2, 0), mone(masks[1], 64), ALU.mult).then_inc(ch_ev, 1)
                    e.tensor_copy(mkv[:, 1, :, :], q4(2, 1)).then_inc(ch_ev, 1)
                else:
                    e.tensor_copy(bk[:, :, :, :], q8(3)).then_inc(ch_ev, 1)

            def x_out(n, l):
                e.wait_ge(ch_x, n * (LEVELS - 1) + (l + 1))
                e.tensor_copy(xx[:, :, :], q4(0)).then_inc(ch_xe, 1)

            def d_out(n, l):
                e.wait_ge(ch_d, n * (LEVELS - 1) + (l + 1))
                e.tensor_tensor(tt[:, :, :, :], tt[:, :, :, :], q8(1), ALU.add).then_inc(ch_te, 1)

            for bank in range(4):
                gram_out(0, bank, 0, own["ch0"], ("ms0", "ms1"))
            for l in range(LEVELS - 1):
                x_out(0, l)
                d_out(0, l)
            ln = Line(e, own["chunk0"])
            e.wait_ge(s_s0, 16)
            for hp in range(HP):
                if hp:
                    e.wait_ge(ss_y, hp)
                for a, src in ((0, sA), (1, sR)):
                    i = e.tensor_tensor(ex[a], src[:, hp:hp + 1, :].to_broadcast([P, DB, C]), colm, ALU.mult)
                i.then_inc(ss_ex, 1)
                e.wait_ge(ss_w, hp + 1)
                e.tensor_copy(ww[:, hp, :], ps[:, 2, hp * C:(hp + 1) * C]).then_inc(ss_we, 1)
                e.wait_ge(ss_u, hp + 1)
                e.tensor_copy(uu[:, hp, :], ps[:, 3, hp * C:(hp + 1) * C]).then_inc(ss_ue, 1)
                e.wait_ge(ss_ue, hp + 1)
                if hp:
                    e.wait_ge(ss_s, hp)
                for a, src in ((2, uu[:, hp:hp + 1, :]), (3, mkv[:, 1, hp:hp + 1, :])):
                    i = e.tensor_tensor(ex[a], src.to_broadcast([P, DB, C]),
                                        rowm.rearrange("p (b o) -> p b o", o=1).to_broadcast([P, DB, C]), ALU.mult)
                i.then_inc(ss_ex, 1)
                e.wait_ge(ss_y, hp + 1)
                ln.did(e.tensor_copy(R[:, hp, SEQ:T], ps[:, 4, hp * C:(hp + 1) * C]))
                e.wait_ge(ss_s if hp < HP - 1 else ch_s, hp + 1 if hp < HP - 1 else 1)
                ln.did(e.tensor_tensor(s0[:, hp, :, :], s0[:, hp, :, :], ps[:, 6, :].rearrange("p (b n) -> p b n", b=DB), ALU.add))
                ln.settle()
                e.tensor_tensor(s0[:, hp, :, :], s0[:, hp, :, :],
                                lc[:, hp, 8:16].rearrange("p (b o) -> p b o", o=1).to_broadcast([P, DB, C]), ALU.mult).then_inc(ss_st, 1)

            e.sem_inc(sa_oo, 1)
            e.wait_ge(ws_stored, 16)
            DL = 15
            with e.Fori(0, DB) as b:
                ln = Line(e, own["loop"], b * DL)
                for g in range(NGRP):
                    if g < 2:
                        gram_out(b + 1, 2 * g, b * 1, own["chl"], ("mp0", "mp1"))
                        gram_out(b + 1, 2 * g + 1, b * 1, own["chl"], ("mp0", "mp1"))
                    elif g % 2 == 0:
                        x_out(b + 1, g // 2 - 1)
                    else:
                        d_out(b + 1, g // 2 - 1)
                    e.wait_ge(sa_ev, b * (2 * NGRP) + (2 * g + 2))
                    i = e.tensor_reduce(bm[:, 2 * g:2 * g + 2], lg[:, 512 * g:512 * g + 512].rearrange("p (a n) -> p a n", a=2), AX.X, ALU.max)
                ln.did(i)
                e.wait_ge(sa_lg, b + 2)
                ln.did(e.tensor_tensor(lg[:, PAST:PAST + NS], ps[:, 4, 0:NS], cst[:, bass.ds(b * 64 + CV["newm"], 64)], ALU.add))
                gi = gs.rearrange("p (o n) -> p o n", o=1).to_broadcast([P, NBLK, NBLK])
                gj = gs.rearrange("p (n o) -> p n o", o=1).to_broadcast([P, NBLK, NBLK])
                ln.did(e.tensor_tensor(cmp1, gi, gj, ALU.is_gt))
                ln.did(e.tensor_tensor(cmp2, gi, gj, ALU.is_equal))
                ln.settle()
                ln.did(e.tensor_reduce(bm[:, NBLK:NBLK + 1], lg[:, PAST:PAST + NS], AX.X, ALU.max))
                ln.did(e.tensor_tensor(cmp2, cmp2, tri, ALU.mult))
                ln.settle()
                ln.did(e.tensor_tensor(cmp1, cmp1, cmp2, ALU.add))
                ln.settle()
                ln.did(e.tensor_reduce(mb[:, 0:NBLK], cmp1, AX.X, ALU.add))
                ln.settle()
                ln.did(e.tensor_scalar(mb[:, 0:NBLK], mb[:, 0:NBLK], TOPK - 0.5, NEG, ALU.is_ge, ALU.mult))
                ln.settle()
                ln.did(e.tensor_tensor(bm, bm, mb, ALU.add))
                ln.settle()
                ln.did(e.tensor_reduce(sc[:, 0:1], bm, AX.X, ALU.max))
                ln.settle()
                ln.did(e.tensor_scalar(sc[:, 1:2], sc[:, 0:1], -SCALE, None, ALU.mult))
                ln.settle()
                e.tensor_scalar(bi, mb, sc[:, 1:2], None, ALU.add).then_inc(sa_bi, 1)
                for l in range(3, LEVELS - 1):
                    x_out(b + 1, l)
                    d_out(b + 1, l)
                e.wait_ge(ch_w, b + 1)
                e.tensor_copy(ww[:, :, :], q4(2)).then_inc(ch_we, 1)
                e.wait_ge(ch_u, b + 1)
                e.tensor_copy(uu[:, :, :], q4(3)).then_inc(ch_ue, 1)
                e.wait_ge(ch_y, b + 1)
                e.tensor_copy(R[:, :, bass.ds(b * C, C)], q4(2)).then_inc(ch_ye, 1)
                e.wait_ge(ch_s, b + 2)
                ln.did(e.tensor_tensor(st[:, :, :], st[:, :, :], q4(0), ALU.add))
                ln.settle()
                e.tensor_tensor(st[:, :, :], st[:, :, :], lc[:, :, bass.ds(b, 1)].to_broadcast([P, HP, C]), ALU.mult).then_inc(st_ready, 1)
                e.wait_ge(sa_ex, b + 1)
                ln.did(e.tensor_reduce(sc[:, 2:3], psm, AX.X, ALU.add))
                ln.settle()
                ln.did(e.reciprocal(sc[:, 3:4], sc[:, 2:3]))
                ln.settle()
                e.wait_ge(sa_nw, b + 1)
                e.tensor_scalar(ob, ps[:, 7, 0:P], sc[:, 3:4], None, ALU.mult).then_inc(sa_ob, 1)
                e.wait_ge(sa_ot, b + 1)
                for half in range(2):
                    r = slice(64 * half, 64 * half + 64)
                    i = e.tensor_copy(oa[r, :, bass.ds(b * DT + SEQ, DT)],
                                      ps[r, 6, 0:P].rearrange("p (a n) -> p a n", a=HP)[:, :, 8 * half:8 * half + 8])
                i.then_inc(sa_oo, 1)
                assert ln.n == DL

            e.wait_ge(kv_used, 2 * DB * NGRP)
            normed("ln1")
            ln = Line(e, own["gn"])
            for hp in range(HP):
                e.wait_ge(gn_mm, 2 * hp + 1)
                ln.did(e.scalar_tensor_tensor(out=lin(tmp[0]), in0=pair(0), scalar=-1.0 / HD, in1=lin(R[:, hp, :]),
                                              op0=ALU.mult, op1=ALU.add))
                ln.settle()
                e.tensor_tensor(tmp[1], tmp[0], tmp[0], ALU.mult).then_inc(gn_sq, 1)
                e.wait_ge(gn_mm, 2 * hp + 2)
                e.tensor_scalar(lin(tmp[2]), pair(1), 1.0 / HD, GN_EPS, ALU.mult, ALU.add).then_inc(gn_v, 1)
                e.wait_ge(gn_rt, hp + 1)
                ln.did(e.reciprocal(tmp[2], tmp[2]))
                ln.settle()
                ln.did(e.tensor_tensor(tmp[0], tmp[0], tmp[2], ALU.mult))
                ln.settle()
                ln.did(e.tensor_scalar(tmp[0], tmp[0], pcol("lg", hp), pcol("lb", hp), ALU.mult, ALU.add))
                ln.settle()
                ln.did(e.tensor_tensor(tmp[0], tmp[0], yb[:, hp, :], ALU.add))
                ln.settle()
                e.tensor_tensor(lin(yb[:, hp, :]), lin(tmp[0]), pair(2), ALU.mult).then_inc(gn_out, 1)

            e.wait_ge(gn_out, HP)
            for s in (2, 3):
                e.sem_inc(ga_free[s], 1)
            e.sem_inc(m_done, 1)
            with e.Fori(0, NG) as c:
                for s, g in ((2, g0), (3, g1)):
                    e.wait_ge(ga_free[s - 2], c + 2)
                    e.wait_ge(ga_mm, c * 4 + (s + 1))
                    e.tensor_tensor(lin(g), lin(g), pair(s), ALU.mult).then_inc(ga_free[s], 1)
                e.wait_ge(ga_free[2], c + 2)
                e.wait_ge(ga_free[3], c + 2)
                e.tensor_tensor(m[:, bass.ds(c, 1), :].rearrange("p o n -> p (o n)"), g0, g1, ALU.add).then_inc(m_done, 1)
            for c in range(KT):
                e.wait_ge(o_mm, c + 1)
                e.tensor_tensor(lin(x[:, c, :]), lin(x[:, c, :]), pair(c % 4), ALU.add).then_inc(h_done, 1)
            rstd(1)
            normed("ln2")
            e.wait_ge(up_z, 1)

            def up(it):
                for s in range(4):
                    col = it * 2 + (s // 2 + NF * (s % 2))
                    base = it * 8
                    e.wait_ge(up_c0, it * 4 + (s + 1))
                    ln = Line(e, own["up"], it * 4 + s)
                    ln.did(e.scalar_tensor_tensor(out=cc[s], in0=cu[s][:, 1:593], scalar=pcol("cw1", col), in1=cc[s],
                                                  op0=ALU.mult, op1=ALU.add))
                    ln.settle()
                    e.scalar_tensor_tensor(out=cc[s], in0=cu[s][:, 0:592], scalar=pcol("cw0", col), in1=cc[s],
                                           op0=ALU.mult, op1=ALU.add).then_inc(up_cv, 1)
                for s in (1, 3):
                    e.wait_ge(up_si, it * 2 + (s // 2 + 1))
                    e.wait_ge(up_cv, it * 4 + (s + 1))
                    j = it * 2 + s // 2
                    at_ = slice(j, j + 1) if isinstance(j, int) else bass.ds(j, 1)
                    dst = hh[:, at_, :].rearrange("p o n -> p (o n)")
                    e.tensor_tensor(dst[:, 0:SEQ], cc[s][:, 0:SEQ], cc[s - 1][:, 0:SEQ], ALU.mult)
                    e.tensor_tensor(dst[:, SEQ:T].rearrange("p (b n) -> p b n", b=DB),
                                    cc[s][:, 512:592].rearrange("p (b n) -> p b n", b=DB)[:, :, 2:10],
                                    cc[s - 1][:, 512:592].rearrange("p (b n) -> p b n", b=DB)[:, :, 2:10], ALU.mult).then_inc(up_h, 1)

            up(0)
            with e.Fori(1, NF // 2) as it:
                up(it)
            with e.Fori(0, KT // 2) as it:
                for s in range(2):
                    c = bass.ds(it * 2 + s, 1)
                    e.wait_ge(dn_mm, it * 2 + (s + 1))
                    e.tensor_tensor(lin3(x[:, c, :]), lin3(x[:, c, :]), pair(s), ALU.add).then_inc(y_done, 1)
            rstd(2)
            normed("lnf")


_ARGS = ["xin", "kcache", "vcache", "pages", "s0t", "sshift", "sconv", "pvec", "consts", "lora", "w_in", "w_br", "w_o", "w_up", "w_down"]
_OUTS = [("yT", (P, KT, T)), ("kT", (P, HP, T)), ("v", (P, 4, WA)), ("vs", (NS, WA)), ("wkvp", (P, HP * HD)),
         ("tsh", (P, NPB, 9)), ("conv", (P, 2 * NF, 18)), ("wkvs", (P, HP * DB * HD))]


def kernel(**inputs):
    import concourse.bacc as bacc
    from concourse.bass_utils import run_bass_kernel_spmd

    a = {k: np.asarray(v) for k, v in inputs.items()}

    def tiles(w, nk, cols=None):
        w = w if cols is None else w[:, cols[0]:cols[1]]
        return w.reshape(nk, P, -1, P).transpose(2, 1, 0, 3)

    def fm(v):
        return v.reshape(-1, P).T

    npool = a["cache_k"].shape[1]
    xt = np.concatenate([a["x_prompt"].reshape(SEQ, D), a["x_sample"].reshape(NS, D)])
    cw = a["conv_w"][0]
    d = {
        "xin": xt.T.reshape(KT, P, T).transpose(1, 0, 2),
        "kcache": a["cache_k"][0].transpose(0, 2, 3, 1).reshape(npool, HP, P, PAGE).transpose(0, 2, 1, 3).reshape(npool, P, WA),
        "vcache": a["cache_v"][0].reshape(npool, PAGE, WA),
        "pages": a["page_table"].reshape(1, -1),
        "s0t": a["state_wkv"][0].transpose(1, 3, 0, 2).reshape(HP, P, DB, HD).transpose(1, 0, 2, 3).reshape(P, -1),
        "sshift": a["state_tshift"][0].T.reshape(NPB, P, DB).transpose(1, 0, 2),
        "sconv": a["state_conv"][0].transpose(2, 0, 1).reshape(2 * NF, P, DB * 2).transpose(1, 0, 2),
        "pvec": np.concatenate([fm(a[n][0].reshape(-1)) for n in ("ln1_g", "mu", "w0", "a0", "k_k", "k_a", "r_k", "lnx_g", "lnx_b", "ln2_g")]
                               + [fm(a["lnf_g"]), fm(cw[0]), fm(cw[1]), fm(cw[2]), fm(a["conv_b"][0])], axis=1),
        "consts": constants(),
        "lora": np.concatenate([np.concatenate([a["w2"][0], a["a2"][0]]), a["g2"][0]], axis=1),
        "w_in": tiles(a["w_in"][0], KT),
        "w_br": np.concatenate([tiles(a["w_br_a"][0], HP), tiles(a["w_br_b"][0], HP)], axis=2),
        "w_o": tiles(a["w_o"][0], KT),
        "w_up": tiles(a["w_up"][0], KT),
        "w_down": tiles(a["w_down"][0], NF),
    }
    nc = bacc.Bacc("TRN2", target_bir_lowering=False, num_devices=1)
    arrays, args = {}, []
    for name in _ARGS:
        v = np.ascontiguousarray(d[name])
        arrays["in_" + name] = v
        args.append(nc.dram_tensor("in_" + name, v.shape, mybir.dt.from_np(v.dtype), kind="ExternalInput").ap())
    for name, shape in _OUTS:
        args.append(nc.dram_tensor("out_" + name, shape, F32, kind="ExternalOutput").ap())
    build(nc, *args)
    res = run_bass_kernel_spmd(nc, [arrays], core_ids=[0]).results[0]
    o = {name: np.asarray(res["out_" + name]) for name, _ in _OUTS}
    y = o["yT"].transpose(2, 1, 0).reshape(T, D)
    k = o["kT"].transpose(2, 1, 0).reshape(T, WA)
    v = o["v"].transpose(1, 0, 2).reshape(SEQ, WA)
    tsh = o["tsh"].transpose(2, 1, 0).reshape(9, NPB * P)
    conv = o["conv"].transpose(2, 1, 0).reshape(9, 2, 2 * DFF)
    wp = o["wkvp"].reshape(2, HD, HP, HD).transpose(2, 0, 3, 1).reshape(1, 1, 8, HD, HD)
    ws = o["wkvs"].reshape(2, HD, HP, DB, HD).transpose(3, 2, 0, 4, 1).reshape(1, DB, 8, HD, HD)
    c = np.ascontiguousarray
    return (c(y[:SEQ].reshape(1, SEQ, D)), c(y[SEQ:].reshape(DB, DT, D)),
            c(k[:SEQ].reshape(1, 1, SEQ, 8, HD)), c(v.reshape(1, 1, SEQ, 8, HD)), c(wp),
            c(tsh[0:1].reshape(1, 1, -1)), c(conv[0:1].reshape(1, 1, 2, -1)),
            c(k[SEQ:].reshape(1, DB, DT, 8, HD)), c(o["vs"].reshape(1, DB, DT, 8, HD)), c(ws),
            c(tsh[1:].reshape(1, DB, -1)), c(conv[1:].reshape(1, DB, 2, -1)))
```

```python
from contextlib import ExitStack

import numpy as np

import concourse.bass as bass
from concourse import mybir

F32 = mybir.dt.float32
F32R = mybir.dt.float32r
I32 = mybir.dt.int32
ALU = mybir.AluOpType
ACT = mybir.ActivationFunctionType
AX = mybir.AxisListType

P = 128
D = 1024
KT = D // P
SEQ = 512
DB, DT = 8, 8
NS = DB * DT
T = SEQ + NS
HALF = T // 2
HD = 64
HP = 4
WA = 512
NPB = 1792 // P
NG = D // P
DFF = 2816
NF = DFF // P
PAST = 4096
PAGE = 128
NPG = PAST // PAGE
GP = 4
NGRP = NPG // GP
BLK = 256
NBLK = PAST // BLK
TOPK = 3
C = 64
NCH = SEQ // C
SCALE = HD ** -0.5
NEG = -1e30
EPS = 1e-6
GN_EPS = 64e-5
EM05 = float(np.exp(-0.5))
LEVELS = 6
ARENA = 52864
ALIGN = 8
W_GATE = 26
W_OUT = W_GATE + 3 * NG
W_UP = W_OUT + KT
W_DOWN = W_UP + 2 * NF
KH = NF // 2

PV = {}
_at = 0
for _n, _w in (("ln1", 8), ("mu", 14), ("w0", 4), ("a0", 4), ("kk", 4), ("ka", 4), ("rk", 4), ("lg", 4),
               ("lb", 4), ("ln2", 8), ("lnf", 8), ("cw0", 44), ("cw1", 44), ("cw2", 44), ("cb", 44)):
    PV[_n] = _at
    _at += _w
NPV = _at

CV = {}
_at = 0
for _n, _w in (("ident", 128), ("ones", 128), ("bones", 128), ("causal", 128), ("eye2", 128),
               ("mp0", 128), ("mp1", 128), ("ms0", 128), ("ms1", 128), ("lvl", LEVELS * 128),
               ("colm", DB * 64), ("rowm", DB), ("newm", DB * 64), ("tri", 256), ("reset", T)):
    CV[_n] = _at
    _at += _w
NCV = _at


def constants():
    c = np.zeros((P, NCV), np.float32)
    p = np.arange(P)
    f = np.arange(P)
    s = (p % 64)[:, None]
    t = np.arange(64)[None, :]

    def put(name, a):
        a = np.asarray(a, np.float32).reshape(P, -1)
        c[:, CV[name]:CV[name] + a.shape[1]] = a

    put("ident", np.eye(P))
    put("ones", np.ones((P, P)))
    put("bones", (p[:, None] // 64) == (f[None, :] // 64))
    put("causal", np.where(f[None, :] <= p[:, None], 0.0, NEG))
    eye = s == t
    put("eye2", np.concatenate([eye, eye], 1))
    same = (s // DT) == (t // DT)
    put("mp0", np.concatenate([t < s, s < t], 1))
    put("mp1", np.concatenate([s < t, s <= t], 1))
    put("ms0", np.concatenate([(t < s) & same, (s < t) & same], 1))
    put("ms1", np.concatenate([(s < t) & same, (s <= t) & same], 1))
    lv = []
    for l in range(LEVELS):
        m = 1 << l
        low = (s // (2 * m) == t // (2 * m)) & ((s // m) % 2 == 1) & ((t // m) % 2 == 0)
        up = (s // (2 * m) == t // (2 * m)) & ((t // m) % 2 == 1) & ((s // m) % 2 == 0)
        lv.append(np.concatenate([low, up], 1))
    put("lvl", np.concatenate(lv, 1))
    b = np.arange(DB)
    put("colm", np.broadcast_to((np.arange(64)[None, :] // DT == b[:, None])[None], (P, DB, 64)))
    put("rowm", ((p % 64) // DT)[:, None] == b[None, :])
    tt = (p % DT)[:, None, None]
    key = np.arange(64)[None, None, :]
    ok = (key // DT == b[None, :, None]) & (key % DT <= tt)
    put("newm", np.where(ok, 0.0, NEG))
    i = np.arange(NBLK)
    put("tri", np.broadcast_to((i[None, :] < i[:, None])[None], (P, NBLK, NBLK)))
    start = np.ones(T)
    start[np.arange(0, SEQ, C)] = 0
    start[np.arange(SEQ, T, DT)] = 0
    put("reset", np.broadcast_to(start[None], (P, T)))
    return c


class Line:

    def __init__(self, eng, sem, base=0):
        self.eng, self.sem, self.base, self.n = eng, sem, base, 0

    def did(self, ins):
        ins.then_inc(self.sem, 1)
        self.n += 1
        return ins

    def settle(self):
        self.eng.wait_ge(self.sem, self.base + self.n)


def build(nc, xin, kcache, vcache, pages, s0t, sshift, sconv, pvec, consts, lora, w_in, w_br, w_o, w_up, w_down,
          yT, kT_out, v_out, vs_out, wkvp, tsh_out, conv_out, wkvs):
    ctx = ExitStack()
    with ctx:
        with nc.sbuf_tensor("below_ptab", [P, ARENA], F32), nc.sbuf_tensor("ptab", [1, DB * NPG], I32) as ptab:
            pass
        placed = [0]

        def view(at, *shape, dtype=F32):
            placed[0] += 1
            n = int(np.prod(shape))
            assert at + n <= ARENA and at % ALIGN == 0
            with ExitStack() as scope:
                if at:
                    scope.enter_context(nc.sbuf_tensor(f"before{placed[0]}", [P, at], F32))
                v = scope.enter_context(nc.sbuf_tensor(f"buffer{placed[0]}_at{at}", [P, n], dtype))[:, :]
            if len(shape) == 2:
                return v.rearrange("p (a b) -> p a b", a=shape[0])
            if len(shape) == 3:
                return v.rearrange("p (a b c) -> p a b c", a=shape[0], b=shape[1])
            return v

        def split_view(at, *shape):
            return view(at, *shape, dtype=F32R)

        xh, xl = split_view(39296, KT, T), split_view(4608, KT, T)
        wl = [split_view(9216 + 1024 * i, KT, P) for i in range(4)]
        wh = [split_view(a, KT, P) for i, a in enumerate((34304, 35328, 37760))]
        wvh = [view(27392 + 2048 * i, 2, KT, P, dtype=F32R) for i in range(2)]
        wvl = [view(9216 + 2048 * i, 2, KT, P, dtype=F32R) for i in range(2)]
        oah, oal = split_view(20224, HP, T), split_view(13312, HP, T)
        ybh, ybl = split_view(22528, HP, T), split_view(15616, HP, T)
        mh, ml = split_view(29696, KT, T), split_view(25088, KT, T)
        wuh = [split_view(13312 + 1024 * i, KT, P) for i in range(2)]
        hhh, hhl = split_view(4608, NF, T), split_view(17280, NF, T)
        wdh = [split_view(37888 + 1408 * i, KH, P) for i in range(4)]
        wdl = [split_view(29952 + 1408 * i, KH, P) for i in range(4)]
        ps = ctx.enter_context(nc.psum_tensor("ps", [P, 8, 512], F32))

        def sem(name):
            return ctx.enter_context(nc.semaphore(name))

        def sems(name, n):
            return [sem(f"{name}{i}") for i in range(n)]

        x = view(0, KT, T)
        xn = view(4608, KT, T)
        wr = [view(9216 + 1024 * i, KT, P) for i in range(4)]
        kring = [view(4608 + 2048 * i, GP, HP, PAGE) for i in range(4)]
        vring = [view(4608 + 2048 * i, GP, WA) for i in range(4)]
        oa = view(13312, HP, T)
        yb = view(15616, HP, T)
        sqb = [view(17920 + T * i, T) for i in range(2)]
        ub = [view(15616 + 600 * i, 600) for i in range(2)]
        df = view(15616 + 1200, 600)
        qk = view(17920, 2 * HP, T)
        tmp = [view(17920 + T * i, T) for i in range(8)]
        s0 = view(17920, HP, DB, 64)
        ex = [view(17920 + 2048 + 512 * i, DB, 64) for i in range(4)]
        lg = view(17920, PAST + NS)
        vp = view(22528, HP, WA)
        vsm = view(22528 + 2048, WA)
        rw = view(25088, 20, T)
        R, K, V, AL, BE = (rw[:, 4 * i:4 * i + 4, :] for i in range(5))
        wad = view(36608, T)
        gd = view(36608 + T, T)
        stg = view(37760, 20, C)
        sR, sK, sV, sA, sB = (stg[:, 4 * i:4 * i + 4, :] for i in range(5))
        aa = view(39040, 2, HP, C)
        mm1 = view(39552, 2, HP, C)
        mkv = view(40064, 2, HP, C)
        bk = view(40576, 2, HP, C)
        tt = view(41088, 2, HP, C)
        amt = view(41600, LEVELS - 1, HP, C)
        xx = view(42880, HP, C)
        ww = view(43136, HP, C)
        uu = view(43392, HP, C)
        st = view(43648, HP, C)
        pr = [view(37760 + 512 * i, SEQ) for i in range(2)]
        prT = [view(37760 + 1024 + 512 * i, HP, P) for i in range(2)]
        at = [43904]

        def take(*shape):
            v = view(at[0], *shape)
            at[0] += -(-int(np.prod(shape)) // ALIGN) * ALIGN
            return v

        cst = take(NCV)
        pv = take(NPV)
        omka = take(HP)
        shs = take(NPB, DB)
        lo = take(2 * WA)
        w2a2, g2 = lo[:, 0:WA], lo[:, WA:2 * WA]
        qks = take(2 * HP, NS)
        tsh = take(NPB, 9)
        qbd = take(HP, 32)
        lc = take(HP, 16)
        gs = take(16)
        bm = take(17)
        mb = take(17)
        bi = take(17)
        psm = take(17)
        sc = take(8)
        cmp1 = take(16, 16)
        cmp2 = take(16, 16)
        mx = take(8)
        nmx = take(8)
        rsm = take(8)
        rin = take(8)
        pT = [take(GP, P) for _ in range(2)]
        ob = take(P)
        rs = take(T)
        assert at[0] <= ARENA, at[0]
        m = view(25088, KT, T)
        g0 = view(17920, T)
        g1 = view(17920 + T, T)
        hh = view(17280, NF, T)
        wd = [view(29952 + 1408 * i, KH, P) for i in range(4)]
        cu = [view(31360 + 608 * i, 608) for i in range(4)]
        cc = [view(33792 + 592 * i, 592) for i in range(4)]
        scv = view(36160, 2 * NF, DB * 2)
        cvo = view(36864, 2 * NF, 18)

        ident, ones, bones, causal = (cst[:, CV[n]:CV[n] + P] for n in ("ident", "ones", "bones", "causal"))
        reset = cst[:, CV["reset"]:CV["reset"] + T]
        tri = cst[:, CV["tri"]:CV["tri"] + 256].rearrange("p (a b) -> p a b", a=16)
        colm = cst[:, CV["colm"]:CV["colm"] + 512].rearrange("p (a b) -> p a b", a=DB)
        rowm = cst[:, CV["rowm"]:CV["rowm"] + DB]

        def mpair(name, at=0):
            a = CV[name] + at
            return cst[:, a:a + 128].rearrange("p (a o b) -> p a o b", a=2, o=1).to_broadcast([P, 2, HP, C])

        def mone(name, at=0):
            a = CV[name] + at
            return cst[:, a:a + 64].rearrange("p (o b) -> p o b", o=1).to_broadcast([P, HP, C])

        def pcol(name, i):
            if isinstance(i, int):
                return pv[:, PV[name] + i:PV[name] + i + 1]
            return pv[:, bass.ds(i + PV[name], 1)]

        def tile_of(w, i):
            if isinstance(i, int):
                return w[i]
            return w[bass.ds(i, 1)].rearrange("o p k n -> p (o k) n")

        def pair(b):
            return ps[:, 2 * b:2 * b + 2, 0:HALF]

        def lin(a):
            return a.rearrange("p (h n) -> p h n", h=2)

        def lin3(a):
            return a.rearrange("p o (h n) -> p (o h) n", h=2)

        def q4(bank, j=0):
            return ps[:, bank, 256 * j:256 * j + 256].rearrange("p (a b) -> p a b", a=HP)

        def q8(bank):
            return ps[:, bank, :].rearrange("p (c a b) -> p c a b", c=2, a=HP)

        def heads():
            for hp in range(HP):
                for half in range(2):
                    yield hp, slice(64 * half, 64 * half + 64)

        s_c0, s_c1, s_pv, s_pt, s_lora, s_s0, s_sc = (sem(n) for n in (
            "ones_in", "const_in", "params_in", "pages_in", "lora_in", "states_in", "conv_in"))
        s_x = sems("x_in", 4)
        w_a, w_g, w_ob, w_u, w_d = sems("w_in", 4), sems("w_gate", 3), sems("w_o", 4), sems("w_up", 4), sems("w_down", 4)
        w_hi, w_lo, xh_ready, xs_even, xs_odd, hh_hi, hh_lo, yb_split, oa_split, st_stored = (sem(n) for n in (
            "w_hi", "w_lo", "xn_hi", "xn_lo_even", "xn_lo_odd", "hh_hi", "hh_lo", "yb_split", "oa_split", "state_stored"))
        kv_in = sems("kv_in", 4)
        sq_ready, sq_used, ms_ready, rt_ready, xn_ready = (sem(n) for n in ("sq_ready", "sq_used", "ms_ready", "rt_ready", "xn_ready"))
        qk_tile, qk_out, v_tile, v_evac, rw_tile, u_ready, xm_done, tsh_done, qks_done = (sem(n) for n in (
            "qk_tile", "qk_out", "v_tile", "v_evac", "rw_tile", "u_ready", "xm_done", "tsh_done", "qks_done"))
        own = {n: sem("own_" + n) for n in ("setup", "shift", "attn", "prep", "chunk0", "loop", "gn", "merge", "up", "norm", "ch0", "chl")}
        init_done = sem("init_done")
        at_lg, at_mx, at_ex, at_pn, at_tp, at_tc, at_pv, at_oe = (sem(n) for n in (
            "at_logits", "at_max", "at_exp", "at_norm", "at_transposed", "at_pt", "at_pv", "at_out"))
        pr_sq, pr_ss, pr_mx, pr_rt, pr_kk, pr_lin, pr_w, pr_sig, pr_exc, pr_exp, pr_b, pr_bp, pr_done = (sem(n) for n in (
            "kk_sq", "kk_ss", "kk_ms", "kk_rt", "kk_done", "lora_act", "lora_mm", "lora_sig", "excl", "decays", "bonus_in", "bonus_mm", "prep_done"))
        ch_stg, ch_g, ch_ev, ch_amt, ch_x, ch_xe, ch_d, ch_te, ch_w, ch_we, ch_u, ch_ue, ch_y, ch_ye, ch_s, st_ready = (sem(n) for n in (
            "c_staged", "c_gram", "c_gram_out", "c_levels", "c_x", "c_x_out", "c_d", "c_t", "c_w", "c_w_out", "c_u", "c_u_out",
            "c_y", "c_y_out", "c_s", "state_ready"))
        ss_ex, ss_w, ss_we, ss_u, ss_ue, ss_y, ss_s, ss_st = (sem(n) for n in (
            "ss_exp", "ss_w", "ss_w_out", "ss_u", "ss_u_out", "ss_y", "ss_s", "ss_state"))
        sa_q, kv_used, sa_ev, sa_lg, sa_bi, sa_ex, sa_tp, sa_tc, sa_nw, sa_ob, sa_ot, sa_oo = (sem(n) for n in (
            "s_q", "kv_used", "s_logits_out", "s_new_logits", "s_bias", "s_exp", "s_transposed", "s_pt", "s_pv_new",
            "s_o", "s_ot", "s_oa"))
        gn_mm, gn_sq, gn_v, gn_rt, gn_out = (sem(n) for n in ("gn_mm", "gn_sq", "gn_var", "gn_rt", "gn_out"))
        ga_mm, ga_sig, m_done = sem("gate_mm"), sem("gate_sig"), sem("m_done")
        ga_free = sems("gate_free", 4)
        o_mm, h_done = sem("o_mm"), sem("h_done")
        up_mm, up_ev, up_st, up_c0, up_cv, up_si, up_h, up_cp, up_z = (sem(n) for n in (
            "up_mm", "up_u", "up_state", "up_c0", "up_cv", "up_silu", "up_h", "up_conv_out", "up_zero"))
        dn_mm, y_done = sem("down_mm"), sem("y_done")
        stored = sem("stored")
        k_stored, ws_stored = sem("k_stored"), sem("wkvs_stored")
        waited = sem("waited")
        N_STORES = 6

        block = ctx.enter_context(nc.Block())

        @block.sync
        def _(e):
            e.dma_start(cst[:, 0:256], consts[:, 0:256]).then_inc(s_c0, 16)
            for i in range(4):
                e.dma_start(x[:, 2 * i:2 * i + 2, :], xin[:, 2 * i:2 * i + 2, :]).then_inc(s_x[i], 16)
            e.dma_start(pv[:, :], pvec).then_inc(s_pv, 16)
            for s in range(4):
                e.dma_start(wr[s], w_in[s]).then_inc(w_a[s], 16)
            e.dma_start(cst[:, 256:NCV], consts[:, 256:NCV]).then_inc(s_c1, 16)
            e.dma_start(shs[:, :, :], sshift).then_inc(s_c1, 16)
            e.dma_start(lo[:, :], lora).then_inc(s_lora, 16)
            e.dma_start(ptab[:, :], pages).then_inc(s_pt, 16)

            def w_tile(i, s, used, n):
                e.wait_ge(used, n)
                e.dma_start(wr[s], tile_of(w_in, i)).then_inc(w_a[s], 16)

            for s in range(4):
                w_tile(4 + s, s, qk_tile, s + 1)
            for s in range(4):
                w_tile(8 + s, s, qk_tile, 4 + s + 1)
            for s in range(4):
                w_tile(12 + s, s, v_tile, 5 * (s // 2 + 1))
            with e.Fori(0, 2) as it:
                for s in range(4):
                    w_tile(it * 4 + (16 + s), s, rw_tile, it * 4 + (s + 1))
            for s in range(2):
                w_tile(24 + s, s, rw_tile, 8 + s + 1)

            e.wait_ge(qk_out, 2 * HP)
            e.dma_start(kT_out, qk[:, HP:2 * HP, :]).then_inc(k_stored, 16)
            e.wait_ge(v_evac, 10)
            e.dma_start(v_out, vp[:, :, :]).then_inc(stored, 16)
            e.dma_start(vs_out, vsm[0:NS, :]).then_inc(stored, 16)
            e.wait_ge(tsh_done, NPB)
            e.dma_start(tsh_out, tsh[:, :, :]).then_inc(stored, 16)

            e.wait_ge(s_pt, 16)
            e.wait_ge(rw_tile, NPB)

            def page_group(b, g, value, n):
                _, pgs = nc.values_load_multi_w_load_instructions(
                    ptab[0:1, bass.ds(b * NPG + g * GP, GP)], engines=(mybir.EngineType.SP,), min_val=0, max_val=kcache.shape[0] - 1)
                if n is not None:
                    e.wait_ge(kv_used, n)
                for q, pg in enumerate(pgs):
                    slot = (vring if value else kring)[g % 4][:, q:q + 1]
                    slot = slot.rearrange("p o a -> p (o a)") if value else slot.rearrange("p o a b -> p (o a b)")
                    cache = vcache if value else kcache
                    e.dma_start(slot, cache[bass.ds(pg, 1)].rearrange("o p n -> p (o n)")).then_inc(kv_in[g % 4], 16)

            for g in range(4):
                page_group(0, g, False, None)
            e.wait_ge(pr_done, 1)
            e.dma_start(s0[:, :, :, :].rearrange("p a b c -> p (a b c)"), s0t).then_inc(s_s0, 16)
            e.wait_ge(ss_st, HP)
            e.dma_start(wkvs, s0[:, :, :, :].rearrange("p a b c -> p (a b c)")).then_inc(ws_stored, 16)
            for g in range(4, NGRP):
                page_group(0, g, False, g - 3)
            for g in range(NGRP):
                page_group(0, g, True, NGRP + g - 3)
            with e.Fori(1, DB) as b:
                for g in range(NGRP):
                    page_group(b, g, False, b * (2 * NGRP) + (g - 3))
                for g in range(NGRP):
                    page_group(b, g, True, b * (2 * NGRP) + (NGRP + g - 3))

            e.wait_ge(st_ready, NCH + 1)
            e.dma_start(wkvp, st[:, :, :].rearrange("p a b -> p (a b)")).then_inc(st_stored, 16)
            e.wait_ge(kv_used, 2 * DB * NGRP)
            for s in range(2):
                e.dma_start(wr[s], w_in[26 + 8 * s]).then_inc(w_g[s], 16)
            e.dma_start(wr[2], w_br[0]).then_inc(w_g[2], 16)
            with e.Fori(1, NG) as c:
                for s in range(2):
                    e.wait_ge(ga_mm, c * 4 + (s - 3))
                    e.dma_start(wr[s], tile_of(w_in, c + (26 + 8 * s))).then_inc(w_g[s], 16)
                e.wait_ge(ga_mm, c * 4)
                e.dma_start(wr[2], tile_of(w_br, c)).then_inc(w_g[2], 16)
            for i in range(KT):
                if i in (1, 2, 3):
                    e.wait_ge(ga_mm, (0, 4 * NG - 3, 4 * NG - 2, 4 * NG)[i])
                elif i >= 4:
                    e.wait_ge(o_mm, i - 3)
                e.dma_start(wr[(i + 3) % 4], w_o[i]).then_inc(w_ob[(i + 3) % 4], 16)

            def up_tiles(it):
                for s in range(4):
                    if isinstance(it, int):
                        e.wait_ge(o_mm, (6, 7, 8, 5)[s])
                    else:
                        e.wait_ge(up_mm, it * 4 + (s - 3))
                    e.dma_start(wr[s], tile_of(w_up, it * 2 + (s // 2 + NF * (s % 2)))).then_inc(w_u[s], 16)

            up_tiles(0)
            e.dma_start(scv[:, :, :], sconv).then_inc(s_sc, 16)
            with e.Fori(1, NF // 2) as it:
                up_tiles(it)

            def down_half(c, h, s):
                e.dma_start(wd[s], tile_of(w_down, c)[:, h * KH:(h + 1) * KH, :]).then_inc(w_d[s], 16)

            down_half(0, 0, 0)
            e.wait_ge(up_h, NF)
            e.wait_ge(up_cp, 2 * NF)
            for s in range(1, 4):
                down_half(s // 2, s % 2, s)
            with e.Fori(1, KT // 2) as it:
                for s in range(4):
                    e.wait_ge(dn_mm, it * 4 + (s - 3))
                    down_half(it * 2 + s // 2, s % 2, s)
            e.wait_ge(up_cp, 2 * NF)
            e.dma_start(conv_out, cvo[:, :, :]).then_inc(stored, 16)
            for i in range(2):
                e.wait_ge(xn_ready, 3 * KT + 4 * (i + 1))
                e.dma_start(yT[:, 4 * i:4 * i + 4, :], xn[:, 4 * i:4 * i + 4, :]).then_inc(stored, 16)
            e.wait_ge(k_stored, 16)
            e.wait_ge(ws_stored, 16)
            e.wait_ge(st_stored, 16)
            e.wait_ge(stored, 16 * N_STORES)

        @block.tensor
        def _(e):
            def wait(s, n):
                e.wait_ge(s, n)
                e.sem_inc(waited, 1)

            def sumsq(n):
                for k in range(KT):
                    e.wait_ge(sq_ready, n * KT + k + 1)
                    for h in range(2):
                        i = e.matmul(ps[:, h, 0:HALF], ones, sqb[k % 2][:, h * HALF:(h + 1) * HALF],
                                     start=(k == 0), stop=(k == KT - 1))
                    i.then_inc(sq_used, 1)

            def split_product(outs, w, act, start, stop):
                wh_, wl_ = w
                for i, (lhs, rhs) in enumerate(((wh_, act[0]), (wh_, act[1]), (wl_, act[0]))):
                    for out, cols in outs:
                        ins = e.matmul(out, lhs, rhs[:, cols], start=(start and i == 0), stop=(stop and i == 2))
                return ins

            def halves_of(b):
                return [(ps[:, 2 * b + h, 0:HALF], slice(h * HALF, (h + 1) * HALF)) for h in range(2)]

            def padded_of(b):
                return [(ps[:, 2 * b, 0:256], slice(0, 256)), (ps[:, 2 * b + 1, 0:320], slice(256, T))]

            def project(outs, w, act, nk, done, k0=0, start=True, stop=True, a0=0, act_ready=None):
                for k in range(nk):
                    if act_ready is not None:
                        act_ready(a0 + k)
                    i = split_product(outs, (w[0][:, k0 + k, :], w[1][:, k0 + k, :]), (act[0][:, a0 + k, :], act[1][:, a0 + k, :]),
                                      start and k == 0, stop and k == nk - 1)
                i.then_inc(done, 1)

            def xn_split(n):
                def ready(k):
                    e.wait_ge((xs_even, xs_odd)[k % 2], n * (KT // 2) + k // 2 + 1)
                return ready

            xs = (xh, xl)
            e.wait_ge(s_c0, 16)
            sumsq(0)
            for r in range(2):
                for s in range(4):
                    e.wait_ge(w_lo, 4 * r + s + 1)
                    if r:
                        e.wait_ge(qk_out, s + 1)
                    project(halves_of(s), (wh[s % 2], wl[s]), xs, KT, qk_tile, act_ready=xn_split(0) if not r and not s else None)
            for j in range(2):
                e.wait_ge(w_lo, 8 + 2 * j + 2)
                for t4 in range(5):
                    if j == 0:
                        e.wait_ge(qk_out, 4 + t4 // 2 + 1)
                    else:
                        e.wait_ge(v_evac, t4 + 1)
                    t0 = t4 * P if t4 < 4 else T - P
                    for k in range(KT):
                        for n, (a, w) in enumerate(((xh, wvh), (xh, wvl), (xl, wvh))):
                            i = e.matmul(ps[:, t4, 256 * j:256 * j + 256], a[:, k, t0:t0 + P], w[j][:, :, k, :],
                                         start=(k == 0 and n == 0), stop=(k == KT - 1 and n == 2))
                    i.then_inc(v_tile, 1)
            for s in range(4):
                e.wait_ge(w_lo, 12 + s + 1)
                e.wait_ge(v_evac, (7, 9, 10, 10)[s])
                project(padded_of(s), (wh[s % 2], wl[s]), xs, KT, rw_tile)

            def rw_proj(it, s):
                e.wait_ge(w_lo, it * 4 + (12 + s + 1))
                e.wait_ge(u_ready, it * 4 + (s - 3))
                project(padded_of(s), (wh[s % 2], wl[s]), xs, KT, rw_tile)

            with e.Fori(1, 3) as it:
                for s in range(4):
                    rw_proj(it, s)
            for s in range(2):
                rw_proj(3, s)

            units = [(h, qt) for h in range(8) for qt in range(4)]
            e.wait_ge(u_ready, NPB)
            e.wait_ge(s_c1, 32)

            def logits(u):
                h, qt = units[u]
                hp, r = h // 2, slice(64 * (h % 2), 64 * (h % 2) + 64)
                if u >= 4:
                    e.wait_ge(at_ex, u - 3)
                e.matmul(ps[:, u % 4, 0:P * (qt + 1)], qk[r, hp, qt * P:(qt + 1) * P], qk[r, HP + hp, 0:P * (qt + 1)],
                         start=True, stop=True).then_inc(at_lg, 1)

            def turn(u):
                h, qt = units[u]
                e.wait_ge(at_pn, u + 1)
                if u >= 2:
                    e.wait_ge(at_tc, u - 1)
                for k in range(qt + 1):
                    i = e.transpose(ps[:, 4 + u % 2, k * P:(k + 1) * P], pr[u % 2][:, k * P:(k + 1) * P], ident)
                i.then_inc(at_tp, 1)

            def values(u):
                h, qt = units[u]
                hp, r = h // 2, slice(64 * (h % 2), 64 * (h % 2) + 64)
                e.wait_ge(at_tc, u + 1)
                if u % 8 == 0 and hp >= 2:
                    e.wait_ge(at_oe, hp - 1)
                for k in range(qt + 1):
                    i = e.matmul(ps[r, 6 + hp % 2, qt * P:(qt + 1) * P], vp[:, k, h * HD:(h + 1) * HD], prT[u % 2][:, k, :],
                                 start=(k == 0), stop=(k == qt))
                i.then_inc(at_pv, 1)

            n = len(units)
            logits(0)
            logits(1)
            for u in range(n + 2):
                if u + 2 < n:
                    logits(u + 2)
                if 1 <= u <= n:
                    turn(u - 1)
                if u >= 2:
                    values(u - 2)

            e.wait_ge(at_oe, HP)
            for hp in range(HP):
                e.wait_ge(pr_sq, hp + 1)
                for h in range(2):
                    i = e.matmul(ps[:, 2 * hp + h, 0:HALF], bones, tmp[hp][:, h * HALF:(h + 1) * HALF], start=True, stop=True)
                i.then_inc(pr_ss, 1)
            e.wait_ge(pr_mx, HP)
            e.wait_ge(s_lora, 16)
            e.wait_ge(pr_lin, 1)
            for hp in range(HP):
                if hp >= 2:
                    e.wait_ge(pr_sig, 2 * (hp - 1))
                for w in range(2):
                    r = slice(64 * w, 64 * w + 64)
                    for h in range(2):
                        i = e.matmul(ps[:, 4 * (hp % 2) + 2 * w + h, 0:HALF], w2a2[r, hp * P:(hp + 1) * P],
                                     wad[r, h * HALF:(h + 1) * HALF], start=True, stop=True)
                    i.then_inc(pr_w, 1)
            e.wait_ge(pr_sig, 2 * HP)
            for hp in range(HP):
                e.wait_ge(pr_b, hp + 1)
                for h in range(2):
                    i = e.matmul(ps[:, h, 0:HALF], bones, tmp[5][:, h * HALF:(h + 1) * HALF], start=True, stop=True)
                i.then_inc(pr_bp, 1)

            def gram(n, bank):
                if bank == 0:
                    wait(ch_stg, n + 1)
                ops = (((sA, sB), (sB, sA)), ((sK, sA), (sB, sR)), ((sK, sR), (sV, None)), ((sB, None), (sK, None)))[bank]
                for j, (lhs, rhs) in enumerate(ops):
                    for hp, r in heads():
                        right = rhs[r, hp, :] if rhs is not None else ident[r, r]
                        i = e.matmul(ps[r, bank, j * 256 + hp * C:j * 256 + (hp + 1) * C], lhs[r, hp, :], right,
                                     start=True, stop=True)
                i.then_inc(ch_g, 1)

            def level_x(n, l):
                if l == 0:
                    wait(ch_amt, n + 1)
                wait(ch_te, n * LEVELS + (l + 1))
                for hp, r in heads():
                    i = e.matmul(ps[r, 0, hp * C:(hp + 1) * C], amt[r, l, hp, :], tt[r, 0, hp, :], start=True, stop=True)
                i.then_inc(ch_x, 1)

            def level_d(n, l):
                if l == 0:
                    wait(ch_ev, n * 5 + 5)
                wait(ch_xe, n * (LEVELS - 1) + (l + 1))
                for hp, r in heads():
                    e.matmul(ps[r, 1, hp * C:(hp + 1) * C], tt[r, 1, hp, :], xx[r, hp, :], start=True, stop=True)
                for hp, r in heads():
                    i = e.matmul(ps[r, 1, 256 + hp * C:256 + (hp + 1) * C], xx[r, hp, :], tt[r, 1, hp, :],
                                 start=True, stop=True)
                i.then_inc(ch_d, 1)

            def chunk_w(c):
                wait(st_ready, c + 1)
                for hp, r in heads():
                    e.matmul(ps[r, 2, hp * C:(hp + 1) * C], sA[r, hp, :], st[r, hp, :], start=True, stop=False)
                    i = e.matmul(ps[r, 2, hp * C:(hp + 1) * C], mm1[r, 0, hp, :], mkv[r, 1, hp, :], start=False, stop=True)
                i.then_inc(ch_w, 1)

            def chunk_u(c):
                wait(ch_we, c + 1)
                wait(ch_te, c * LEVELS + 2 * LEVELS)
                for hp, r in heads():
                    i = e.matmul(ps[r, 3, hp * C:(hp + 1) * C], tt[r, 1, hp, :], ww[r, hp, :], start=True, stop=True)
                i.then_inc(ch_u, 1)

            def chunk_y(c):
                wait(ch_ue, c + 1)
                for hp, r in heads():
                    d = ps[r, 2, hp * C:(hp + 1) * C]
                    e.matmul(d, st[r, hp, :], sR[r, hp, :], start=True, stop=False)
                    e.matmul(d, uu[r, hp, :], mm1[r, 1, hp, :], start=False, stop=False)
                    i = e.matmul(d, mkv[r, 1, hp, :], mkv[r, 0, hp, :], start=False, stop=True)
                i.then_inc(ch_y, 1)
                for hp, r in heads():
                    d = ps[r, 0, hp * C:(hp + 1) * C]
                    e.matmul(d, bk[r, 0, hp, :], uu[r, hp, :], start=True, stop=False)
                    i = e.matmul(d, bk[r, 1, hp, :], mkv[r, 1, hp, :], start=False, stop=True)
                i.then_inc(ch_s, 1)

            e.wait_ge(pr_done, 1)
            for bank in range(4):
                gram(0, bank)
            for l in range(LEVELS - 1):
                level_x(0, l)
                level_d(0, l)
            wait(ch_te, LEVELS)
            e.wait_ge(s_s0, 16)
            halves = [slice(0, 64), slice(64, 128)]
            for hp in range(HP):
                cols = slice(hp * C, (hp + 1) * C)
                e.wait_ge(ss_ex, 2 * hp + 1)
                for r in halves:
                    for b in range(DB):
                        e.matmul(ps[r, 2, cols], ex[0][r, b, :], s0[r, hp, b, :], start=(b == 0), stop=False)
                    i = e.matmul(ps[r, 2, cols], mm1[r, 0, hp, :], mkv[r, 1, hp, :], start=False, stop=True)
                i.then_inc(ss_w, 1)
                e.wait_ge(ss_we, hp + 1)
                for r in halves:
                    i = e.matmul(ps[r, 3, cols], tt[r, 1, hp, :], ww[r, hp, :], start=True, stop=True)
                i.then_inc(ss_u, 1)
                e.wait_ge(ss_ue, hp + 1)
                for r in halves:
                    for b in range(DB):
                        e.matmul(ps[r, 4, cols], s0[r, hp, b, :], ex[1][r, b, :], start=(b == 0), stop=False)
                    e.matmul(ps[r, 4, cols], mkv[r, 1, hp, :], mkv[r, 0, hp, :], start=False, stop=False)
                    i = e.matmul(ps[r, 4, cols], uu[r, hp, :], mm1[r, 1, hp, :], start=False, stop=True)
                i.then_inc(ss_y, 1)
                e.wait_ge(ss_ex, 2 * hp + 2)
                if hp:
                    e.wait_ge(ss_st, hp)
                for r in halves:
                    e.matmul(ps[r, 6, :], bk[r, 0, hp, :], ex[2][r, :, :], start=True, stop=False)
                    i = e.matmul(ps[r, 6, :], bk[r, 1, hp, :], ex[3][r, :, :], start=False, stop=True)
                i.then_inc(ss_s if hp < HP - 1 else ch_s, 1)
            e.wait_ge(ss_st, HP)

            PER = 2 * NGRP

            def qk_group(b, g):
                wait(kv_in[g % 4], b * 256 + 64 * (g // 4 + 1))
                if g >= 2:
                    wait(sa_ev, b * PER + 2 * (g - 1))
                for hp in range(HP):
                    i = e.matmul(ps[32 * hp:32 * hp + 32, 4 + g % 2, :], qbd[:, hp, :], kring[g % 4][:, :, hp, :],
                                 start=True, stop=True)
                i.then_inc(kv_used, 1)

            def pv_turn(b, g):
                wait(sa_ex, b * (NGRP + 1) + (g + 1))
                if g >= 2:
                    wait(sa_tc, b * (NGRP + 1) + (g - 1))
                if g < NGRP:
                    for q in range(GP):
                        i = e.transpose(ps[:, 4 + g % 2, q * P:(q + 1) * P], lg[:, (g * GP + q) * P:(g * GP + q + 1) * P], ident)
                else:
                    i = e.transpose(ps[0:NS, 4 + g % 2, 0:P], lg[:, PAST:PAST + NS], ident)
                i.then_inc(sa_tp, 1)

            def pv_group(b, g):
                wait(sa_tc, b * (NGRP + 1) + (g + 1))
                if g < NGRP:
                    wait(kv_in[g % 4], b * 256 + 64 * (g // 4 + 3))
                    for q in range(GP):
                        for hp in range(HP):
                            i = e.matmul(ps[32 * hp:32 * hp + 32, 7, 0:P], pT[g % 2][:, q, 32 * hp:32 * hp + 32],
                                         vring[g % 4][:, q, hp * P:(hp + 1) * P], start=(g == 0 and q == 0), stop=False)
                    i.then_inc(kv_used, 1)
                else:
                    for hp in range(HP):
                        i = e.matmul(ps[32 * hp:32 * hp + 32, 7, 0:P], pT[g % 2][0:NS, 0, 32 * hp:32 * hp + 32],
                                     vsm[0:NS, hp * P:(hp + 1) * P], start=False, stop=True)
                    i.then_inc(sa_nw, 1)

            e.sem_inc(sa_lg, 1)
            with e.Fori(0, DB) as b:
                wait(sa_q, b * 2 + 2)
                for g in range(NGRP):
                    qk_group(b, g)
                    if g < 2:
                        gram(b + 1, 2 * g)
                        gram(b + 1, 2 * g + 1)
                    elif g % 2 == 0:
                        level_x(b + 1, g // 2 - 1)
                    else:
                        level_d(b + 1, g // 2 - 1)
                wait(sa_ev, b * PER + 2 * (NGRP - 1))
                for hp in range(HP):
                    i = e.matmul(ps[32 * hp:32 * hp + 32, 4, 0:NS], qbd[:, hp, :], qks[:, HP + hp, :], start=True, stop=True)
                i.then_inc(sa_lg, 1)
                for l in range(3, LEVELS - 1):
                    level_x(b + 1, l)
                    level_d(b + 1, l)
                chunk_w(b)
                for g in range(NGRP + 2):
                    if g <= NGRP:
                        pv_turn(b, g)
                    if g >= 1:
                        pv_group(b, g - 1)
                    if g == 1:
                        chunk_u(b)
                    if g == 3:
                        chunk_y(b)
                e.wait_ge(sa_ob, b + 1)
                e.wait_ge(sa_oo, b + 1)
                e.transpose(ps[:, 6, 0:P], ob, ident).then_inc(sa_ot, 1)

            e.wait_ge(ch_ye, NCH)
            e.wait_ge(sa_oo, DB + 1)
            for hp in range(HP):
                if hp:
                    e.wait_ge(gn_out, hp)
                for h in range(2):
                    e.matmul(ps[:, 4 + h, 0:HALF], g2[:, hp * P:(hp + 1) * P], gd[:, h * HALF:(h + 1) * HALF], start=True, stop=True)
                for h in range(2):
                    i = e.matmul(ps[:, h, 0:HALF], bones, R[:, hp, h * HALF:(h + 1) * HALF], start=True, stop=True)
                i.then_inc(gn_mm, 1)
                e.wait_ge(gn_sq, hp + 1)
                for h in range(2):
                    i = e.matmul(ps[:, 2 + h, 0:HALF], bones, tmp[1][:, h * HALF:(h + 1) * HALF], start=True, stop=True)
                i.then_inc(gn_mm, 1)

            e.wait_ge(gn_out, HP)

            def gates(c):
                first = isinstance(c, int)
                for s in range(2):
                    e.wait_ge(w_lo, c * 3 + (W_GATE + s + 1))
                    e.wait_ge(ga_free[s], c + 1)
                    project(halves_of(s), (wh[s], wl[s]), xs, KT, ga_mm, act_ready=xn_split(1) if first and not s else None)
                e.wait_ge(w_lo, c * 3 + (W_GATE + 3))
                for s, act in ((2, (oah, oal)), (3, (ybh, ybl))):
                    if first:
                        e.wait_ge((oa_split, yb_split)[s - 2], (1, HP)[s - 2])
                    e.wait_ge(ga_free[s], c + 1)
                    project(halves_of(s), (wh[2], wl[2]), act, HP, ga_mm, k0=HP * (s - 2))

            gates(0)
            with e.Fori(1, NG) as c:
                gates(c)
            for i in range(KT):
                e.wait_ge(w_lo, W_OUT + i + 1)
                if i == 0:
                    e.wait_ge(ga_free[0], NG + 1)
                elif i < 4:
                    e.wait_ge(ga_free[i], NG + 1)
                else:
                    e.wait_ge(h_done, i - 3)
                project(halves_of(i % 4), (wh[i % 3], wl[(i + 3) % 4]), (mh, ml), KT, o_mm,
                        act_ready=(lambda k: e.wait_ge(m_done, k + 2)) if i == 0 else None)
            e.wait_ge(h_done, KT)
            sumsq(1)

            def up(it):
                first = isinstance(it, int)
                for s in range(4):
                    e.wait_ge(w_lo, it * 4 + (W_UP + s + 1))
                    if not first:
                        e.wait_ge(up_ev, it * 4 + (s - 3))
                    if first and s == 0:
                        e.wait_ge(ms_ready, 2)
                    project(padded_of(s), (wuh[s % 2], wl[s]), xs, KT, up_mm, act_ready=xn_split(2) if first and not s else None)

            up(0)
            with e.Fori(1, NF // 2) as it:
                up(it)

            def down(it):
                first = isinstance(it, int)
                for s in range(4):
                    e.wait_ge(w_lo, it * 4 + (W_DOWN + s + 1))
                    if not first and s % 2 == 0:
                        e.wait_ge(y_done, it * 2 + (s // 2 - 1))
                    project(halves_of(s // 2), (wdh[s], wdl[s]), (hhh, hhl), KH, dn_mm, start=(s % 2 == 0), stop=(s % 2 == 1),
                            a0=KH * (s % 2), act_ready=(lambda k: e.wait_ge(hh_lo, k + 1)) if first and s < 2 else None)

            down(0)
            with e.Fori(1, KT // 2) as it:
                down(it)
            e.wait_ge(y_done, KT)
            sumsq(2)

        @block.scalar
        def _(e):
            def squares(n):
                for k in range(KT):
                    if n == 0:
                        e.wait_ge(s_x[k // 2], 16)
                    if k >= 2:
                        e.wait_ge(sq_used, n * KT + k - 1)
                    e.activation(sqb[k % 2], x[:, k, :], ACT.Square).then_inc(sq_ready, 1)

            def root(n):
                e.wait_ge(ms_ready, n + 1)
                e.activation(rs, rs, ACT.Sqrt).then_inc(rt_ready, 1)

            def w_split(hi, raw, arrived, n):
                e.wait_ge(arrived, n)
                e.activation(hi[:, :, :], raw, ACT.Copy).then_inc(w_hi, 1)

            def x_split(n):
                for k in range(KT):
                    e.wait_ge(xn_ready, n * KT + k + 1)
                    e.activation(xh[:, k, :], xn[:, k, :], ACT.Copy).then_inc(xh_ready, 1)

            squares(0)
            w_split(wh[0], wr[0], w_a[0], 16)
            root(0)
            x_split(0)
            w_split(wh[1], wr[1], w_a[1], 16)
            for c in range(2 * HP):
                e.wait_ge(qk_tile, c + 1)
                e.activation(lin(qk[:, c, :]), pair(c % 4), ACT.Copy).then_inc(qk_out, 1)
                if c < 6:
                    w_split(wh[c % 2], wr[(c + 2) % 4], w_a[(c + 2) % 4], 16 * ((c + 2) // 4 + 1))
                else:
                    w_split(wvh[0][:, c - 6], wr[c - 6], w_a[c - 6], 48)
            for s in range(2):
                w_split(wvh[1][:, s], wr[2 + s], w_a[2 + s], 48)
            for s in range(2):
                w_split(wh[s], wr[s], w_a[s], 64)

            def shift_in(it, s):
                u = ub[s % 2]
                e.wait_ge(rw_tile, it * 4 + (s + 1))
                if s >= 2 or not (isinstance(it, int) and it == 0):
                    e.wait_ge(xm_done, it * 4 + (s - 1))
                    e.wait_ge(tsh_done, it * 4 + (s - 1))
                e.activation(u[:, 1:513].rearrange("p (h n) -> p h n", h=2), ps[:, 2 * s:2 * s + 2, 0:256], ACT.Copy)
                e.activation(u[:, 513:585].rearrange("p (b n) -> p b n", b=DB)[:, :, 1:9],
                             ps[:, 2 * s + 1, 256:320].rearrange("p (b n) -> p b n", b=DB), ACT.Copy).then_inc(u_ready, 1)
                if not (isinstance(it, int) and it == 3):
                    n = (s + 2) % 4
                    w_split(wh[s % 2], wr[n], w_a[n], it * 16 + (64 if s < 2 else 80))

            e.wait_ge(init_done, 1)
            for s in range(4):
                shift_in(0, s)
            with e.Fori(1, 3) as it:
                for s in range(4):
                    shift_in(it, s)
            for s in range(2):
                shift_in(3, s)

            units = [(h, qt) for h in range(8) for qt in range(4)]
            n = len(units)
            for u in range(n + 1):
                if u < n:
                    w = P * (units[u][1] + 1)
                    e.wait_ge(at_mx, u + 1)
                    if u >= 2:
                        e.wait_ge(at_tp, u - 1)
                    e.activation(pr[u % 2][:, 0:w], ps[:, u % 4, 0:w], ACT.Exp, bias=nmx[:, u % 8:u % 8 + 1], scale=SCALE,
                                 accum_out=rsm[:, u % 8:u % 8 + 1]).then_inc(at_ex, 1)
                if u >= 1:
                    v = u - 1
                    w = P * (units[v][1] + 1)
                    e.wait_ge(at_tp, v + 1)
                    if v >= 2:
                        e.wait_ge(at_pv, v - 1)
                    e.activation(prT[v % 2][:, :, :].rearrange("p a b -> p (a b)")[:, 0:w], ps[:, 4 + v % 2, 0:w],
                                 ACT.Copy).then_inc(at_tc, 1)

            for hp in range(HP):
                e.wait_ge(pr_mx, hp + 1)
                e.activation(tmp[4 + hp], tmp[4 + hp], ACT.Sqrt).then_inc(pr_rt, 1)
            e.wait_ge(xm_done, NPB)
            e.activation(wad[0:64, :], wad[0:64, :], ACT.Tanh).then_inc(pr_lin, 1)
            e.activation(gd, gd, ACT.Sigmoid)
            for hp in range(HP):
                for w, (dst, name) in enumerate(((AL, "w0"), (BE, "a0"))):
                    e.wait_ge(pr_w, 2 * hp + w + 1)
                    e.activation(lin(dst[:, hp, :]), pair(2 * (hp % 2) + w), ACT.Sigmoid, bias=pcol(name, hp)).then_inc(pr_sig, 1)
            for hp in range(HP):
                e.wait_ge(pr_exc, hp + 1)
                e.activation(tmp[3], tmp[1], ACT.Exp)
                e.activation(tmp[4], tmp[1], ACT.Exp, scale=-1.0)
                e.activation(tmp[2], tmp[2], ACT.Exp).then_inc(pr_exp, 1)

            e.wait_ge(ws_stored, 16)
            with e.Fori(0, DB) as b:
                for g in range(NGRP):
                    e.wait_ge(kv_used, b * (2 * NGRP) + (g + 1))
                    for j in range(2):
                        blk = 2 * g + j
                        e.activation(lg[:, blk * BLK:(blk + 1) * BLK], ps[:, 4 + g % 2, j * BLK:(j + 1) * BLK], ACT.Identity,
                                     accum_out=gs[:, blk:blk + 1]).then_inc(sa_ev, 1)
                e.wait_ge(sa_bi, b + 1)
                for g in range(NGRP + 2):
                    if g < NGRP:
                        for k in (2 * g, 2 * g + 1):
                            i = e.activation(lg[:, k * BLK:(k + 1) * BLK], lg[:, k * BLK:(k + 1) * BLK], ACT.Exp,
                                             bias=bi[:, k:k + 1], scale=SCALE, accum_out=psm[:, k:k + 1])
                        i.then_inc(sa_ex, 1)
                    elif g == NGRP:
                        e.activation(lg[:, PAST:PAST + NS], lg[:, PAST:PAST + NS], ACT.Exp, bias=bi[:, NBLK:NBLK + 1],
                                     scale=SCALE, accum_out=psm[:, NBLK:NBLK + 1]).then_inc(sa_ex, 1)
                    if g >= 1:
                        v = g - 1
                        e.wait_ge(sa_tp, b * (NGRP + 1) + (v + 1))
                        if v >= 2:
                            e.wait_ge(kv_used, b * (2 * NGRP) + (NGRP + v - 1))
                        if v < NGRP:
                            e.activation(pT[v % 2][:, :, :].rearrange("p a b -> p (a b)"), ps[:, 4 + v % 2, :], ACT.Copy).then_inc(sa_tc, 1)
                        else:
                            e.activation(pT[v % 2][0:NS, 0, :], ps[0:NS, 4 + v % 2, 0:P], ACT.Copy).then_inc(sa_tc, 1)

            e.wait_ge(st_stored, 16)
            x_split(1)
            w_split(wh[0], wr[0], w_g[0], 16)
            for hp in range(HP):
                e.wait_ge(gn_v, hp + 1)
                e.activation(tmp[2], tmp[2], ACT.Sqrt).then_inc(gn_rt, 1)
            w_split(wh[1], wr[1], w_g[1], 16)

            for s in range(2):
                e.sem_inc(ga_free[s], 1)

            def gates(c, last=False):
                e.wait_ge(m_done, c + 1)
                for s, g in ((0, g0), (1, g1)):
                    e.wait_ge(ga_mm, c * 4 + (s + 1))
                    e.activation(lin(g), pair(s), ACT.Sigmoid).then_inc(ga_free[s], 1)
                    if s == 0:
                        w_split(wh[2], wr[2], w_g[2], c * 16 + 16)
                    elif not last:
                        w_split(wh[0], wr[0], w_g[0], c * 16 + 32)
                        w_split(wh[1], wr[1], w_g[1], c * 16 + 32)

            with e.Fori(0, NG - 1) as c:
                gates(c)
            gates(NG - 1, last=True)
            for i in range(KT):
                if i == 2:
                    e.wait_ge(ga_mm, 4 * NG)
                elif i >= 3:
                    e.wait_ge(o_mm, i - 2)
                w_split(wh[i % 3], wr[(i + 3) % 4], w_ob[(i + 3) % 4], 16 * (i // 4 + 1))

            e.wait_ge(h_done, KT)
            squares(1)
            w_split(wuh[0], wr[0], w_u[0], 16)
            root(1)
            x_split(2)
            w_split(wuh[1], wr[1], w_u[1], 16)

            def up(it, last=False):
                later = last or not isinstance(it, int)
                for s in range(4):
                    col = it * 2 + (s // 2 + NF * (s % 2))
                    e.wait_ge(up_mm, it * 4 + (s + 1))
                    if later:
                        e.wait_ge(up_cp, it * 4 + (s - 3))
                        e.wait_ge(up_h, it * 2 + (s // 2 - 1))
                    e.activation(cu[s][:, 2:514].rearrange("p (h n) -> p h n", h=2), ps[:, 2 * s:2 * s + 2, 0:256], ACT.Copy)
                    e.activation(cu[s][:, 514:594].rearrange("p (b n) -> p b n", b=DB)[:, :, 2:10],
                                 ps[:, 2 * s + 1, 256:320].rearrange("p (b n) -> p b n", b=DB), ACT.Copy).then_inc(up_ev, 1)
                    if s < 2 or not last:
                        n = (s + 2) % 4
                        w_split(wuh[s % 2], wr[n], w_u[n], it * 16 + (16 if s < 2 else 32))
                    e.wait_ge(up_ev, it * 4 + (s + 1))
                    e.wait_ge(up_st, it * 4 + (s + 1))
                    e.activation(cc[s], cu[s][:, 2:594], ACT.Identity, bias=pcol("cb", col), scale=pcol("cw2", col)).then_inc(up_c0, 1)
                for s in (1, 3):
                    e.wait_ge(up_cv, it * 4 + (s + 1))
                    e.activation(cc[s], cc[s], ACT.Silu).then_inc(up_si, 1)

            up(0)
            with e.Fori(1, NF // 2 - 1) as it:
                up(it)
            up(NF // 2 - 1, last=True)
            for s in range(2):
                w_split(wdh[s], wd[s], w_d[s], 16)
                for k in range(KH * s, KH * (s + 1)):
                    e.wait_ge(up_h, k + 1)
                    e.activation(hhh[:, k, :], hh[:, k, :], ACT.Copy).then_inc(hh_hi, 1)
            for s in range(2, 4):
                w_split(wdh[s], wd[s], w_d[s], 16)
            with e.Fori(1, KT // 2) as it:
                for s in range(4):
                    w_split(wdh[s], wd[s], w_d[s], it * 16 + 16)
            e.wait_ge(y_done, KT)
            squares(2)
            root(2)

        @block.gpsimd
        def _(e):
            def w_split(n, lo, raw, hi):
                e.wait_ge(w_hi, n + 1)
                e.tensor_tensor(lo[:, :, :], raw, hi[:, :, :], ALU.subtract).then_inc(w_lo, 1)

            def x_split(n):
                for k in range(1, KT, 2):
                    e.wait_ge(xh_ready, n * KT + k + 1)
                    e.tensor_tensor(xl[:, k, :], xn[:, k, :], xh[:, k, :], ALU.subtract).then_inc(xs_odd, 1)

            w_split(0, wl[0], wr[0], wh[0])
            x_split(0)
            for n in range(1, 14):
                if 8 <= n < 12:
                    w_split(n, wvl[(n - 8) // 2][:, n % 2], wr[n % 4], wvh[(n - 8) // 2][:, n % 2])
                else:
                    w_split(n, wl[n % 4], wr[n % 4], wh[n % 2])
            e.wait_ge(qk_out, 2 * HP)
            e.tensor_copy(qks[:, :, :], qk[:, :, SEQ:T]).then_inc(qks_done, 1)

            def last_rows(g, s):
                e.wait_ge(u_ready, g + 1)
                dst = tsh[:, g:g + 1, :] if isinstance(g, int) else tsh[:, bass.ds(g, 1), :]
                e.tensor_copy(dst, ub[s % 2][:, 512:593].rearrange("p (o b n) -> p o b n", o=1, n=9)[:, :, :, 0]).then_inc(tsh_done, 1)

            with e.Fori(0, 3) as it:
                for s in range(4):
                    last_rows(it * 4 + s, s)
                    n = (s + 2) % 4
                    w_split(it * 4 + (14 + s), wl[n], wr[n], wh[s % 2])
            for s in range(2):
                last_rows(12 + s, s)

            def stage(n, cols):
                if not (isinstance(n, int) and n == 0):
                    e.wait_ge(ch_s, n)
                e.tensor_copy(stg[:, :, :], rw[:, :, cols]).then_inc(ch_stg, 1)
                e.wait_ge(ch_ev, n * 5 + 1)
                for l in range(LEVELS - 1):
                    i = e.tensor_tensor(amt[:, l, :, :], aa[:, 1, :, :], mone("lvl", 128 * (l + 1) + 64), ALU.mult)
                i.then_inc(ch_amt, 1)

            e.wait_ge(pr_done, 1)
            stage(0, slice(SEQ, T))
            with e.Fori(0, DB) as b:
                e.wait_ge(sa_lg, b + 1)
                e.tensor_copy(qbd[0:64, :, 0:8], qks[0:64, 0:HP, bass.ds(b * DT, DT)]).then_inc(sa_q, 1)
                e.wait_ge(sa_q, b * 2 + 1)
                e.tensor_copy(qbd[64:128, :, 8:16], qks[64:128, 0:HP, bass.ds(b * DT, DT)]).then_inc(sa_q, 1)
                e.wait_ge(sa_q, b * 2 + 2)
                stage(b + 1, bass.ds(b * C, C))

            x_split(1)
            with e.Fori(0, NG) as c:
                for s in range(3):
                    w_split(c * 3 + (W_GATE + s), wl[s], wr[s], wh[s])
            for i in range(KT):
                w_split(W_OUT + i, wl[(i + 3) % 4], wr[(i + 3) % 4], wh[i % 3])
            e.wait_ge(o_mm, KT)
            for s in range(4):
                i = e.memset(cu[s][:, 0:2], 0.0)
            i.then_inc(up_z, 1)
            w_split(W_UP, wl[0], wr[0], wuh[0])
            x_split(2)
            w_split(W_UP + 1, wl[1], wr[1], wuh[1])
            e.wait_ge(s_sc, 16)

            def conv_rows(it, last=False):
                for s in range(4):
                    col = it * 2 + (s // 2 + NF * (s % 2))
                    at_ = bass.ds(col, 1)
                    if isinstance(it, int):
                        at_ = slice(col, col + 1)
                    if last or not isinstance(it, int):
                        e.wait_ge(up_cv, it * 4 + (s - 3))
                    e.tensor_copy(cu[s][:, 514:594].rearrange("p (b n) -> p b n", b=DB)[:, :, 0:2],
                                  scv[:, at_, :].rearrange("p o (b n) -> p (o b) n", b=DB)).then_inc(up_st, 1)
                    e.wait_ge(up_ev, it * 4 + (s + 1))
                    e.tensor_copy(cvo[:, at_, :].rearrange("p o (b n) -> p (o b) n", b=9),
                                  cu[s][:, 512:602].rearrange("p (b n) -> p b n", b=9)[:, :, 0:2]).then_inc(up_cp, 1)
                    if s < 2 or not last:
                        n = (s + 2) % 4
                        w_split(it * 4 + (W_UP + s + 2), wl[n], wr[n], wuh[s % 2])

            conv_rows(0)
            with e.Fori(1, NF // 2 - 1) as it:
                conv_rows(it)
            conv_rows(NF // 2 - 1, last=True)
            with e.Fori(0, KT // 2) as it:
                for s in range(4):
                    w_split(it * 4 + (W_DOWN + s), wdl[s], wd[s], wdh[s])

        @block.vector
        def _(e):
            def rstd(n):
                own_ = Line(e, own["norm"], 2 * n)
                e.wait_ge(sq_used, (n + 1) * KT)
                own_.did(e.tensor_scalar(lin(rs), pair(0), 1.0 / D, EPS, ALU.mult, ALU.add))
                own_.settle()
                e.sem_inc(ms_ready, 1)
                e.wait_ge(rt_ready, n + 1)
                own_.did(e.reciprocal(rs, rs))
                own_.settle()

            def normed(gain, n=None):
                for k in range(KT + 2):
                    if k < KT:
                        e.scalar_tensor_tensor(out=xn[:, k, :], in0=x[:, k, :], scalar=pcol(gain, k), in1=rs,
                                               op0=ALU.mult, op1=ALU.mult).then_inc(xn_ready, 1)
                    if n is not None and k >= 2 and k % 2 == 0:
                        e.wait_ge(xh_ready, n * KT + k - 1)
                        e.tensor_tensor(xl[:, k - 2, :], xn[:, k - 2, :], xh[:, k - 2, :], ALU.subtract).then_inc(xs_even, 1)

            ln = Line(e, own["setup"])
            for u in ub:
                ln.did(e.memset(u[:, :], 0.0))
            ln.did(e.memset(qbd[:, :, :], 0.0))
            ln.did(e.memset(mb[:, :], 0.0))
            ln.settle()
            e.sem_inc(init_done, 1)
            e.wait_ge(s_pv, 16)
            rstd(0)
            normed("ln1", 0)
            e.tensor_scalar(omka, pv[:, PV["ka"]:PV["ka"] + HP], -1.0, 1.0, ALU.mult, ALU.add)
            for j in range(2):
                cols = slice(256 * j, 256 * j + 256)
                for t4 in range(5):
                    e.wait_ge(v_tile, 5 * j + t4 + 1)
                    if t4 < 4:
                        e.tensor_copy(vp[:, t4, cols], ps[:, t4, cols]).then_inc(v_evac, 1)
                    else:
                        e.tensor_copy(vsm[0:NS, cols], ps[P - NS:P, t4, cols]).then_inc(v_evac, 1)

            SH = 2
            e.wait_ge(s_c1, 32)

            def shift(g, s, base, dst):
                ln = Line(e, own["shift"], base)
                u = ub[s % 2]
                e.wait_ge(u_ready, g + 1)
                src = shs[:, g, :] if isinstance(g, int) else shs[:, bass.ds(g, 1), :].rearrange("p o b -> p (o b)")
                ln.did(e.tensor_scalar(u[:, 513:585].rearrange("p (b n) -> p b n", b=DB)[:, :, 0], src, 1.0, None, ALU.mult))
                ln.settle()
                ln.did(e.tensor_tensor(df[:, 0:584], u[:, 0:584], u[:, 1:585], ALU.subtract))
                ln.settle()
                mu = pcol("mu", g)
                e.scalar_tensor_tensor(out=dst[:, 0:SEQ], in0=df[:, 0:SEQ], scalar=mu, in1=u[:, 1:513],
                                       op0=ALU.mult, op1=ALU.add)
                e.scalar_tensor_tensor(out=dst[:, SEQ:T].rearrange("p (b n) -> p b n", b=DB),
                                       in0=df[:, 513:585].rearrange("p (b n) -> p b n", b=DB)[:, :, 0:8], scalar=mu,
                                       in1=u[:, 514:586].rearrange("p (b n) -> p b n", b=DB)[:, :, 0:8],
                                       op0=ALU.mult, op1=ALU.add).then_inc(xm_done, 1)
                assert ln.n == SH

            with e.Fori(0, 3) as it:
                for s in range(4):
                    shift(it * 4 + s, s, it * (4 * SH) + SH * s, rw[:, bass.ds(it * 4 + s, 1), :].rearrange("p o n -> p (o n)"))
            for s, dst in enumerate((wad, gd)):
                shift(12 + s, s, SH * (12 + s), dst)

            ln = Line(e, own["attn"])
            units = [(h, qt) for h in range(8) for qt in range(4)]
            n = len(units)
            for u in range(n + 2):
                if u < n:
                    qt = units[u][1]
                    w, j = P * (qt + 1), u % 8
                    e.wait_ge(at_lg, u + 1)
                    diag = ps[:, u % 4, w - P:w]
                    ln.did(e.tensor_tensor(diag, diag, causal, ALU.add))
                    ln.settle()
                    ln.did(e.tensor_reduce(mx[:, j:j + 1], ps[:, u % 4, 0:w], AX.X, ALU.max))
                    ln.settle()
                    e.tensor_scalar(nmx[:, j:j + 1], mx[:, j:j + 1], -SCALE, None, ALU.mult).then_inc(at_mx, 1)
                if 1 <= u <= n:
                    v = u - 1
                    w, j = P * (units[v][1] + 1), v % 8
                    e.wait_ge(at_ex, v + 1)
                    ln.did(e.reciprocal(rin[:, j:j + 1], rsm[:, j:j + 1]))
                    ln.settle()
                    e.tensor_scalar(pr[v % 2][:, 0:w], pr[v % 2][:, 0:w], rin[:, j:j + 1], None, ALU.mult).then_inc(at_pn, 1)
                if u >= 9 and (u - 9) % 8 == 0:
                    hp = (u - 9) // 8
                    e.wait_ge(at_pv, 8 * hp + 8)
                    e.tensor_copy(oa[:, hp, 0:SEQ], ps[:, 6 + hp % 2, :]).then_inc(at_oe, 1)

            ln = Line(e, own["prep"])
            e.wait_ge(qks_done, 1)
            e.wait_ge(tsh_done, NPB)
            e.wait_ge(k_stored, 16)
            for hp in range(HP):
                ln.did(e.tensor_scalar(yb[:, hp, :], K[:, hp, :], pcol("kk", hp), None, ALU.mult))
                ln.settle()
                e.tensor_tensor(tmp[hp], yb[:, hp, :], yb[:, hp, :], ALU.mult).then_inc(pr_sq, 1)
            for hp in range(HP):
                e.wait_ge(pr_ss, hp + 1)
                e.tensor_scalar(lin(tmp[4 + hp]), pair(hp), 1e-24, None, ALU.max).then_inc(pr_mx, 1)
            for hp in range(HP):
                e.wait_ge(pr_rt, hp + 1)
                ln.did(e.reciprocal(tmp[4 + hp], tmp[4 + hp]))
                ln.settle()
                ln.did(e.tensor_tensor(yb[:, hp, :], yb[:, hp, :], tmp[4 + hp], ALU.mult))
            ln.settle()
            for hp in range(HP):
                r_, k_, v_, al, be, kk = (a[:, hp, :] for a in (R, K, V, AL, BE, yb))
                e.wait_ge(pr_sig, 2 * hp + 2)
                ln.did(e.tensor_scalar(tmp[0], al, -EM05, None, ALU.mult))
                ln.settle()
                ln.did(e.tensor_tensor_scan(tmp[1], reset, tmp[0], 0.0, ALU.mult, ALU.add))
                ln.settle()
                e.tensor_tensor(tmp[2], tmp[1], tmp[0], ALU.subtract).then_inc(pr_exc, 1)
                ln.did(e.tensor_scalar(tmp[5], be, pcol("ka", hp), omka[:, hp:hp + 1], ALU.mult, ALU.add))
                ln.settle()
                ln.did(e.tensor_tensor(k_, k_, tmp[5], ALU.mult))
                ln.settle()
                e.scalar_tensor_tensor(out=tmp[5], in0=r_, scalar=pcol("rk", hp), in1=k_, op0=ALU.mult, op1=ALU.mult).then_inc(pr_b, 1)
                ln.did(e.tensor_tensor(be, be, kk, ALU.mult))
                ln.settle()
                e.wait_ge(pr_exp, hp + 1)
                ln.did(e.scalar_tensor_tensor(out=al, in0=kk, scalar=-1.0, in1=tmp[2], op0=ALU.mult, op1=ALU.mult))
                ln.did(e.tensor_tensor(be, be, tmp[4], ALU.mult))
                e.wait_ge(pr_b, hp + 1)
                ln.did(e.tensor_tensor(k_, k_, tmp[4], ALU.mult))
                ln.did(e.tensor_tensor(r_, r_, tmp[3], ALU.mult))
                ln.did(e.tensor_copy(lc[:, hp, 0:8], tmp[3][:, 0:SEQ].rearrange("p (c n) -> p c n", n=C)[:, :, C - 1]))
                ln.did(e.tensor_copy(lc[:, hp, 8:16], tmp[3][:, SEQ:T].rearrange("p (c n) -> p c n", n=DT)[:, :, DT - 1]))
                ln.settle()
                e.wait_ge(pr_bp, hp + 1)
                ln.did(e.tensor_tensor(lin(kk), lin(v_), pair(0), ALU.mult))
                ln.settle()
            ln.did(e.memset(st[:, :, :], 0.0))
            ln.settle()
            e.sem_inc(st_ready, 1)
            e.sem_inc(pr_done, 1)

            def gram_out(n, bank, base, own_sem, masks):
                e.wait_ge(ch_g, n * 4 + (bank + 1))
                if bank == 0:
                    ln = Line(e, own_sem, base)
                    e.tensor_tensor(aa[:, :, :, :], q8(0), mpair(masks[0]), ALU.mult).then_inc(ch_ev, 1)
                    e.wait_ge(ch_ev, n * 5 + 1)
                    ln.did(e.tensor_tensor(tt[:, :, :, :], aa[:, :, :, :], mpair("lvl"), ALU.mult))
                    ln.settle()
                    e.tensor_tensor(tt[:, :, :, :], tt[:, :, :, :], mpair("eye2"), ALU.add).then_inc(ch_te, 1)
                elif bank == 1:
                    e.tensor_tensor(mm1[:, :, :, :], q8(1), mpair(masks[1]), ALU.mult).then_inc(ch_ev, 1)
                elif bank == 2:
                    e.tensor_tensor(mkv[:, 0, :, :], q4(2, 0), mone(masks[1], 64), ALU.mult).then_inc(ch_ev, 1)
                    e.tensor_copy(mkv[:, 1, :, :], q4(2, 1)).then_inc(ch_ev, 1)
                else:
                    e.tensor_copy(bk[:, :, :, :], q8(3)).then_inc(ch_ev, 1)

            def x_out(n, l):
                e.wait_ge(ch_x, n * (LEVELS - 1) + (l + 1))
                e.tensor_copy(xx[:, :, :], q4(0)).then_inc(ch_xe, 1)

            def d_out(n, l):
                e.wait_ge(ch_d, n * (LEVELS - 1) + (l + 1))
                e.tensor_tensor(tt[:, :, :, :], tt[:, :, :, :], q8(1), ALU.add).then_inc(ch_te, 1)

            for bank in range(4):
                gram_out(0, bank, 0, own["ch0"], ("ms0", "ms1"))
            for l in range(LEVELS - 1):
                x_out(0, l)
                d_out(0, l)
            ln = Line(e, own["chunk0"])
            e.wait_ge(s_s0, 16)
            for hp in range(HP):
                if hp:
                    e.wait_ge(ss_y, hp)
                for a, src in ((0, sA), (1, sR)):
                    i = e.tensor_tensor(ex[a], src[:, hp:hp + 1, :].to_broadcast([P, DB, C]), colm, ALU.mult)
                i.then_inc(ss_ex, 1)
                e.wait_ge(ss_w, hp + 1)
                e.tensor_copy(ww[:, hp, :], ps[:, 2, hp * C:(hp + 1) * C]).then_inc(ss_we, 1)
                e.wait_ge(ss_u, hp + 1)
                e.tensor_copy(uu[:, hp, :], ps[:, 3, hp * C:(hp + 1) * C]).then_inc(ss_ue, 1)
                e.wait_ge(ss_ue, hp + 1)
                if hp:
                    e.wait_ge(ss_s, hp)
                for a, src in ((2, uu[:, hp:hp + 1, :]), (3, mkv[:, 1, hp:hp + 1, :])):
                    i = e.tensor_tensor(ex[a], src.to_broadcast([P, DB, C]),
                                        rowm.rearrange("p (b o) -> p b o", o=1).to_broadcast([P, DB, C]), ALU.mult)
                i.then_inc(ss_ex, 1)
                e.wait_ge(ss_y, hp + 1)
                ln.did(e.tensor_copy(R[:, hp, SEQ:T], ps[:, 4, hp * C:(hp + 1) * C]))
                e.wait_ge(ss_s if hp < HP - 1 else ch_s, hp + 1 if hp < HP - 1 else 1)
                ln.did(e.tensor_tensor(s0[:, hp, :, :], s0[:, hp, :, :], ps[:, 6, :].rearrange("p (b n) -> p b n", b=DB), ALU.add))
                ln.settle()
                e.tensor_tensor(s0[:, hp, :, :], s0[:, hp, :, :],
                                lc[:, hp, 8:16].rearrange("p (b o) -> p b o", o=1).to_broadcast([P, DB, C]), ALU.mult).then_inc(ss_st, 1)

            e.sem_inc(sa_oo, 1)
            e.wait_ge(ws_stored, 16)
            DL = 15
            with e.Fori(0, DB) as b:
                ln = Line(e, own["loop"], b * DL)
                for g in range(NGRP):
                    if g < 2:
                        gram_out(b + 1, 2 * g, b * 1, own["chl"], ("mp0", "mp1"))
                        gram_out(b + 1, 2 * g + 1, b * 1, own["chl"], ("mp0", "mp1"))
                    elif g % 2 == 0:
                        x_out(b + 1, g // 2 - 1)
                    else:
                        d_out(b + 1, g // 2 - 1)
                    e.wait_ge(sa_ev, b * (2 * NGRP) + (2 * g + 2))
                    i = e.tensor_reduce(bm[:, 2 * g:2 * g + 2], lg[:, 512 * g:512 * g + 512].rearrange("p (a n) -> p a n", a=2), AX.X, ALU.max)
                ln.did(i)
                e.wait_ge(sa_lg, b + 2)
                ln.did(e.tensor_tensor(lg[:, PAST:PAST + NS], ps[:, 4, 0:NS], cst[:, bass.ds(b * 64 + CV["newm"], 64)], ALU.add))
                gi = gs.rearrange("p (o n) -> p o n", o=1).to_broadcast([P, NBLK, NBLK])
                gj = gs.rearrange("p (n o) -> p n o", o=1).to_broadcast([P, NBLK, NBLK])
                ln.did(e.tensor_tensor(cmp1, gi, gj, ALU.is_gt))
                ln.did(e.tensor_tensor(cmp2, gi, gj, ALU.is_equal))
                ln.settle()
                ln.did(e.tensor_reduce(bm[:, NBLK:NBLK + 1], lg[:, PAST:PAST + NS], AX.X, ALU.max))
                ln.did(e.tensor_tensor(cmp2, cmp2, tri, ALU.mult))
                ln.settle()
                ln.did(e.tensor_tensor(cmp1, cmp1, cmp2, ALU.add))
                ln.settle()
                ln.did(e.tensor_reduce(mb[:, 0:NBLK], cmp1, AX.X, ALU.add))
                ln.settle()
                ln.did(e.tensor_scalar(mb[:, 0:NBLK], mb[:, 0:NBLK], TOPK - 0.5, NEG, ALU.is_ge, ALU.mult))
                ln.settle()
                ln.did(e.tensor_tensor(bm, bm, mb, ALU.add))
                ln.settle()
                ln.did(e.tensor_reduce(sc[:, 0:1], bm, AX.X, ALU.max))
                ln.settle()
                ln.did(e.tensor_scalar(sc[:, 1:2], sc[:, 0:1], -SCALE, None, ALU.mult))
                ln.settle()
                e.tensor_scalar(bi, mb, sc[:, 1:2], None, ALU.add).then_inc(sa_bi, 1)
                for l in range(3, LEVELS - 1):
                    x_out(b + 1, l)
                    d_out(b + 1, l)
                e.wait_ge(ch_w, b + 1)
                e.tensor_copy(ww[:, :, :], q4(2)).then_inc(ch_we, 1)
                e.wait_ge(ch_u, b + 1)
                e.tensor_copy(uu[:, :, :], q4(3)).then_inc(ch_ue, 1)
                e.wait_ge(ch_y, b + 1)
                e.tensor_copy(R[:, :, bass.ds(b * C, C)], q4(2)).then_inc(ch_ye, 1)
                e.wait_ge(ch_s, b + 2)
                ln.did(e.tensor_tensor(st[:, :, :], st[:, :, :], q4(0), ALU.add))
                ln.settle()
                e.tensor_tensor(st[:, :, :], st[:, :, :], lc[:, :, bass.ds(b, 1)].to_broadcast([P, HP, C]), ALU.mult).then_inc(st_ready, 1)
                e.wait_ge(sa_ex, b * (NGRP + 1) + (NGRP + 1))
                ln.did(e.tensor_reduce(sc[:, 2:3], psm, AX.X, ALU.add))
                ln.settle()
                ln.did(e.reciprocal(sc[:, 3:4], sc[:, 2:3]))
                ln.settle()
                e.wait_ge(sa_nw, b + 1)
                e.tensor_scalar(ob, ps[:, 7, 0:P], sc[:, 3:4], None, ALU.mult).then_inc(sa_ob, 1)
                e.wait_ge(sa_ot, b + 1)
                for half in range(2):
                    r = slice(64 * half, 64 * half + 64)
                    i = e.tensor_copy(oa[r, :, bass.ds(b * DT + SEQ, DT)],
                                      ps[r, 6, 0:P].rearrange("p (a n) -> p a n", a=HP)[:, :, 8 * half:8 * half + 8])
                i.then_inc(sa_oo, 1)
                assert ln.n == DL

            e.wait_ge(kv_used, 2 * DB * NGRP)
            normed("ln1", 1)
            ln = Line(e, own["gn"])
            for hp in range(HP):
                e.wait_ge(gn_mm, 2 * hp + 1)
                ln.did(e.scalar_tensor_tensor(out=lin(tmp[0]), in0=pair(0), scalar=-1.0 / HD, in1=lin(R[:, hp, :]),
                                              op0=ALU.mult, op1=ALU.add))
                ln.settle()
                e.tensor_tensor(tmp[1], tmp[0], tmp[0], ALU.mult).then_inc(gn_sq, 1)
                e.wait_ge(gn_mm, 2 * hp + 2)
                e.tensor_scalar(lin(tmp[2]), pair(1), 1.0 / HD, GN_EPS, ALU.mult, ALU.add).then_inc(gn_v, 1)
                e.wait_ge(gn_rt, hp + 1)
                ln.did(e.reciprocal(tmp[2], tmp[2]))
                ln.settle()
                ln.did(e.tensor_tensor(tmp[0], tmp[0], tmp[2], ALU.mult))
                ln.settle()
                ln.did(e.tensor_scalar(tmp[0], tmp[0], pcol("lg", hp), pcol("lb", hp), ALU.mult, ALU.add))
                ln.settle()
                ln.did(e.tensor_tensor(tmp[0], tmp[0], yb[:, hp, :], ALU.add))
                ln.settle()
                e.tensor_tensor(lin(yb[:, hp, :]), lin(tmp[0]), pair(2), ALU.mult).then_inc(gn_out, 1)
                e.wait_ge(gn_out, hp + 1)
                ln.did(e.tensor_copy(ybh[:, hp, :], yb[:, hp, :]))
                ln.settle()
                e.tensor_tensor(ybl[:, hp, :], yb[:, hp, :], ybh[:, hp, :], ALU.subtract).then_inc(yb_split, 1)
            ln.did(e.tensor_copy(oah[:, :, :], oa[:, :, :]))
            ln.settle()
            e.tensor_tensor(oal[:, :, :], oa[:, :, :], oah[:, :, :], ALU.subtract).then_inc(oa_split, 1)

            e.wait_ge(gn_out, HP)
            for s in (2, 3):
                e.sem_inc(ga_free[s], 1)
            e.sem_inc(m_done, 1)
            with e.Fori(0, NG) as c:
                for s, g in ((2, g0), (3, g1)):
                    e.wait_ge(ga_free[s - 2], c + 2)
                    e.wait_ge(ga_mm, c * 4 + (s + 1))
                    e.tensor_tensor(lin(g), lin(g), pair(s), ALU.mult).then_inc(ga_free[s], 1)
                e.wait_ge(ga_free[2], c + 2)
                e.wait_ge(ga_free[3], c + 2)
                ln = Line(e, own["merge"], c * 2)
                mc, mhc, mlc = (a[:, bass.ds(c, 1), :].rearrange("p o n -> p (o n)") for a in (m, mh, ml))
                ln.did(e.tensor_tensor(mc, g0, g1, ALU.add))
                ln.settle()
                ln.did(e.tensor_copy(mhc, mc))
                ln.settle()
                e.tensor_tensor(mlc, mc, mhc, ALU.subtract).then_inc(m_done, 1)
            for c in range(KT):
                e.wait_ge(o_mm, c + 1)
                e.tensor_tensor(lin(x[:, c, :]), lin(x[:, c, :]), pair(c % 4), ALU.add).then_inc(h_done, 1)
            rstd(1)
            normed("ln2", 2)
            e.wait_ge(up_z, 1)

            def up(it):
                for s in range(4):
                    col = it * 2 + (s // 2 + NF * (s % 2))
                    e.wait_ge(up_c0, it * 4 + (s + 1))
                    ln = Line(e, own["up"], it * 4 + s)
                    ln.did(e.scalar_tensor_tensor(out=cc[s], in0=cu[s][:, 1:593], scalar=pcol("cw1", col), in1=cc[s],
                                                  op0=ALU.mult, op1=ALU.add))
                    ln.settle()
                    e.scalar_tensor_tensor(out=cc[s], in0=cu[s][:, 0:592], scalar=pcol("cw0", col), in1=cc[s],
                                           op0=ALU.mult, op1=ALU.add).then_inc(up_cv, 1)
                for s in (1, 3):
                    e.wait_ge(up_si, it * 2 + (s // 2 + 1))
                    e.wait_ge(up_cv, it * 4 + (s + 1))
                    j = it * 2 + s // 2
                    at_ = slice(j, j + 1) if isinstance(j, int) else bass.ds(j, 1)
                    dst = hh[:, at_, :].rearrange("p o n -> p (o n)")
                    e.tensor_tensor(dst[:, 0:SEQ], cc[s][:, 0:SEQ], cc[s - 1][:, 0:SEQ], ALU.mult)
                    e.tensor_tensor(dst[:, SEQ:T].rearrange("p (b n) -> p b n", b=DB),
                                    cc[s][:, 512:592].rearrange("p (b n) -> p b n", b=DB)[:, :, 2:10],
                                    cc[s - 1][:, 512:592].rearrange("p (b n) -> p b n", b=DB)[:, :, 2:10], ALU.mult).then_inc(up_h, 1)

            up(0)
            with e.Fori(1, NF // 2) as it:
                up(it)
            for k in range(NF):
                e.wait_ge(hh_hi, k + 1)
                e.tensor_tensor(hhl[:, k, :], hh[:, k, :], hhh[:, k, :], ALU.subtract).then_inc(hh_lo, 1)
            with e.Fori(0, KT // 2) as it:
                for s in range(2):
                    c = bass.ds(it * 2 + s, 1)
                    e.wait_ge(dn_mm, it * 4 + (2 * s + 2))
                    e.tensor_tensor(lin3(x[:, c, :]), lin3(x[:, c, :]), pair(s), ALU.add).then_inc(y_done, 1)
            rstd(2)
            normed("lnf")


_ARGS = ["xin", "kcache", "vcache", "pages", "s0t", "sshift", "sconv", "pvec", "consts", "lora", "w_in", "w_br", "w_o", "w_up", "w_down"]
_OUTS = [("yT", (P, KT, T)), ("kT", (P, HP, T)), ("v", (P, 4, WA)), ("vs", (NS, WA)), ("wkvp", (P, HP * HD)),
         ("tsh", (P, NPB, 9)), ("conv", (P, 2 * NF, 18)), ("wkvs", (P, HP * DB * HD))]


def kernel(**inputs):
    import concourse.bacc as bacc
    from concourse.bass_utils import run_bass_kernel_spmd

    a = {k: np.asarray(v) for k, v in inputs.items()}

    def tiles(w, nk, cols=None):
        w = w if cols is None else w[:, cols[0]:cols[1]]
        return w.reshape(nk, P, -1, P).transpose(2, 1, 0, 3)

    def fm(v):
        return v.reshape(-1, P).T

    npool = a["cache_k"].shape[1]
    xt = np.concatenate([a["x_prompt"].reshape(SEQ, D), a["x_sample"].reshape(NS, D)])
    cw = a["conv_w"][0]
    d = {
        "xin": xt.T.reshape(KT, P, T).transpose(1, 0, 2),
        "kcache": a["cache_k"][0].transpose(0, 2, 3, 1).reshape(npool, HP, P, PAGE).transpose(0, 2, 1, 3).reshape(npool, P, WA),
        "vcache": a["cache_v"][0].reshape(npool, PAGE, WA),
        "pages": a["page_table"].reshape(1, -1),
        "s0t": a["state_wkv"][0].transpose(1, 3, 0, 2).reshape(HP, P, DB, HD).transpose(1, 0, 2, 3).reshape(P, -1),
        "sshift": a["state_tshift"][0].T.reshape(NPB, P, DB).transpose(1, 0, 2),
        "sconv": a["state_conv"][0].transpose(2, 0, 1).reshape(2 * NF, P, DB * 2).transpose(1, 0, 2),
        "pvec": np.concatenate([fm(a[n][0].reshape(-1)) for n in ("ln1_g", "mu", "w0", "a0", "k_k", "k_a", "r_k", "lnx_g", "lnx_b", "ln2_g")]
                               + [fm(a["lnf_g"]), fm(cw[0]), fm(cw[1]), fm(cw[2]), fm(a["conv_b"][0])], axis=1),
        "consts": constants(),
        "lora": np.concatenate([np.concatenate([a["w2"][0], a["a2"][0]]), a["g2"][0]], axis=1),
        "w_in": tiles(a["w_in"][0], KT),
        "w_br": np.concatenate([tiles(a["w_br_a"][0], HP), tiles(a["w_br_b"][0], HP)], axis=2),
        "w_o": tiles(a["w_o"][0], KT),
        "w_up": tiles(a["w_up"][0], KT),
        "w_down": tiles(a["w_down"][0], NF),
    }
    nc = bacc.Bacc("TRN2", target_bir_lowering=False, num_devices=1)
    arrays, args = {}, []
    for name in _ARGS:
        v = np.ascontiguousarray(d[name])
        arrays["in_" + name] = v
        args.append(nc.dram_tensor("in_" + name, v.shape, mybir.dt.from_np(v.dtype), kind="ExternalInput").ap())
    for name, shape in _OUTS:
        args.append(nc.dram_tensor("out_" + name, shape, F32, kind="ExternalOutput").ap())
    build(nc, *args)
    res = run_bass_kernel_spmd(nc, [arrays], core_ids=[0]).results[0]
    o = {name: np.asarray(res["out_" + name]) for name, _ in _OUTS}
    y = o["yT"].transpose(2, 1, 0).reshape(T, D)
    k = o["kT"].transpose(2, 1, 0).reshape(T, WA)
    v = o["v"].transpose(1, 0, 2).reshape(SEQ, WA)
    tsh = o["tsh"].transpose(2, 1, 0).reshape(9, NPB * P)
    conv = o["conv"].transpose(2, 1, 0).reshape(9, 2, 2 * DFF)
    wp = o["wkvp"].reshape(2, HD, HP, HD).transpose(2, 0, 3, 1).reshape(1, 1, 8, HD, HD)
    ws = o["wkvs"].reshape(2, HD, HP, DB, HD).transpose(3, 2, 0, 4, 1).reshape(1, DB, 8, HD, HD)
    c = np.ascontiguousarray
    return (c(y[:SEQ].reshape(1, SEQ, D)), c(y[SEQ:].reshape(DB, DT, D)),
            c(k[:SEQ].reshape(1, 1, SEQ, 8, HD)), c(v.reshape(1, 1, SEQ, 8, HD)), c(wp),
            c(tsh[0:1].reshape(1, 1, -1)), c(conv[0:1].reshape(1, 1, 2, -1)),
            c(k[SEQ:].reshape(1, DB, DT, 8, HD)), c(o["vs"].reshape(1, DB, DT, 8, HD)), c(ws),
            c(tsh[1:].reshape(1, DB, -1)), c(conv[1:].reshape(1, DB, 2, -1)))
```

```python
from contextlib import ExitStack

import numpy as np

import concourse.bass as bass
from concourse import mybir

F32 = mybir.dt.float32
F32R = mybir.dt.float32r
I32 = mybir.dt.int32
ALU = mybir.AluOpType
ACT = mybir.ActivationFunctionType
AX = mybir.AxisListType

P = 128
D = 1024
KT = D // P
SEQ = 512
DB, DT = 8, 8
NS = DB * DT
T = SEQ + NS
HALF = T // 2
HD = 64
HP = 4
WA = 512
NPB = 1792 // P
NG = D // P
DFF = 2816
NF = DFF // P
PAST = 4096
PAGE = 128
NPG = PAST // PAGE
GP = 4
NGRP = NPG // GP
BLK = 256
NBLK = PAST // BLK
TOPK = 3
C = 64
NCH = SEQ // C
SCALE = HD ** -0.5
NEG = -1e30
EPS = 1e-6
GN_EPS = 64e-5
EM05 = float(np.exp(-0.5))
LEVELS = 6
SAMPLE_LEVELS = 3
ARENA = 52864
ALIGN = 8
W_GATE = 26
W_OUT = W_GATE + 3 * NG
W_UP = W_OUT + KT
W_DOWN = W_UP + 2 * NF
KH = NF // 2

PV = {}
_at = 0
for _n, _w in (("ln1", 8), ("mu", 14), ("w0", 4), ("a0", 4), ("kk", 4), ("ka", 4), ("rk", 4), ("lg", 4),
               ("lb", 4), ("ln2", 8), ("lnf", 8), ("cw0", 44), ("cw1", 44), ("cw2", 44), ("cb", 44)):
    PV[_n] = _at
    _at += _w
NPV = _at

CV = {}
_at = 0
for _n, _w in (("ident", 128), ("ones", 128), ("bones", 128), ("causal", 128), ("eye2", 128),
               ("mp0", 128), ("mp1", 128), ("ms0", 128), ("ms1", 128), ("lvl", LEVELS * 128),
               ("colm", DB * 64), ("rowm", DB), ("newm", DB * 64), ("tri", 256), ("reset", T), ("geps", 8)):
    CV[_n] = _at
    _at += _w
NCV = _at


def constants():
    c = np.zeros((P, NCV), np.float32)
    p = np.arange(P)
    f = np.arange(P)
    s = (p % 64)[:, None]
    t = np.arange(64)[None, :]

    def put(name, a):
        a = np.asarray(a, np.float32).reshape(P, -1)
        c[:, CV[name]:CV[name] + a.shape[1]] = a

    put("ident", np.eye(P))
    put("ones", np.ones((P, P)))
    put("bones", (p[:, None] // 64) == (f[None, :] // 64))
    put("causal", np.where(f[None, :] <= p[:, None], 0.0, NEG))
    eye = s == t
    put("eye2", np.concatenate([eye, eye], 1))
    same = (s // DT) == (t // DT)
    put("mp0", np.concatenate([t < s, s < t], 1))
    put("mp1", np.concatenate([s < t, s <= t], 1))
    put("ms0", np.concatenate([(t < s) & same, (s < t) & same], 1))
    put("ms1", np.concatenate([(s < t) & same, (s <= t) & same], 1))
    lv = []
    for l in range(LEVELS):
        m = 1 << l
        low = (s // (2 * m) == t // (2 * m)) & ((s // m) % 2 == 1) & ((t // m) % 2 == 0)
        up = (s // (2 * m) == t // (2 * m)) & ((t // m) % 2 == 1) & ((s // m) % 2 == 0)
        lv.append(np.concatenate([low, up], 1))
    put("lvl", np.concatenate(lv, 1))
    b = np.arange(DB)
    put("colm", np.broadcast_to((np.arange(64)[None, :] // DT == b[:, None])[None], (P, DB, 64)))
    put("rowm", ((p % 64) // DT)[:, None] == b[None, :])
    tt = (p % DT)[:, None, None]
    key = np.arange(64)[None, None, :]
    ok = (key // DT == b[None, :, None]) & (key % DT <= tt)
    put("newm", np.where(ok, 0.0, NEG))
    i = np.arange(NBLK)
    put("tri", np.broadcast_to((i[None, :] < i[:, None])[None], (P, NBLK, NBLK)))
    start = np.ones(T)
    start[np.arange(0, SEQ, C)] = 0
    start[np.arange(SEQ, T, DT)] = 0
    put("geps", np.full((P, 8), GN_EPS))
    put("reset", np.broadcast_to(start[None], (P, T)))
    return c


class Line:

    def __init__(self, eng, sem, base=0):
        self.eng, self.sem, self.base, self.n = eng, sem, base, 0

    def did(self, ins):
        ins.then_inc(self.sem, 1)
        self.n += 1
        return ins

    def settle(self):
        self.eng.wait_ge(self.sem, self.base + self.n)


def build(nc, xin, kcache, vcache, pages, s0t, sshift, sconv, pvec, consts, lora, w_in, w_br, w_o, w_up, w_down,
          yT, kT_out, v_out, vs_out, wkvp, tsh_out, conv_out, wkvs):
    ctx = ExitStack()
    with ctx:
        with nc.sbuf_tensor("below_ptab", [P, ARENA], F32), nc.sbuf_tensor("ptab", [1, DB * NPG], I32) as ptab:
            pass
        placed = [0]

        def view(at, *shape, dtype=F32):
            placed[0] += 1
            n = int(np.prod(shape))
            assert at + n <= ARENA and at % ALIGN == 0
            with ExitStack() as scope:
                if at:
                    scope.enter_context(nc.sbuf_tensor(f"before{placed[0]}", [P, at], F32))
                v = scope.enter_context(nc.sbuf_tensor(f"buffer{placed[0]}_at{at}", [P, n], dtype))[:, :]
            if len(shape) == 2:
                return v.rearrange("p (a b) -> p a b", a=shape[0])
            if len(shape) == 3:
                return v.rearrange("p (a b c) -> p a b c", a=shape[0], b=shape[1])
            return v

        def split_view(at, *shape):
            return view(at, *shape, dtype=F32R)

        xh, xl = split_view(39296, KT, T), split_view(4608, KT, T)
        wl = [split_view(9216 + 1024 * i, KT, P) for i in range(4)]
        wh = [split_view(a, KT, P) for i, a in enumerate((34304, 35328, 37760))]
        wvh = [view(27392 + 2048 * i, 2, KT, P, dtype=F32R) for i in range(2)]
        wvl = [view(9216 + 2048 * i, 2, KT, P, dtype=F32R) for i in range(2)]
        oah, oal = split_view(20224, HP, T), split_view(13312, HP, T)
        ybh, ybl = split_view(22528, HP, T), split_view(15616, HP, T)
        mh, ml = split_view(29696, KT, T), split_view(25088, KT, T)
        wuh = [split_view(13312 + 1024 * i, KT, P) for i in range(2)]
        hhh, hhl = split_view(4608, NF, T), split_view(17280, NF, T)
        wdh = [split_view(37888 + 1408 * i, KH, P) for i in range(4)]
        wdl = [split_view(29952 + 1408 * i, KH, P) for i in range(4)]
        ps = ctx.enter_context(nc.psum_tensor("ps", [P, 8, 512], F32))

        def sem(name):
            return ctx.enter_context(nc.semaphore(name))

        def sems(name, n):
            return [sem(f"{name}{i}") for i in range(n)]

        x = view(0, KT, T)
        xn = view(4608, KT, T)
        wr = [view(9216 + 1024 * i, KT, P) for i in range(4)]
        kring = [view(4608 + 2048 * i, GP, HP, PAGE) for i in range(4)]
        vring = [view(4608 + 2048 * i, GP, WA) for i in range(4)]
        oa = view(13312, HP, T)
        yb = view(15616, HP, T)
        sqb = [view(17920 + T * i, T) for i in range(2)]
        ub = [view(15616 + 600 * i, 600) for i in range(2)]
        df = view(15616 + 1200, 600)
        qk = view(17920, 2 * HP, T)
        tmp = [view(17920 + T * i, T) for i in range(8)]
        s0 = view(17920, HP, DB, 64)
        ex = [view(17920 + 2048 + 512 * i, DB, 64) for i in range(4)]
        lg = view(17920, PAST + NS)
        vp = view(22528, HP, WA)
        vsm = view(22528 + 2048, WA)
        rw = view(25088, 20, T)
        R, K, V, AL, BE = (rw[:, 4 * i:4 * i + 4, :] for i in range(5))
        wad = view(36608, T)
        gd = view(36608 + T, T)
        stg = view(37760, 20, C)
        sR, sK, sV, sA, sB = (stg[:, 4 * i:4 * i + 4, :] for i in range(5))
        aa = view(39040, 2, HP, C)
        mm1 = view(39552, 2, HP, C)
        mkv = view(40064, 2, HP, C)
        bk = view(40576, 2, HP, C)
        tt = view(41088, 2, HP, C)
        amt = view(41600, LEVELS - 1, HP, C)
        xx = view(42880, HP, C)
        ww = view(43136, HP, C)
        uu = view(43392, HP, C)
        st = view(43648, HP, C)
        pr = [view(37760 + 512 * i, SEQ) for i in range(2)]
        prT = [view(37760 + 1024 + 512 * i, HP, P) for i in range(2)]
        at = [43904]

        def take(*shape):
            v = view(at[0], *shape)
            at[0] += -(-int(np.prod(shape)) // ALIGN) * ALIGN
            return v

        cst = take(NCV)
        pv = take(NPV)
        omka = take(HP)
        shs = take(NPB, DB)
        lo = take(2 * WA)
        w2a2, g2 = lo[:, 0:WA], lo[:, WA:2 * WA]
        qks = take(2 * HP, NS)
        tsh = take(NPB, 9)
        qbd = take(HP, 32)
        lc = take(HP, 16)
        gs = take(16)
        bm = take(17)
        mb = take(17)
        bi = take(17)
        psm = take(17)
        sc = take(8)
        cmp1 = take(16, 16)
        cmp2 = take(16, 16)
        mx = take(8)
        nmx = take(8)
        rsm = take(8)
        rin = take(8)
        pT = [take(GP, P) for _ in range(2)]
        ob = take(P)
        rs = take(T)
        assert at[0] <= ARENA, at[0]
        m = view(25088, KT, T)
        g0 = view(17920, T)
        g1 = view(17920 + T, T)
        hh = view(17280, NF, T)
        wd = [view(29952 + 1408 * i, KH, P) for i in range(4)]
        cu = [view(31360 + 608 * i, 608) for i in range(4)]
        cc = [view(33792 + 592 * i, 592) for i in range(4)]
        scv = view(36160, 2 * NF, DB * 2)
        cvo = view(36864, 2 * NF, 18)

        ident, ones, bones, causal = (cst[:, CV[n]:CV[n] + P] for n in ("ident", "ones", "bones", "causal"))
        geps = cst[:, CV["geps"]:CV["geps"] + 1]
        reset = cst[:, CV["reset"]:CV["reset"] + T]
        tri = cst[:, CV["tri"]:CV["tri"] + 256].rearrange("p (a b) -> p a b", a=16)
        colm = cst[:, CV["colm"]:CV["colm"] + 512].rearrange("p (a b) -> p a b", a=DB)
        rowm = cst[:, CV["rowm"]:CV["rowm"] + DB]

        def mpair(name, at=0):
            a = CV[name] + at
            return cst[:, a:a + 128].rearrange("p (a o b) -> p a o b", a=2, o=1).to_broadcast([P, 2, HP, C])

        def mone(name, at=0):
            a = CV[name] + at
            return cst[:, a:a + 64].rearrange("p (o b) -> p o b", o=1).to_broadcast([P, HP, C])

        def pcol(name, i):
            if isinstance(i, int):
                return pv[:, PV[name] + i:PV[name] + i + 1]
            return pv[:, bass.ds(i + PV[name], 1)]

        def tile_of(w, i):
            if isinstance(i, int):
                return w[i]
            return w[bass.ds(i, 1)].rearrange("o p k n -> p (o k) n")

        def pair(b):
            return ps[:, 2 * b:2 * b + 2, 0:HALF]

        def lin(a):
            return a.rearrange("p (h n) -> p h n", h=2)

        def lin3(a):
            return a.rearrange("p o (h n) -> p (o h) n", h=2)

        def q4(bank, j=0):
            return ps[:, bank, 256 * j:256 * j + 256].rearrange("p (a b) -> p a b", a=HP)

        def q8(bank):
            return ps[:, bank, :].rearrange("p (c a b) -> p c a b", c=2, a=HP)

        def products(c):
            return 0 if c is None else c * (LEVELS - 1) + (SAMPLE_LEVELS - 1)

        def versions(c):
            return 0 if c is None else c * LEVELS + SAMPLE_LEVELS

        def heads():
            for hp in range(HP):
                for half in range(2):
                    yield hp, slice(64 * half, 64 * half + 64)

        s_c0, s_c1, s_pv, s_pt, s_s0, s_sc = (sem(n) for n in (
            "ones_in", "const_in", "params_in", "pages_in", "states_in", "conv_in"))
        s_x = sems("x_in", 4)
        w_a, w_g, w_ob, w_u, w_d = sems("w_in", 4), sems("w_gate", 3), sems("w_o", 4), sems("w_up", 4), sems("w_down", 4)
        w_hi, w_lo, xh_ready, xs_even, xs_odd, hh_hi, hh_lo, yb_split, oa_split, st_stored = (sem(n) for n in (
            "w_hi", "w_lo", "xn_hi", "xn_lo_even", "xn_lo_odd", "hh_hi", "hh_lo", "yb_split", "oa_split", "state_stored"))
        kv_in = sems("kv_in", 4)
        sq_ready, sq_used, ms_ready, rt_ready, xn_ready = (sem(n) for n in ("sq_ready", "sq_used", "ms_ready", "rt_ready", "xn_ready"))
        qk_tile, qk_out, v_tile, v_evac, rw_tile, u_ready, xm_done, tsh_done, qks_done = (sem(n) for n in (
            "qk_tile", "qk_out", "v_tile", "v_evac", "rw_tile", "u_ready", "xm_done", "tsh_done", "qks_done"))
        own = {n: sem("own_" + n) for n in ("shift", "attn", "prep", "chunk0", "loop", "gn", "merge", "up", "norm", "chunk")}
        init_done = sem("init_done")
        at_lg, at_mx, at_ex, at_pn, at_tp, at_tc, at_pv, at_oe = (sem(n) for n in (
            "at_logits", "at_max", "at_exp", "at_norm", "at_transposed", "at_pt", "at_pv", "at_out"))
        pr_sq, pr_ss, pr_mx, pr_rt, pr_r, pr_lin, pr_w, pr_sig, pr_exc, pr_exp, pr_b, pr_bp, pr_done = (sem(n) for n in (
            "kk_sq", "kk_ss", "kk_ms", "kk_rt", "r_decayed", "lora_act", "lora_mm", "lora_sig", "excl", "decays", "bonus_in", "bonus_mm", "prep_done"))
        ch_stg, ch_g, ch_ev, ch_amt, ch_x, ch_xe, ch_d, ch_te, ch_w, ch_we, ch_u, ch_ue, ch_y, ch_ye, ch_s, st_ready = (sem(n) for n in (
            "c_staged", "c_gram", "c_gram_out", "c_levels", "c_x", "c_x_out", "c_d", "c_t", "c_w", "c_w_out", "c_u", "c_u_out",
            "c_y", "c_y_out", "c_s", "state_ready"))
        ss_ex, ss_w, ss_we, ss_u, ss_ue, ss_y, ss_s, ss_st = (sem(n) for n in (
            "ss_exp", "ss_w", "ss_w_out", "ss_u", "ss_u_out", "ss_y", "ss_s", "ss_state"))
        sa_q, kv_used, sa_ev, sa_lg, sa_bi, sa_ex, sa_tp, sa_tc, sa_nw, sa_ob, sa_ot, sa_oo = (sem(n) for n in (
            "s_q", "kv_used", "s_logits_out", "s_new_logits", "s_bias", "s_exp", "s_transposed", "s_pt", "s_pv_new",
            "s_o", "s_ot", "s_oa"))
        gn_mm, gn_dev, gn_sq, gn_rt, gn_nm, gn_aff, gn_out, yb_hi = (sem(n) for n in (
            "gn_mm", "gn_deviation", "gn_sq", "gn_rt", "gn_normed", "gn_affine", "gn_out", "yb_hi"))
        ga_mm, m_done = sem("gate_mm"), sem("m_done")
        ga_free = sems("gate_free", 4)
        o_mm, h_done = sem("o_mm"), sem("h_done")
        up_mm, up_ev, up_st, up_c0, up_cv, up_si, up_h, up_cp, up_z = (sem(n) for n in (
            "up_mm", "up_u", "up_state", "up_c0", "up_cv", "up_silu", "up_h", "up_conv_out", "up_zero"))
        dn_mm, y_done = sem("down_mm"), sem("y_done")
        stored = sem("stored")
        k_stored, ws_stored = sem("k_stored"), sem("wkvs_stored")
        waited = sem("waited")
        N_STORES = 6

        block = ctx.enter_context(nc.Block())

        @block.sync
        def _(e):
            e.dma_start(cst[:, 0:256], consts[:, 0:256]).then_inc(s_c0, 16)
            for i in range(4):
                e.dma_start(x[:, 2 * i:2 * i + 2, :], xin[:, 2 * i:2 * i + 2, :]).then_inc(s_x[i], 16)
            e.dma_start(pv[:, :], pvec).then_inc(s_pv, 16)
            for s in range(4):
                e.dma_start(wr[s], w_in[s]).then_inc(w_a[s], 16)
            e.dma_start(cst[:, 256:NCV], consts[:, 256:NCV]).then_inc(s_c1, 16)
            e.dma_start(shs[:, :, :], sshift).then_inc(s_c1, 16)
            e.dma_start(lo[:, :], lora).then_inc(s_c1, 16)
            e.dma_start(ptab[:, :], pages).then_inc(s_pt, 16)

            def w_tile(i, s, used, n):
                e.wait_ge(used, n)
                e.dma_start(wr[s], tile_of(w_in, i)).then_inc(w_a[s], 16)

            for s in range(4):
                w_tile(4 + s, s, qk_tile, s + 1)
            for s in range(4):
                w_tile(8 + s, s, qk_tile, 4 + s + 1)
            for s in range(4):
                w_tile(12 + s, s, v_tile, 5 * (s // 2 + 1))
            with e.Fori(0, 2) as it:
                for s in range(4):
                    w_tile(it * 4 + (16 + s), s, rw_tile, it * 4 + (s + 1))
            for s in range(2):
                w_tile(24 + s, s, rw_tile, 8 + s + 1)

            e.wait_ge(qk_out, 2 * HP)
            e.dma_start(kT_out, qk[:, HP:2 * HP, :]).then_inc(k_stored, 16)
            e.wait_ge(v_evac, 10)
            e.dma_start(v_out, vp[:, :, :]).then_inc(stored, 16)
            e.dma_start(vs_out, vsm[0:NS, :]).then_inc(stored, 16)
            e.wait_ge(tsh_done, NPB)
            e.dma_start(tsh_out, tsh[:, :, :]).then_inc(stored, 16)

            e.wait_ge(s_pt, 16)
            e.wait_ge(rw_tile, NPB)

            def page_group(b, g, value, n):
                _, pgs = nc.values_load_multi_w_load_instructions(
                    ptab[0:1, bass.ds(b * NPG + g * GP, GP)], engines=(mybir.EngineType.SP,), min_val=0, max_val=kcache.shape[0] - 1)
                if n is not None:
                    e.wait_ge(kv_used, n)
                for q, pg in enumerate(pgs):
                    slot = (vring if value else kring)[g % 4][:, q:q + 1]
                    slot = slot.rearrange("p o a -> p (o a)") if value else slot.rearrange("p o a b -> p (o a b)")
                    cache = vcache if value else kcache
                    e.dma_start(slot, cache[bass.ds(pg, 1)].rearrange("o p n -> p (o n)")).then_inc(kv_in[g % 4], 16)

            for g in range(4):
                page_group(0, g, False, None)
            e.wait_ge(pr_done, 1)
            e.dma_start(s0[:, :, :, :].rearrange("p a b c -> p (a b c)"), s0t).then_inc(s_s0, 16)
            e.wait_ge(ss_st, HP)
            e.dma_start(wkvs, s0[:, :, :, :].rearrange("p a b c -> p (a b c)")).then_inc(ws_stored, 16)
            for g in range(4, NGRP):
                page_group(0, g, False, g - 3)
            for g in range(NGRP):
                page_group(0, g, True, NGRP + g - 3)
            with e.Fori(1, DB) as b:
                for g in range(NGRP):
                    page_group(b, g, False, b * (2 * NGRP) + (g - 3))
                for g in range(NGRP):
                    page_group(b, g, True, b * (2 * NGRP) + (NGRP + g - 3))

            e.wait_ge(st_ready, NCH + 1)
            e.dma_start(wkvp, st[:, :, :].rearrange("p a b -> p (a b)")).then_inc(st_stored, 16)
            e.wait_ge(kv_used, 2 * DB * NGRP)
            for s in range(2):
                e.dma_start(wr[s], w_in[26 + 8 * s]).then_inc(w_g[s], 16)
            e.dma_start(wr[2], w_br[0]).then_inc(w_g[2], 16)
            with e.Fori(1, NG) as c:
                for s in range(2):
                    e.wait_ge(ga_mm, c * 4 + (s - 3))
                    e.dma_start(wr[s], tile_of(w_in, c + (26 + 8 * s))).then_inc(w_g[s], 16)
                e.wait_ge(ga_mm, c * 4)
                e.dma_start(wr[2], tile_of(w_br, c)).then_inc(w_g[2], 16)
            for i in range(KT):
                if i in (1, 2, 3):
                    e.wait_ge(ga_mm, (0, 4 * NG - 3, 4 * NG - 2, 4 * NG)[i])
                elif i >= 4:
                    e.wait_ge(o_mm, i - 3)
                e.dma_start(wr[(i + 3) % 4], w_o[i]).then_inc(w_ob[(i + 3) % 4], 16)

            def up_tiles(it):
                for s in range(4):
                    if isinstance(it, int):
                        e.wait_ge(o_mm, (6, 7, 8, 5)[s])
                    else:
                        e.wait_ge(up_mm, it * 4 + (s - 3))
                    e.dma_start(wr[s], tile_of(w_up, it * 2 + (s // 2 + NF * (s % 2)))).then_inc(w_u[s], 16)

            up_tiles(0)
            e.dma_start(scv[:, :, :], sconv).then_inc(s_sc, 16)
            with e.Fori(1, NF // 2) as it:
                up_tiles(it)

            def down_half(c, h, s):
                e.dma_start(wd[s], tile_of(w_down, c)[:, h * KH:(h + 1) * KH, :]).then_inc(w_d[s], 16)

            down_half(0, 0, 0)
            e.wait_ge(up_h, NF)
            e.wait_ge(up_cp, 2 * NF)
            for s in range(1, 4):
                down_half(s // 2, s % 2, s)
            with e.Fori(1, KT // 2) as it:
                for s in range(4):
                    e.wait_ge(dn_mm, it * 4 + (s - 3))
                    down_half(it * 2 + s // 2, s % 2, s)
            e.wait_ge(up_cp, 2 * NF)
            e.dma_start(conv_out, cvo[:, :, :]).then_inc(stored, 16)
            for i in range(2):
                e.wait_ge(xn_ready, 3 * KT + 4 * (i + 1))
                e.dma_start(yT[:, 4 * i:4 * i + 4, :], xn[:, 4 * i:4 * i + 4, :]).then_inc(stored, 16)
            e.wait_ge(k_stored, 16)
            e.wait_ge(ws_stored, 16)
            e.wait_ge(st_stored, 16)
            e.wait_ge(stored, 16 * N_STORES)

        @block.tensor
        def _(e):
            def wait(s, n):
                e.wait_ge(s, n)
                e.sem_inc(waited, 1)

            def sumsq_tile(n, k, b):
                e.wait_ge(sq_ready, n * KT + k + 1)
                for h in range(2):
                    i = e.matmul(ps[:, 2 * b + h, 0:HALF], ones, sqb[k % 2][:, h * HALF:(h + 1) * HALF],
                                 start=(k == 0), stop=(k == KT - 1))
                i.then_inc(sq_used, 1)

            def sumsq(n):
                for k in range(KT):
                    sumsq_tile(n, k, 0)

            def split_product(outs, w, act, start, stop):
                wh_, wl_ = w
                for i, (lhs, rhs) in enumerate(((wh_, act[0]), (wh_, act[1]), (wl_, act[0]))):
                    for out, cols in outs:
                        ins = e.matmul(out, lhs, rhs[:, cols], start=(start and i == 0), stop=(stop and i == 2))
                return ins

            def halves_of(b):
                return [(ps[:, 2 * b + h, 0:HALF], slice(h * HALF, (h + 1) * HALF)) for h in range(2)]

            def padded_of(b):
                return [(ps[:, 2 * b, 0:256], slice(0, 256)), (ps[:, 2 * b + 1, 0:320], slice(256, T))]

            def project(outs, w, act, nk, done, k0=0, start=True, stop=True, a0=0, act_ready=None):
                for k in range(nk):
                    if act_ready is not None:
                        act_ready(a0 + k)
                    i = split_product(outs, (w[0][:, k0 + k, :], w[1][:, k0 + k, :]), (act[0][:, a0 + k, :], act[1][:, a0 + k, :]),
                                      start and k == 0, stop and k == nk - 1)
                i.then_inc(done, 1)

            def xn_split(n):
                def ready(k):
                    e.wait_ge((xs_even, xs_odd)[k % 2], n * (KT // 2) + k // 2 + 1)
                return ready

            xs = (xh, xl)
            e.wait_ge(s_c0, 16)
            sumsq(0)
            for r in range(2):
                for s in range(4):
                    e.wait_ge(w_lo, 4 * r + s + 1)
                    if r:
                        e.wait_ge(qk_out, s + 1)
                    project(halves_of(s), (wh[s % 2], wl[s]), xs, KT, qk_tile, act_ready=xn_split(0) if not r and not s else None)
            for j in range(2):
                e.wait_ge(w_lo, 8 + 2 * j + 2)
                for t4 in range(5):
                    if j == 0:
                        e.wait_ge(qk_out, 4 + t4 // 2 + 1)
                    else:
                        e.wait_ge(v_evac, t4 + 1)
                    t0 = t4 * P if t4 < 4 else T - P
                    for k in range(KT):
                        for n, (a, w) in enumerate(((xh, wvh), (xh, wvl), (xl, wvh))):
                            i = e.matmul(ps[:, t4, 256 * j:256 * j + 256], a[:, k, t0:t0 + P], w[j][:, :, k, :],
                                         start=(k == 0 and n == 0), stop=(k == KT - 1 and n == 2))
                    i.then_inc(v_tile, 1)
            for s in range(4):
                e.wait_ge(w_lo, 12 + s + 1)
                e.wait_ge(v_evac, (7, 9, 10, 10)[s])
                project(padded_of(s), (wh[s % 2], wl[s]), xs, KT, rw_tile)

            def rw_proj(it, s):
                e.wait_ge(w_lo, it * 4 + (12 + s + 1))
                e.wait_ge(u_ready, it * 4 + (s - 3))
                project(padded_of(s), (wh[s % 2], wl[s]), xs, KT, rw_tile)

            with e.Fori(1, 3) as it:
                for s in range(4):
                    rw_proj(it, s)
            for s in range(2):
                rw_proj(3, s)

            units = [(h, qt) for h in range(8) for qt in range(4)]
            e.wait_ge(u_ready, NPB)
            e.wait_ge(s_c1, 48)

            def logits(u):
                h, qt = units[u]
                hp, r = h // 2, slice(64 * (h % 2), 64 * (h % 2) + 64)
                if u >= 4:
                    e.wait_ge(at_ex, u - 3)
                e.matmul(ps[:, u % 4, 0:P * (qt + 1)], qk[r, hp, qt * P:(qt + 1) * P], qk[r, HP + hp, 0:P * (qt + 1)],
                         start=True, stop=True).then_inc(at_lg, 1)

            def turn(u):
                h, qt = units[u]
                e.wait_ge(at_pn, u + 1)
                if u >= 2:
                    e.wait_ge(at_tc, u - 1)
                for k in range(qt + 1):
                    i = e.transpose(ps[:, 4 + u % 2, k * P:(k + 1) * P], pr[u % 2][:, k * P:(k + 1) * P], ident)
                i.then_inc(at_tp, 1)

            def values(u):
                h, qt = units[u]
                hp, r = h // 2, slice(64 * (h % 2), 64 * (h % 2) + 64)
                e.wait_ge(at_tc, u + 1)
                if u % 8 == 0 and hp >= 2:
                    e.wait_ge(at_oe, hp - 1)
                for k in range(qt + 1):
                    i = e.matmul(ps[r, 6 + hp % 2, qt * P:(qt + 1) * P], vp[:, k, h * HD:(h + 1) * HD], prT[u % 2][:, k, :],
                                 start=(k == 0), stop=(k == qt))
                i.then_inc(at_pv, 1)

            n = len(units)
            logits(0)
            logits(1)
            for u in range(n + 2):
                if u + 2 < n:
                    logits(u + 2)
                if 1 <= u <= n:
                    turn(u - 1)
                if u >= 2:
                    values(u - 2)

            e.wait_ge(at_oe, HP)
            for hp in range(HP):
                e.wait_ge(pr_sq, hp + 1)
                for h in range(2):
                    i = e.matmul(ps[:, 2 * hp + h, 0:HALF], bones, tmp[hp][:, h * HALF:(h + 1) * HALF], start=True, stop=True)
                i.then_inc(pr_ss, 1)
            e.wait_ge(pr_mx, HP)
            e.wait_ge(pr_lin, 1)
            for hp in range(HP):
                if hp >= 2:
                    e.wait_ge(pr_sig, 2 * (hp - 1))
                for w in range(2):
                    r = slice(64 * w, 64 * w + 64)
                    for h in range(2):
                        i = e.matmul(ps[:, 4 * (hp % 2) + 2 * w + h, 0:HALF], w2a2[r, hp * P:(hp + 1) * P],
                                     wad[r, h * HALF:(h + 1) * HALF], start=True, stop=True)
                    i.then_inc(pr_w, 1)
            e.wait_ge(pr_sig, 2 * HP)
            for hp in range(HP):
                e.wait_ge(pr_b, hp + 1)
                for h in range(2):
                    i = e.matmul(ps[:, h, 0:HALF], bones, tmp[4 * (hp % 2) + 3][:, h * HALF:(h + 1) * HALF], start=True, stop=True)
                i.then_inc(pr_bp, 1)

            def gram(n, bank):
                if bank == 0:
                    wait(ch_stg, n + 1)
                ops = (((sA, sB), (sB, sA)), ((sK, sA), (sB, sR)), ((sK, sR), (sV, None)), ((sB, None), (sK, None)))[bank]
                for j, (lhs, rhs) in enumerate(ops):
                    for hp, r in heads():
                        right = rhs[r, hp, :] if rhs is not None else ident[r, r]
                        i = e.matmul(ps[r, bank, j * 256 + hp * C:j * 256 + (hp + 1) * C], lhs[r, hp, :], right,
                                     start=True, stop=True)
                i.then_inc(ch_g, 1)

            def level_x(c, l):
                if l == 0:
                    wait(ch_amt, 1 if c is None else c + 2)
                wait(ch_te, versions(c) + (l + 1))
                for hp, r in heads():
                    i = e.matmul(ps[r, 0, hp * C:(hp + 1) * C], amt[r, l, hp, :], tt[r, 0, hp, :], start=True, stop=True)
                i.then_inc(ch_x, 1)

            def level_d(c, l):
                if l == 0:
                    wait(ch_ev, 5 if c is None else c * 5 + 10)
                wait(ch_xe, products(c) + (l + 1))
                for hp, r in heads():
                    e.matmul(ps[r, 1, hp * C:(hp + 1) * C], tt[r, 1, hp, :], xx[r, hp, :], start=True, stop=True)
                for hp, r in heads():
                    i = e.matmul(ps[r, 1, 256 + hp * C:256 + (hp + 1) * C], xx[r, hp, :], tt[r, 1, hp, :],
                                 start=True, stop=True)
                i.then_inc(ch_d, 1)

            def chunk_w(c):
                wait(st_ready, c + 1)
                for hp, r in heads():
                    e.matmul(ps[r, 2, hp * C:(hp + 1) * C], sA[r, hp, :], st[r, hp, :], start=True, stop=False)
                    i = e.matmul(ps[r, 2, hp * C:(hp + 1) * C], mm1[r, 0, hp, :], mkv[r, 1, hp, :], start=False, stop=True)
                i.then_inc(ch_w, 1)

            def chunk_u(c):
                wait(ch_we, c + 1)
                wait(ch_te, c * LEVELS + (SAMPLE_LEVELS + LEVELS))
                for hp, r in heads():
                    i = e.matmul(ps[r, 3, hp * C:(hp + 1) * C], tt[r, 1, hp, :], ww[r, hp, :], start=True, stop=True)
                i.then_inc(ch_u, 1)

            def chunk_y(c):
                wait(ch_ue, c + 1)
                for hp, r in heads():
                    d = ps[r, 2, hp * C:(hp + 1) * C]
                    e.matmul(d, st[r, hp, :], sR[r, hp, :], start=True, stop=False)
                    e.matmul(d, uu[r, hp, :], mm1[r, 1, hp, :], start=False, stop=False)
                    i = e.matmul(d, mkv[r, 1, hp, :], mkv[r, 0, hp, :], start=False, stop=True)
                i.then_inc(ch_y, 1)
                for hp, r in heads():
                    d = ps[r, 0, hp * C:(hp + 1) * C]
                    e.matmul(d, bk[r, 0, hp, :], uu[r, hp, :], start=True, stop=False)
                    i = e.matmul(d, bk[r, 1, hp, :], mkv[r, 1, hp, :], start=False, stop=True)
                i.then_inc(ch_s, 1)

            e.wait_ge(pr_done, 1)
            for bank in range(4):
                gram(0, bank)
            for l in range(SAMPLE_LEVELS - 1):
                level_x(None, l)
                level_d(None, l)
            wait(ch_te, SAMPLE_LEVELS)
            e.wait_ge(s_s0, 16)
            halves = [slice(0, 64), slice(64, 128)]
            for hp in range(HP):
                cols = slice(hp * C, (hp + 1) * C)
                e.wait_ge(ss_ex, hp + 1)
                for r in halves:
                    for b in range(DB):
                        e.matmul(ps[r, 2, cols], ex[hp % 2][r, b, :], s0[r, hp, b, :], start=(b == 0), stop=False)
                    i = e.matmul(ps[r, 2, cols], mm1[r, 0, hp, :], mkv[r, 1, hp, :], start=False, stop=True)
                i.then_inc(ss_w, 1)
            e.wait_ge(ss_we, 1)
            for hp, r in heads():
                i = e.matmul(ps[r, 3, hp * C:(hp + 1) * C], tt[r, 1, hp, :], ww[r, hp, :], start=True, stop=True)
            i.then_inc(ss_u, 1)
            e.wait_ge(ss_ue, 1)
            for hp in range(HP):
                cols = slice(hp * C, (hp + 1) * C)
                e.wait_ge(ss_ex, HP + hp + 1)
                for r in halves:
                    for b in range(DB):
                        e.matmul(ps[r, 4, cols], s0[r, hp, b, :], ex[hp % 2][r, b, :], start=(b == 0), stop=False)
                    e.matmul(ps[r, 4, cols], mkv[r, 1, hp, :], mkv[r, 0, hp, :], start=False, stop=False)
                    i = e.matmul(ps[r, 4, cols], uu[r, hp, :], mm1[r, 1, hp, :], start=False, stop=True)
                i.then_inc(ss_y, 1)
            for hp in range(HP):
                exu, exv = (ex[2], ex[3]) if hp % 2 == 0 else (ex[0], ex[1])
                e.wait_ge(ss_ex, 2 * HP + hp + 1)
                if hp >= 2:
                    e.wait_ge(ss_st, hp - 1)
                for r in halves:
                    e.matmul(ps[r, 6 + hp % 2, :], bk[r, 0, hp, :], exu[r, :, :], start=True, stop=False)
                    i = e.matmul(ps[r, 6 + hp % 2, :], bk[r, 1, hp, :], exv[r, :, :], start=False, stop=True)
                i.then_inc(ss_s if hp < HP - 1 else ch_s, 1)
            e.wait_ge(ss_st, HP)

            PER = 2 * NGRP

            def qk_group(b, g):
                wait(kv_in[g % 4], b * 256 + 64 * (g // 4 + 1))
                if g >= 2:
                    wait(sa_ev, b * PER + 2 * (g - 1))
                for hp in range(HP):
                    i = e.matmul(ps[32 * hp:32 * hp + 32, 4 + g % 2, :], qbd[:, hp, :], kring[g % 4][:, :, hp, :],
                                 start=True, stop=True)
                i.then_inc(kv_used, 1)

            def pv_turn(b, g):
                wait(sa_ex, b * (NGRP + 1) + (g + 1))
                if g >= 2:
                    wait(sa_tc, b * (NGRP + 1) + (g - 1))
                if g < NGRP:
                    for q in range(GP):
                        i = e.transpose(ps[:, 4 + g % 2, q * P:(q + 1) * P], lg[:, (g * GP + q) * P:(g * GP + q + 1) * P], ident)
                else:
                    i = e.transpose(ps[0:NS, 4 + g % 2, 0:P], lg[:, PAST:PAST + NS], ident)
                i.then_inc(sa_tp, 1)

            def pv_group(b, g):
                wait(sa_tc, b * (NGRP + 1) + (g + 1))
                if g < NGRP:
                    wait(kv_in[g % 4], b * 256 + 64 * (g // 4 + 3))
                    for q in range(GP):
                        for hp in range(HP):
                            i = e.matmul(ps[32 * hp:32 * hp + 32, 7, 0:P], pT[g % 2][:, q, 32 * hp:32 * hp + 32],
                                         vring[g % 4][:, q, hp * P:(hp + 1) * P], start=(g == 0 and q == 0), stop=False)
                    i.then_inc(kv_used, 1)
                else:
                    for hp in range(HP):
                        i = e.matmul(ps[32 * hp:32 * hp + 32, 7, 0:P], pT[g % 2][0:NS, 0, 32 * hp:32 * hp + 32],
                                     vsm[0:NS, hp * P:(hp + 1) * P], start=False, stop=True)
                    i.then_inc(sa_nw, 1)

            e.sem_inc(sa_lg, 1)
            with e.Fori(0, DB) as b:
                wait(sa_q, b * 2 + 2)
                for g in range(NGRP):
                    qk_group(b, g)
                    if g < 2:
                        gram(b + 1, 2 * g)
                        gram(b + 1, 2 * g + 1)
                    elif g % 2 == 0:
                        level_x(b, g // 2 - 1)
                    else:
                        level_d(b, g // 2 - 1)
                wait(sa_ev, b * PER + 2 * (NGRP - 1))
                for hp in range(HP):
                    i = e.matmul(ps[32 * hp:32 * hp + 32, 4, 0:NS], qbd[:, hp, :], qks[:, HP + hp, :], start=True, stop=True)
                i.then_inc(sa_lg, 1)
                level_x(b, 3)
                for g in range(NGRP + 2):
                    if g <= NGRP:
                        pv_turn(b, g)
                    if g >= 1:
                        pv_group(b, g - 1)
                    if g == 1:
                        level_d(b, 3)
                    elif g == 2:
                        level_x(b, 4)
                    elif g == 3:
                        level_d(b, 4)
                    elif g == 4:
                        chunk_w(b)
                    elif g == 5:
                        chunk_u(b)
                    elif g == 6:
                        chunk_y(b)
                e.wait_ge(sa_ob, b + 1)
                e.wait_ge(sa_oo, b + 1)
                e.transpose(ps[:, 6, 0:P], ob, ident).then_inc(sa_ot, 1)

            e.wait_ge(ch_ye, NCH)
            e.wait_ge(sa_oo, DB + 1)
            def head_sums(hp, w, act):
                for h in range(2):
                    i = e.matmul(ps[:, 2 * hp + h, 0:HALF], w, act[:, h * HALF:(h + 1) * HALF], start=True, stop=True)
                i.then_inc(gn_mm, 1)

            for hp in range(HP):
                head_sums(hp, bones, R[:, hp, :])
            for hp in range(HP):
                e.wait_ge(gn_sq, hp + 1)
                head_sums(hp, bones, tmp[4 + hp])
            for hp in range(HP):
                e.wait_ge(gn_rt, hp + 1)
                head_sums(hp, g2[:, hp * P:(hp + 1) * P], gd)

            def gates(c):
                first = isinstance(c, int)
                for s in range(2):
                    e.wait_ge(w_lo, c * 3 + (W_GATE + s + 1))
                    if first:
                        e.wait_ge(gn_out, s + 1)
                    e.wait_ge(ga_free[s], c + 1)
                    project(halves_of(s), (wh[s], wl[s]), xs, KT, ga_mm, act_ready=xn_split(1) if first and not s else None)
                e.wait_ge(w_lo, c * 3 + (W_GATE + 3))
                for s, act in ((2, (oah, oal)), (3, (ybh, ybl))):
                    if first:
                        e.wait_ge((oa_split, yb_split)[s - 2], (1, HP)[s - 2])
                    e.wait_ge(ga_free[s], c + 1)
                    project(halves_of(s), (wh[2], wl[2]), act, HP, ga_mm, k0=HP * (s - 2))

            gates(0)
            with e.Fori(1, NG) as c:
                gates(c)
            for i in range(KT):
                e.wait_ge(w_lo, W_OUT + i + 1)
                if i == 0:
                    e.wait_ge(ga_free[0], NG + 1)
                elif i < 3:
                    e.wait_ge(ga_free[i], NG + 1)
                else:
                    e.wait_ge(h_done, i - 2)
                project(halves_of(i % 3), (wh[i % 3], wl[(i + 3) % 4]), (mh, ml), KT, o_mm,
                        act_ready=(lambda k: e.wait_ge(m_done, k + 2)) if i == 0 else None)
                if i == 2:
                    e.wait_ge(ga_free[3], NG + 1)
                if i >= 2:
                    sumsq_tile(1, i - 2, 3)
            for k in (KT - 2, KT - 1):
                sumsq_tile(1, k, 3)

            def up(it):
                first = isinstance(it, int)
                for s in range(4):
                    e.wait_ge(w_lo, it * 4 + (W_UP + s + 1))
                    if not first:
                        e.wait_ge(up_ev, it * 4 + (s - 3))
                    if first and s == 0:
                        e.wait_ge(ms_ready, 2)
                    project(padded_of(s), (wuh[s % 2], wl[s]), xs, KT, up_mm, act_ready=xn_split(2) if first and not s else None)

            up(0)
            with e.Fori(1, NF // 2) as it:
                up(it)

            def down(it):
                first = isinstance(it, int)
                for s in range(4):
                    e.wait_ge(w_lo, it * 4 + (W_DOWN + s + 1))
                    if not first and s % 2 == 0:
                        e.wait_ge(y_done, it * 2 + (s // 2 - 1))
                    project(halves_of(s // 2), (wdh[s], wdl[s]), (hhh, hhl), KH, dn_mm, start=(s % 2 == 0), stop=(s % 2 == 1),
                            a0=KH * (s % 2), act_ready=(lambda k: e.wait_ge(hh_lo, k + 1)) if first and s < 2 else None)

            down(0)
            with e.Fori(1, KT // 2) as it:
                down(it)
            e.wait_ge(y_done, KT)
            sumsq(2)

        @block.scalar
        def _(e):
            def square(n, k):
                if n == 0:
                    e.wait_ge(s_x[k // 2], 16)
                if k >= 2:
                    e.wait_ge(sq_used, n * KT + k - 1)
                e.activation(sqb[k % 2], x[:, k, :], ACT.Square).then_inc(sq_ready, 1)

            def squares(n):
                for k in range(KT):
                    square(n, k)

            def root(n):
                e.wait_ge(ms_ready, n + 1)
                e.activation(rs, rs, ACT.Sqrt).then_inc(rt_ready, 1)

            def w_split(hi, raw, arrived, n):
                e.wait_ge(arrived, n)
                e.activation(hi[:, :, :], raw, ACT.Copy).then_inc(w_hi, 1)

            def x_split(n):
                for k in range(KT):
                    e.wait_ge(xn_ready, n * KT + k + 1)
                    e.activation(xh[:, k, :], xn[:, k, :], ACT.Copy).then_inc(xh_ready, 1)

            squares(0)
            w_split(wh[0], wr[0], w_a[0], 16)
            root(0)
            x_split(0)
            w_split(wh[1], wr[1], w_a[1], 16)
            for c in range(2 * HP):
                e.wait_ge(qk_tile, c + 1)
                e.activation(lin(qk[:, c, :]), pair(c % 4), ACT.Copy).then_inc(qk_out, 1)
                if c < 6:
                    w_split(wh[c % 2], wr[(c + 2) % 4], w_a[(c + 2) % 4], 16 * ((c + 2) // 4 + 1))
                else:
                    w_split(wvh[0][:, c - 6], wr[c - 6], w_a[c - 6], 48)
            for s in range(2):
                w_split(wvh[1][:, s], wr[2 + s], w_a[2 + s], 48)
            for s in range(2):
                w_split(wh[s], wr[s], w_a[s], 64)

            def shift_in(it, s):
                u = ub[s % 2]
                e.wait_ge(rw_tile, it * 4 + (s + 1))
                if s >= 2 or not (isinstance(it, int) and it == 0):
                    e.wait_ge(xm_done, it * 4 + (s - 1))
                    e.wait_ge(tsh_done, it * 4 + (s - 1))
                e.activation(u[:, 1:513].rearrange("p (h n) -> p h n", h=2), ps[:, 2 * s:2 * s + 2, 0:256], ACT.Copy)
                e.activation(u[:, 513:585].rearrange("p (b n) -> p b n", b=DB)[:, :, 1:9],
                             ps[:, 2 * s + 1, 256:320].rearrange("p (b n) -> p b n", b=DB), ACT.Copy).then_inc(u_ready, 1)
                if not (isinstance(it, int) and it == 3):
                    n = (s + 2) % 4
                    w_split(wh[s % 2], wr[n], w_a[n], it * 16 + (64 if s < 2 else 80))

            e.wait_ge(init_done, 1)
            for s in range(4):
                shift_in(0, s)
            with e.Fori(1, 3) as it:
                for s in range(4):
                    shift_in(it, s)
            for s in range(2):
                shift_in(3, s)

            units = [(h, qt) for h in range(8) for qt in range(4)]
            n = len(units)
            for u in range(n + 1):
                if u < n:
                    w = P * (units[u][1] + 1)
                    e.wait_ge(at_mx, u + 1)
                    if u >= 2:
                        e.wait_ge(at_tp, u - 1)
                    e.activation(pr[u % 2][:, 0:w], ps[:, u % 4, 0:w], ACT.Exp, bias=nmx[:, u % 8:u % 8 + 1], scale=SCALE,
                                 accum_out=rsm[:, u % 8:u % 8 + 1]).then_inc(at_ex, 1)
                if u >= 1:
                    v = u - 1
                    w = P * (units[v][1] + 1)
                    e.wait_ge(at_tp, v + 1)
                    if v >= 2:
                        e.wait_ge(at_pv, v - 1)
                    e.activation(prT[v % 2][:, :, :].rearrange("p a b -> p (a b)")[:, 0:w], ps[:, 4 + v % 2, 0:w],
                                 ACT.Copy).then_inc(at_tc, 1)

            e.wait_ge(xm_done, NPB)
            e.wait_ge(k_stored, 16)
            for hp in range(HP):
                e.activation(tmp[hp], K[:, hp, :], ACT.Square, scale=pcol("kk", hp)).then_inc(pr_sq, 1)
            e.activation(wad[0:64, :], wad[0:64, :], ACT.Tanh).then_inc(pr_lin, 1)
            e.activation(gd, gd, ACT.Sigmoid)
            for hp in range(HP):
                e.wait_ge(pr_mx, hp + 1)
                e.activation(tmp[4 + hp], tmp[4 + hp], ACT.Sqrt).then_inc(pr_rt, 1)
            for hp in range(HP):
                for w, (dst, name) in enumerate(((AL, "w0"), (BE, "a0"))):
                    e.wait_ge(pr_w, 2 * hp + w + 1)
                    e.activation(lin(dst[:, hp, :]), pair(2 * (hp % 2) + w), ACT.Sigmoid, bias=pcol(name, hp)).then_inc(pr_sig, 1)
            for hp in range(HP):
                total, before, up_to, f = tmp[4 * (hp % 2):4 * (hp % 2) + 4]
                e.wait_ge(pr_exc, hp + 1)
                e.activation(f, BE[:, hp, :], ACT.Identity, bias=omka[:, hp:hp + 1], scale=pcol("ka", hp)).then_inc(pr_exp, 1)
                if hp >= 2:
                    e.wait_ge(pr_r, hp - 1)
                e.activation(up_to, total, ACT.Exp, scale=-EM05)
                e.activation(before, before, ACT.Exp, scale=-EM05)
                e.activation(total, total, ACT.Exp, scale=EM05).then_inc(pr_exp, 1)

            e.wait_ge(pr_done, 1)
            e.activation(stg[:, :, :], rw[:, :, SEQ:T], ACT.Copy).then_inc(ch_stg, 1)

            e.wait_ge(ws_stored, 16)
            with e.Fori(0, DB) as b:
                for g in range(NGRP):
                    e.wait_ge(kv_used, b * (2 * NGRP) + (g + 1))
                    for j in range(2):
                        blk = 2 * g + j
                        e.activation(lg[:, blk * BLK:(blk + 1) * BLK], ps[:, 4 + g % 2, j * BLK:(j + 1) * BLK], ACT.Identity,
                                     accum_out=gs[:, blk:blk + 1]).then_inc(sa_ev, 1)
                e.wait_ge(sa_bi, b + 1)
                for g in range(NGRP + 2):
                    if g < NGRP:
                        for k in (2 * g, 2 * g + 1):
                            i = e.activation(lg[:, k * BLK:(k + 1) * BLK], lg[:, k * BLK:(k + 1) * BLK], ACT.Exp,
                                             bias=bi[:, k:k + 1], scale=SCALE, accum_out=psm[:, k:k + 1])
                        i.then_inc(sa_ex, 1)
                    elif g == NGRP:
                        e.activation(lg[:, PAST:PAST + NS], lg[:, PAST:PAST + NS], ACT.Exp, bias=bi[:, NBLK:NBLK + 1],
                                     scale=SCALE, accum_out=psm[:, NBLK:NBLK + 1]).then_inc(sa_ex, 1)
                    if g >= 1:
                        v = g - 1
                        e.wait_ge(sa_tp, b * (NGRP + 1) + (v + 1))
                        if v >= 2:
                            e.wait_ge(kv_used, b * (2 * NGRP) + (NGRP + v - 1))
                        if v < NGRP:
                            e.activation(pT[v % 2][:, :, :].rearrange("p a b -> p (a b)"), ps[:, 4 + v % 2, :], ACT.Copy).then_inc(sa_tc, 1)
                        else:
                            e.activation(pT[v % 2][0:NS, 0, :], ps[0:NS, 4 + v % 2, 0:P], ACT.Copy).then_inc(sa_tc, 1)

            for hp in range(HP):
                e.wait_ge(gn_dev, hp + 1)
                e.activation(tmp[4 + hp], tmp[hp], ACT.Square).then_inc(gn_sq, 1)
            for hp in range(HP):
                e.wait_ge(gn_mm, HP + hp + 1)
                e.activation(lin(tmp[4 + hp]), pair(hp), ACT.Sqrt, bias=geps, scale=1.0 / HD).then_inc(gn_rt, 1)
            e.wait_ge(st_stored, 16)
            x_split(1)
            w_split(wh[0], wr[0], w_g[0], 16)
            for hp in range(HP):
                e.wait_ge(gn_nm, hp + 1)
                e.activation(tmp[hp], tmp[hp], ACT.Identity, bias=pcol("lb", hp), scale=pcol("lg", hp)).then_inc(gn_aff, 1)
            w_split(wh[1], wr[1], w_g[1], 16)
            for hp in range(HP):
                e.wait_ge(gn_out, hp + 1)
                e.activation(ybh[:, hp, :], yb[:, hp, :], ACT.Copy).then_inc(yb_hi, 1)

            for s in range(2):
                e.sem_inc(ga_free[s], 1)

            def gates(c, last=False):
                e.wait_ge(m_done, c + 1)
                for s, g in ((0, g0), (1, g1)):
                    e.wait_ge(ga_mm, c * 4 + (s + 1))
                    e.activation(lin(g), pair(s), ACT.Sigmoid).then_inc(ga_free[s], 1)
                    if s == 0:
                        w_split(wh[2], wr[2], w_g[2], c * 16 + 16)
                    elif not last:
                        w_split(wh[0], wr[0], w_g[0], c * 16 + 32)
                        w_split(wh[1], wr[1], w_g[1], c * 16 + 32)

            with e.Fori(0, NG - 1) as c:
                gates(c)
            gates(NG - 1, last=True)
            for i in range(KT):
                if i == 2:
                    e.wait_ge(ga_mm, 4 * NG)
                elif i >= 3:
                    e.wait_ge(o_mm, i - 2)
                w_split(wh[i % 3], wr[(i + 3) % 4], w_ob[(i + 3) % 4], 16 * (i // 4 + 1))
                if i >= 3:
                    e.wait_ge(h_done, i - 2)
                    square(1, i - 3)
            for k in range(KT - 3, KT):
                e.wait_ge(h_done, k + 1)
                square(1, k)
            w_split(wuh[0], wr[0], w_u[0], 16)
            root(1)
            x_split(2)
            w_split(wuh[1], wr[1], w_u[1], 16)

            def up(it, last=False):
                later = last or not isinstance(it, int)
                for s in range(4):
                    col = it * 2 + (s // 2 + NF * (s % 2))
                    e.wait_ge(up_mm, it * 4 + (s + 1))
                    if later:
                        e.wait_ge(up_cp, it * 4 + (s - 3))
                        e.wait_ge(up_h, it * 2 + (s // 2 - 1))
                    e.activation(cu[s][:, 2:514].rearrange("p (h n) -> p h n", h=2), ps[:, 2 * s:2 * s + 2, 0:256], ACT.Copy)
                    e.activation(cu[s][:, 514:594].rearrange("p (b n) -> p b n", b=DB)[:, :, 2:10],
                                 ps[:, 2 * s + 1, 256:320].rearrange("p (b n) -> p b n", b=DB), ACT.Copy).then_inc(up_ev, 1)
                    if s < 2 or not last:
                        n = (s + 2) % 4
                        w_split(wuh[s % 2], wr[n], w_u[n], it * 16 + (16 if s < 2 else 32))
                    e.wait_ge(up_ev, it * 4 + (s + 1))
                    e.wait_ge(up_st, it * 4 + (s + 1))
                    e.activation(cc[s], cu[s][:, 2:594], ACT.Identity, bias=pcol("cb", col), scale=pcol("cw2", col)).then_inc(up_c0, 1)
                for s in (1, 3):
                    e.wait_ge(up_cv, it * 4 + (s + 1))
                    e.activation(cc[s], cc[s], ACT.Silu).then_inc(up_si, 1)

            up(0)
            with e.Fori(1, NF // 2 - 1) as it:
                up(it)
            up(NF // 2 - 1, last=True)
            for s in range(2):
                w_split(wdh[s], wd[s], w_d[s], 16)
                for k in range(KH * s, KH * (s + 1)):
                    e.wait_ge(up_h, k + 1)
                    e.activation(hhh[:, k, :], hh[:, k, :], ACT.Copy).then_inc(hh_hi, 1)
            for s in range(2, 4):
                w_split(wdh[s], wd[s], w_d[s], 16)
            with e.Fori(1, KT // 2) as it:
                for s in range(4):
                    w_split(wdh[s], wd[s], w_d[s], it * 16 + 16)
            e.wait_ge(y_done, KT)
            squares(2)
            root(2)

        @block.gpsimd
        def _(e):
            def w_split(n, lo, raw, hi):
                e.wait_ge(w_hi, n + 1)
                e.tensor_tensor(lo[:, :, :], raw, hi[:, :, :], ALU.subtract).then_inc(w_lo, 1)

            def x_split(n):
                for k in range(1, KT, 2):
                    e.wait_ge(xh_ready, n * KT + k + 1)
                    e.tensor_tensor(xl[:, k, :], xn[:, k, :], xh[:, k, :], ALU.subtract).then_inc(xs_odd, 1)

            w_split(0, wl[0], wr[0], wh[0])
            x_split(0)
            for n in range(1, 14):
                if 8 <= n < 12:
                    w_split(n, wvl[(n - 8) // 2][:, n % 2], wr[n % 4], wvh[(n - 8) // 2][:, n % 2])
                else:
                    w_split(n, wl[n % 4], wr[n % 4], wh[n % 2])
            e.wait_ge(qk_out, 2 * HP)
            e.tensor_copy(qks[:, :, :], qk[:, :, SEQ:T]).then_inc(qks_done, 1)

            def last_rows(g, s):
                e.wait_ge(u_ready, g + 1)
                dst = tsh[:, g:g + 1, :] if isinstance(g, int) else tsh[:, bass.ds(g, 1), :]
                e.tensor_copy(dst, ub[s % 2][:, 512:593].rearrange("p (o b n) -> p o b n", o=1, n=9)[:, :, :, 0]).then_inc(tsh_done, 1)

            with e.Fori(0, 3) as it:
                for s in range(4):
                    last_rows(it * 4 + s, s)
                    n = (s + 2) % 4
                    w_split(it * 4 + (14 + s), wl[n], wr[n], wh[s % 2])
            for s in range(2):
                last_rows(12 + s, s)

            def stage(n, cols):
                if cols is not None:
                    e.wait_ge(ch_s, n)
                    e.tensor_copy(stg[:, :, :], rw[:, :, cols]).then_inc(ch_stg, 1)
                e.wait_ge(ch_ev, n * 5 + 1)
                for l in range(LEVELS - 1):
                    i = e.tensor_tensor(amt[:, l, :, :], aa[:, 1, :, :], mone("lvl", 128 * (l + 1) + 64), ALU.mult)
                i.then_inc(ch_amt, 1)

            for hp in range(HP):
                up_to = tmp[4 * (hp % 2) + 2]
                e.wait_ge(pr_b, hp + 1)
                e.wait_ge(pr_exp, 2 * hp + 2)
                e.tensor_copy(lc[:, hp, 0:8], up_to[:, 0:SEQ].rearrange("p (c n) -> p c n", n=C)[:, :, C - 1])
                e.tensor_copy(lc[:, hp, 8:16], up_to[:, SEQ:T].rearrange("p (c n) -> p c n", n=DT)[:, :, DT - 1])
                e.tensor_tensor(R[:, hp, :], R[:, hp, :], up_to, ALU.mult).then_inc(pr_r, 1)
            stage(0, None)
            with e.Fori(0, DB) as b:
                e.wait_ge(sa_lg, b + 1)
                e.tensor_copy(qbd[0:64, :, 0:8], qks[0:64, 0:HP, bass.ds(b * DT, DT)]).then_inc(sa_q, 1)
                e.wait_ge(sa_q, b * 2 + 1)
                e.tensor_copy(qbd[64:128, :, 8:16], qks[64:128, 0:HP, bass.ds(b * DT, DT)]).then_inc(sa_q, 1)
                e.wait_ge(sa_q, b * 2 + 2)
                stage(b + 1, bass.ds(b * C, C))

            x_split(1)
            with e.Fori(0, NG) as c:
                for s in range(3):
                    w_split(c * 3 + (W_GATE + s), wl[s], wr[s], wh[s])
            for i in range(KT):
                w_split(W_OUT + i, wl[(i + 3) % 4], wr[(i + 3) % 4], wh[i % 3])
            e.wait_ge(o_mm, KT)
            for s in range(4):
                i = e.memset(cu[s][:, 0:2], 0.0)
            i.then_inc(up_z, 1)
            w_split(W_UP, wl[0], wr[0], wuh[0])
            x_split(2)
            w_split(W_UP + 1, wl[1], wr[1], wuh[1])
            e.wait_ge(s_sc, 16)

            def conv_rows(it, last=False):
                for s in range(4):
                    col = it * 2 + (s // 2 + NF * (s % 2))
                    at_ = bass.ds(col, 1)
                    if isinstance(it, int):
                        at_ = slice(col, col + 1)
                    if last or not isinstance(it, int):
                        e.wait_ge(up_cv, it * 4 + (s - 3))
                    e.tensor_copy(cu[s][:, 514:594].rearrange("p (b n) -> p b n", b=DB)[:, :, 0:2],
                                  scv[:, at_, :].rearrange("p o (b n) -> p (o b) n", b=DB)).then_inc(up_st, 1)
                    e.wait_ge(up_ev, it * 4 + (s + 1))
                    e.tensor_copy(cvo[:, at_, :].rearrange("p o (b n) -> p (o b) n", b=9),
                                  cu[s][:, 512:602].rearrange("p (b n) -> p b n", b=9)[:, :, 0:2]).then_inc(up_cp, 1)
                    if s < 2 or not last:
                        n = (s + 2) % 4
                        w_split(it * 4 + (W_UP + s + 2), wl[n], wr[n], wuh[s % 2])

            conv_rows(0)
            with e.Fori(1, NF // 2 - 1) as it:
                conv_rows(it)
            conv_rows(NF // 2 - 1, last=True)
            with e.Fori(0, KT // 2) as it:
                for s in range(4):
                    w_split(it * 4 + (W_DOWN + s), wdl[s], wd[s], wdh[s])

        @block.vector
        def _(e):
            def rstd(n):
                own_ = Line(e, own["norm"], 2 * n)
                e.wait_ge(sq_used, (n + 1) * KT)
                own_.did(e.tensor_scalar(lin(rs), pair(3 if n == 1 else 0), 1.0 / D, EPS, ALU.mult, ALU.add))
                own_.settle()
                e.sem_inc(ms_ready, 1)
                e.wait_ge(rt_ready, n + 1)
                own_.did(e.reciprocal(rs, rs))
                own_.settle()

            def normed(gain, n=None):
                for k in range(KT + 2):
                    if k < KT:
                        e.scalar_tensor_tensor(out=xn[:, k, :], in0=x[:, k, :], scalar=pcol(gain, k), in1=rs,
                                               op0=ALU.mult, op1=ALU.mult).then_inc(xn_ready, 1)
                    if n is not None and k >= 2 and k % 2 == 0:
                        e.wait_ge(xh_ready, n * KT + k - 1)
                        e.tensor_tensor(xl[:, k - 2, :], xn[:, k - 2, :], xh[:, k - 2, :], ALU.subtract).then_inc(xs_even, 1)

            ln = Line(e, own["attn"])
            for u in ub:
                ln.did(e.memset(u[:, :], 0.0))
            ln.did(e.memset(qbd[:, :, :], 0.0))
            ln.did(e.memset(mb[:, :], 0.0))
            ln.settle()
            SETUP = ln.n
            e.sem_inc(init_done, 1)
            e.wait_ge(s_pv, 16)
            rstd(0)
            normed("ln1", 0)
            e.tensor_scalar(omka, pv[:, PV["ka"]:PV["ka"] + HP], -1.0, 1.0, ALU.mult, ALU.add)
            for j in range(2):
                cols = slice(256 * j, 256 * j + 256)
                for t4 in range(5):
                    e.wait_ge(v_tile, 5 * j + t4 + 1)
                    if t4 < 4:
                        e.tensor_copy(vp[:, t4, cols], ps[:, t4, cols]).then_inc(v_evac, 1)
                    else:
                        e.tensor_copy(vsm[0:NS, cols], ps[P - NS:P, t4, cols]).then_inc(v_evac, 1)

            SH = 2
            e.wait_ge(s_c1, 48)

            def shift(g, s, base, dst):
                ln = Line(e, own["shift"], base)
                u = ub[s % 2]
                e.wait_ge(u_ready, g + 1)
                src = shs[:, g, :] if isinstance(g, int) else shs[:, bass.ds(g, 1), :].rearrange("p o b -> p (o b)")
                ln.did(e.tensor_scalar(u[:, 513:585].rearrange("p (b n) -> p b n", b=DB)[:, :, 0], src, 1.0, None, ALU.mult))
                ln.settle()
                ln.did(e.tensor_tensor(df[:, 0:584], u[:, 0:584], u[:, 1:585], ALU.subtract))
                ln.settle()
                mu = pcol("mu", g)
                e.scalar_tensor_tensor(out=dst[:, 0:SEQ], in0=df[:, 0:SEQ], scalar=mu, in1=u[:, 1:513],
                                       op0=ALU.mult, op1=ALU.add)
                e.scalar_tensor_tensor(out=dst[:, SEQ:T].rearrange("p (b n) -> p b n", b=DB),
                                       in0=df[:, 513:585].rearrange("p (b n) -> p b n", b=DB)[:, :, 0:8], scalar=mu,
                                       in1=u[:, 514:586].rearrange("p (b n) -> p b n", b=DB)[:, :, 0:8],
                                       op0=ALU.mult, op1=ALU.add).then_inc(xm_done, 1)
                assert ln.n == SH

            with e.Fori(0, 3) as it:
                for s in range(4):
                    shift(it * 4 + s, s, it * (4 * SH) + SH * s, rw[:, bass.ds(it * 4 + s, 1), :].rearrange("p o n -> p (o n)"))
            for s, dst in enumerate((wad, gd)):
                shift(12 + s, s, SH * (12 + s), dst)

            ln = Line(e, own["attn"], SETUP)
            units = [(h, qt) for h in range(8) for qt in range(4)]
            n = len(units)
            for u in range(n + 2):
                if u < n:
                    qt = units[u][1]
                    w, j = P * (qt + 1), u % 8
                    e.wait_ge(at_lg, u + 1)
                    diag = ps[:, u % 4, w - P:w]
                    ln.did(e.tensor_tensor(diag, diag, causal, ALU.add))
                    ln.settle()
                    ln.did(e.tensor_reduce(mx[:, j:j + 1], ps[:, u % 4, 0:w], AX.X, ALU.max))
                    ln.settle()
                    e.tensor_scalar(nmx[:, j:j + 1], mx[:, j:j + 1], -SCALE, None, ALU.mult).then_inc(at_mx, 1)
                if 1 <= u <= n:
                    v = u - 1
                    w, j = P * (units[v][1] + 1), v % 8
                    e.wait_ge(at_ex, v + 1)
                    ln.did(e.reciprocal(rin[:, j:j + 1], rsm[:, j:j + 1]))
                    ln.settle()
                    e.tensor_scalar(pr[v % 2][:, 0:w], pr[v % 2][:, 0:w], rin[:, j:j + 1], None, ALU.mult).then_inc(at_pn, 1)
                if u >= 9 and (u - 9) % 8 == 0:
                    hp = (u - 9) // 8
                    e.wait_ge(at_pv, 8 * hp + 8)
                    e.tensor_copy(oa[:, hp, 0:SEQ], ps[:, 6 + hp % 2, :]).then_inc(at_oe, 1)

            ln = Line(e, own["prep"])
            e.wait_ge(qks_done, 1)
            e.wait_ge(tsh_done, NPB)
            for hp in range(HP):
                e.wait_ge(pr_ss, hp + 1)
                e.tensor_scalar(lin(tmp[4 + hp]), pair(hp), 1e-24, None, ALU.max).then_inc(pr_mx, 1)
            for hp in range(HP):
                e.wait_ge(pr_rt, hp + 1)
                ln.did(e.reciprocal(tmp[4 + hp], tmp[4 + hp]))
            ln.settle()
            for hp in range(HP):
                ln.did(e.scalar_tensor_tensor(out=yb[:, hp, :], in0=K[:, hp, :], scalar=pcol("kk", hp), in1=tmp[4 + hp],
                                              op0=ALU.mult, op1=ALU.mult))
            ln.settle()

            def running(hp):
                total, before, up_to, f = tmp[4 * (hp % 2):4 * (hp % 2) + 4]
                e.wait_ge(pr_sig, 2 * hp + 2)
                ln.did(e.tensor_tensor_scan(total, reset, AL[:, hp, :], 0.0, ALU.mult, ALU.add))
                ln.settle()
                e.tensor_tensor(before, total, AL[:, hp, :], ALU.subtract).then_inc(pr_exc, 1)

            running(0)
            running(1)
            for hp in range(HP):
                r_, k_, v_, al, be, kk = (a[:, hp, :] for a in (R, K, V, AL, BE, yb))
                total, before, up_to, f = tmp[4 * (hp % 2):4 * (hp % 2) + 4]
                e.wait_ge(pr_exp, 2 * hp + 1)
                ln.did(e.tensor_tensor(k_, k_, f, ALU.mult))
                ln.did(e.tensor_tensor(be, be, kk, ALU.mult))
                ln.settle()
                e.scalar_tensor_tensor(out=f, in0=r_, scalar=pcol("rk", hp), in1=k_, op0=ALU.mult, op1=ALU.mult).then_inc(pr_b, 1)
                e.wait_ge(pr_exp, 2 * hp + 2)
                ln.did(e.scalar_tensor_tensor(out=al, in0=kk, scalar=-1.0, in1=before, op0=ALU.mult, op1=ALU.mult))
                ln.did(e.tensor_tensor(be, be, total, ALU.mult))
                e.wait_ge(pr_b, hp + 1)
                ln.did(e.tensor_tensor(k_, k_, total, ALU.mult))
                ln.settle()
                e.wait_ge(pr_bp, hp + 1)
                ln.did(e.tensor_tensor(lin(kk), lin(v_), pair(0), ALU.mult))
                if hp + 2 < HP:
                    ln.settle()
                    running(hp + 2)
            e.wait_ge(pr_r, HP)
            ln.did(e.memset(st[:, :, :], 0.0))
            ln.settle()
            e.sem_inc(st_ready, 1)
            e.sem_inc(pr_done, 1)

            def gram_out(n, bank, base, own_sem, masks):
                e.wait_ge(ch_g, n * 4 + (bank + 1))
                if bank == 0:
                    ln = Line(e, own_sem, base)
                    e.tensor_tensor(aa[:, :, :, :], q8(0), mpair(masks[0]), ALU.mult).then_inc(ch_ev, 1)
                    e.wait_ge(ch_ev, n * 5 + 1)
                    ln.did(e.tensor_tensor(tt[:, :, :, :], aa[:, :, :, :], mpair("lvl"), ALU.mult))
                    ln.settle()
                    e.tensor_tensor(tt[:, :, :, :], tt[:, :, :, :], mpair("eye2"), ALU.add).then_inc(ch_te, 1)
                elif bank == 1:
                    e.tensor_tensor(mm1[:, :, :, :], q8(1), mpair(masks[1]), ALU.mult).then_inc(ch_ev, 1)
                elif bank == 2:
                    e.tensor_tensor(mkv[:, 0, :, :], q4(2, 0), mone(masks[1], 64), ALU.mult).then_inc(ch_ev, 1)
                    e.tensor_copy(mkv[:, 1, :, :], q4(2, 1)).then_inc(ch_ev, 1)
                else:
                    e.tensor_copy(bk[:, :, :, :], q8(3)).then_inc(ch_ev, 1)

            def x_out(c, l):
                e.wait_ge(ch_x, products(c) + (l + 1))
                e.tensor_copy(xx[:, :, :], q4(0)).then_inc(ch_xe, 1)

            def d_out(c, l):
                e.wait_ge(ch_d, products(c) + (l + 1))
                e.tensor_tensor(tt[:, :, :, :], tt[:, :, :, :], q8(1), ALU.add).then_inc(ch_te, 1)

            for bank in range(4):
                gram_out(0, bank, 0, own["chunk"], ("ms0", "ms1"))
            for l in range(SAMPLE_LEVELS - 1):
                x_out(None, l)
                d_out(None, l)
            ln = Line(e, own["chunk0"])
            e.wait_ge(s_s0, 16)
            def by_sequence(a, src):
                return e.tensor_tensor(ex[a], src.to_broadcast([P, DB, C]), colm, ALU.mult)

            def own_rows(a, src):
                return e.tensor_tensor(ex[a], src.to_broadcast([P, DB, C]),
                                       rowm.rearrange("p (b o) -> p b o", o=1).to_broadcast([P, DB, C]), ALU.mult)

            for hp in range(HP):
                if hp >= 2:
                    e.wait_ge(ss_w, hp - 1)
                by_sequence(hp % 2, sA[:, hp:hp + 1, :]).then_inc(ss_ex, 1)
            e.wait_ge(ss_w, HP)
            e.tensor_copy(ww[:, :, :], q4(2)).then_inc(ss_we, 1)
            for hp in range(2):
                by_sequence(hp, sR[:, hp:hp + 1, :]).then_inc(ss_ex, 1)
            e.wait_ge(ss_u, 1)
            e.tensor_copy(uu[:, :, :], q4(3)).then_inc(ss_ue, 1)
            for hp in range(2, HP):
                e.wait_ge(ss_y, hp - 1)
                by_sequence(hp % 2, sR[:, hp:hp + 1, :]).then_inc(ss_ex, 1)
            e.wait_ge(ss_ue, 1)

            def new_state(hp):
                e.wait_ge(ss_s if hp < HP - 1 else ch_s, hp + 1 if hp < HP - 1 else 1)
                ln.did(e.tensor_tensor(s0[:, hp, :, :], s0[:, hp, :, :],
                                       ps[:, 6 + hp % 2, :].rearrange("p (b n) -> p b n", b=DB), ALU.add))
                ln.settle()
                e.tensor_tensor(s0[:, hp, :, :], s0[:, hp, :, :],
                                lc[:, hp, 8:16].rearrange("p (b o) -> p b o", o=1).to_broadcast([P, DB, C]), ALU.mult).then_inc(ss_st, 1)

            for hp in range(HP):
                if hp == 1:
                    e.wait_ge(ss_y, HP)
                if hp >= 2:
                    e.wait_ge(ss_s, hp - 1)
                a = 2 if hp % 2 == 0 else 0
                own_rows(a, uu[:, hp:hp + 1, :])
                own_rows(a + 1, mkv[:, 1, hp:hp + 1, :]).then_inc(ss_ex, 1)
                if hp == 1:
                    e.tensor_copy(R[:, :, SEQ:T], q4(4))
                if hp:
                    new_state(hp - 1)
            new_state(HP - 1)

            e.sem_inc(sa_oo, 1)
            e.wait_ge(ws_stored, 16)
            DL = 15
            with e.Fori(0, DB) as b:
                ln = Line(e, own["loop"], b * DL)
                for g in range(NGRP):
                    if g < 2:
                        gram_out(b + 1, 2 * g, b + 1, own["chunk"], ("mp0", "mp1"))
                        gram_out(b + 1, 2 * g + 1, b + 1, own["chunk"], ("mp0", "mp1"))
                    elif g % 2 == 0:
                        x_out(b, g // 2 - 1)
                    else:
                        d_out(b, g // 2 - 1)
                    e.wait_ge(sa_ev, b * (2 * NGRP) + (2 * g + 2))
                    i = e.tensor_reduce(bm[:, 2 * g:2 * g + 2], lg[:, 512 * g:512 * g + 512].rearrange("p (a n) -> p a n", a=2), AX.X, ALU.max)
                ln.did(i)
                e.wait_ge(sa_lg, b + 2)
                ln.did(e.tensor_tensor(lg[:, PAST:PAST + NS], ps[:, 4, 0:NS], cst[:, bass.ds(b * 64 + CV["newm"], 64)], ALU.add))
                gi = gs.rearrange("p (o n) -> p o n", o=1).to_broadcast([P, NBLK, NBLK])
                gj = gs.rearrange("p (n o) -> p n o", o=1).to_broadcast([P, NBLK, NBLK])
                ln.did(e.tensor_tensor(cmp1, gi, gj, ALU.is_gt))
                ln.did(e.tensor_tensor(cmp2, gi, gj, ALU.is_equal))
                ln.settle()
                ln.did(e.tensor_reduce(bm[:, NBLK:NBLK + 1], lg[:, PAST:PAST + NS], AX.X, ALU.max))
                ln.did(e.tensor_tensor(cmp2, cmp2, tri, ALU.mult))
                ln.settle()
                ln.did(e.tensor_tensor(cmp1, cmp1, cmp2, ALU.add))
                ln.settle()
                ln.did(e.tensor_reduce(mb[:, 0:NBLK], cmp1, AX.X, ALU.add))
                ln.settle()
                ln.did(e.tensor_scalar(mb[:, 0:NBLK], mb[:, 0:NBLK], TOPK - 0.5, NEG, ALU.is_ge, ALU.mult))
                ln.settle()
                ln.did(e.tensor_tensor(bm, bm, mb, ALU.add))
                ln.settle()
                ln.did(e.tensor_reduce(sc[:, 0:1], bm, AX.X, ALU.max))
                ln.settle()
                ln.did(e.tensor_scalar(sc[:, 1:2], sc[:, 0:1], -SCALE, None, ALU.mult))
                ln.settle()
                e.tensor_scalar(bi, mb, sc[:, 1:2], None, ALU.add).then_inc(sa_bi, 1)
                for l in range(3, LEVELS - 1):
                    x_out(b, l)
                    d_out(b, l)
                e.wait_ge(ch_w, b + 1)
                e.tensor_copy(ww[:, :, :], q4(2)).then_inc(ch_we, 1)
                e.wait_ge(ch_u, b + 1)
                e.tensor_copy(uu[:, :, :], q4(3)).then_inc(ch_ue, 1)
                e.wait_ge(ch_y, b + 1)
                e.tensor_copy(R[:, :, bass.ds(b * C, C)], q4(2)).then_inc(ch_ye, 1)
                e.wait_ge(ch_s, b + 2)
                ln.did(e.tensor_tensor(st[:, :, :], st[:, :, :], q4(0), ALU.add))
                ln.settle()
                e.tensor_tensor(st[:, :, :], st[:, :, :], lc[:, :, bass.ds(b, 1)].to_broadcast([P, HP, C]), ALU.mult).then_inc(st_ready, 1)
                e.wait_ge(sa_ex, b * (NGRP + 1) + (NGRP + 1))
                ln.did(e.tensor_reduce(sc[:, 2:3], psm, AX.X, ALU.add))
                ln.settle()
                ln.did(e.reciprocal(sc[:, 3:4], sc[:, 2:3]))
                ln.settle()
                e.wait_ge(sa_nw, b + 1)
                e.tensor_scalar(ob, ps[:, 7, 0:P], sc[:, 3:4], None, ALU.mult).then_inc(sa_ob, 1)
                e.wait_ge(sa_ot, b + 1)
                for half in range(2):
                    r = slice(64 * half, 64 * half + 64)
                    i = e.tensor_copy(oa[r, :, bass.ds(b * DT + SEQ, DT)],
                                      ps[r, 6, 0:P].rearrange("p (a n) -> p a n", a=HP)[:, :, 8 * half:8 * half + 8])
                i.then_inc(sa_oo, 1)
                assert ln.n == DL

            ln = Line(e, own["gn"])
            for hp in range(HP):
                e.wait_ge(gn_mm, hp + 1)
                e.scalar_tensor_tensor(out=lin(tmp[hp]), in0=pair(hp), scalar=-1.0 / HD, in1=lin(R[:, hp, :]),
                                       op0=ALU.mult, op1=ALU.add).then_inc(gn_dev, 1)
            e.wait_ge(kv_used, 2 * DB * NGRP)
            normed("ln1", 1)
            for hp in range(HP):
                e.wait_ge(gn_rt, hp + 1)
                ln.did(e.reciprocal(tmp[4 + hp], tmp[4 + hp]))
            for hp in range(HP):
                e.wait_ge(own["gn"], hp + 1)
                e.tensor_tensor(tmp[hp], tmp[hp], tmp[4 + hp], ALU.mult).then_inc(gn_nm, 1)
            for hp in range(HP):
                e.wait_ge(gn_aff, hp + 1)
                ln.did(e.tensor_tensor(tmp[hp], tmp[hp], yb[:, hp, :], ALU.add))
            for hp in range(HP):
                e.wait_ge(own["gn"], HP + hp + 1)
                e.wait_ge(gn_mm, 2 * HP + hp + 1)
                e.tensor_tensor(lin(yb[:, hp, :]), lin(tmp[hp]), pair(hp), ALU.mult).then_inc(gn_out, 1)
            for hp in range(HP):
                e.wait_ge(yb_hi, hp + 1)
                e.tensor_tensor(ybl[:, hp, :], yb[:, hp, :], ybh[:, hp, :], ALU.subtract).then_inc(yb_split, 1)
            ln.did(e.tensor_copy(oah[:, :, :], oa[:, :, :]))
            ln.settle()
            e.tensor_tensor(oal[:, :, :], oa[:, :, :], oah[:, :, :], ALU.subtract).then_inc(oa_split, 1)

            e.wait_ge(gn_out, HP)
            for s in (2, 3):
                e.sem_inc(ga_free[s], 1)
            e.sem_inc(m_done, 1)
            with e.Fori(0, NG) as c:
                for s, g in ((2, g0), (3, g1)):
                    e.wait_ge(ga_free[s - 2], c + 2)
                    e.wait_ge(ga_mm, c * 4 + (s + 1))
                    e.tensor_tensor(lin(g), lin(g), pair(s), ALU.mult).then_inc(ga_free[s], 1)
                e.wait_ge(ga_free[2], c + 2)
                e.wait_ge(ga_free[3], c + 2)
                ln = Line(e, own["merge"], c * 2)
                mc, mhc, mlc = (a[:, bass.ds(c, 1), :].rearrange("p o n -> p (o n)") for a in (m, mh, ml))
                ln.did(e.tensor_tensor(mc, g0, g1, ALU.add))
                ln.settle()
                ln.did(e.tensor_copy(mhc, mc))
                ln.settle()
                e.tensor_tensor(mlc, mc, mhc, ALU.subtract).then_inc(m_done, 1)
            for c in range(KT):
                e.wait_ge(o_mm, c + 1)
                e.tensor_tensor(lin(x[:, c, :]), lin(x[:, c, :]), pair(c % 3), ALU.add).then_inc(h_done, 1)
            rstd(1)
            normed("ln2", 2)
            e.wait_ge(up_z, 1)

            def up(it):
                for s in range(4):
                    col = it * 2 + (s // 2 + NF * (s % 2))
                    e.wait_ge(up_c0, it * 4 + (s + 1))
                    ln = Line(e, own["up"], it * 4 + s)
                    ln.did(e.scalar_tensor_tensor(out=cc[s], in0=cu[s][:, 1:593], scalar=pcol("cw1", col), in1=cc[s],
                                                  op0=ALU.mult, op1=ALU.add))
                    ln.settle()
                    e.scalar_tensor_tensor(out=cc[s], in0=cu[s][:, 0:592], scalar=pcol("cw0", col), in1=cc[s],
                                           op0=ALU.mult, op1=ALU.add).then_inc(up_cv, 1)
                for s in (1, 3):
                    e.wait_ge(up_si, it * 2 + (s // 2 + 1))
                    e.wait_ge(up_cv, it * 4 + (s + 1))
                    j = it * 2 + s // 2
                    at_ = slice(j, j + 1) if isinstance(j, int) else bass.ds(j, 1)
                    dst = hh[:, at_, :].rearrange("p o n -> p (o n)")
                    e.tensor_tensor(dst[:, 0:SEQ], cc[s][:, 0:SEQ], cc[s - 1][:, 0:SEQ], ALU.mult)
                    e.tensor_tensor(dst[:, SEQ:T].rearrange("p (b n) -> p b n", b=DB),
                                    cc[s][:, 512:592].rearrange("p (b n) -> p b n", b=DB)[:, :, 2:10],
                                    cc[s - 1][:, 512:592].rearrange("p (b n) -> p b n", b=DB)[:, :, 2:10], ALU.mult).then_inc(up_h, 1)

            up(0)
            with e.Fori(1, NF // 2) as it:
                up(it)
            for k in range(NF):
                e.wait_ge(hh_hi, k + 1)
                e.tensor_tensor(hhl[:, k, :], hh[:, k, :], hhh[:, k, :], ALU.subtract).then_inc(hh_lo, 1)
            with e.Fori(0, KT // 2) as it:
                for s in range(2):
                    c = bass.ds(it * 2 + s, 1)
                    e.wait_ge(dn_mm, it * 4 + (2 * s + 2))
                    e.tensor_tensor(lin3(x[:, c, :]), lin3(x[:, c, :]), pair(s), ALU.add).then_inc(y_done, 1)
            rstd(2)
            normed("lnf")


_ARGS = ["xin", "kcache", "vcache", "pages", "s0t", "sshift", "sconv", "pvec", "consts", "lora", "w_in", "w_br", "w_o", "w_up", "w_down"]
_OUTS = [("yT", (P, KT, T)), ("kT", (P, HP, T)), ("v", (P, 4, WA)), ("vs", (NS, WA)), ("wkvp", (P, HP * HD)),
         ("tsh", (P, NPB, 9)), ("conv", (P, 2 * NF, 18)), ("wkvs", (P, HP * DB * HD))]


def kernel(**inputs):
    import concourse.bacc as bacc
    from concourse.bass_utils import run_bass_kernel_spmd

    a = {k: np.asarray(v) for k, v in inputs.items()}

    def tiles(w, nk, cols=None):
        w = w if cols is None else w[:, cols[0]:cols[1]]
        return w.reshape(nk, P, -1, P).transpose(2, 1, 0, 3)

    def fm(v):
        return v.reshape(-1, P).T

    npool = a["cache_k"].shape[1]
    xt = np.concatenate([a["x_prompt"].reshape(SEQ, D), a["x_sample"].reshape(NS, D)])
    cw = a["conv_w"][0]
    d = {
        "xin": xt.T.reshape(KT, P, T).transpose(1, 0, 2),
        "kcache": a["cache_k"][0].transpose(0, 2, 3, 1).reshape(npool, HP, P, PAGE).transpose(0, 2, 1, 3).reshape(npool, P, WA),
        "vcache": a["cache_v"][0].reshape(npool, PAGE, WA),
        "pages": a["page_table"].reshape(1, -1),
        "s0t": a["state_wkv"][0].transpose(1, 3, 0, 2).reshape(HP, P, DB, HD).transpose(1, 0, 2, 3).reshape(P, -1),
        "sshift": a["state_tshift"][0].T.reshape(NPB, P, DB).transpose(1, 0, 2),
        "sconv": a["state_conv"][0].transpose(2, 0, 1).reshape(2 * NF, P, DB * 2).transpose(1, 0, 2),
        "pvec": np.concatenate([fm(a[n][0].reshape(-1)) for n in ("ln1_g", "mu", "w0", "a0", "k_k", "k_a", "r_k", "lnx_g", "lnx_b", "ln2_g")]
                               + [fm(a["lnf_g"]), fm(cw[0]), fm(cw[1]), fm(cw[2]), fm(a["conv_b"][0])], axis=1),
        "consts": constants(),
        "lora": np.concatenate([np.concatenate([a["w2"][0], a["a2"][0]]), a["g2"][0]], axis=1),
        "w_in": tiles(a["w_in"][0], KT),
        "w_br": np.concatenate([tiles(a["w_br_a"][0], HP), tiles(a["w_br_b"][0], HP)], axis=2),
        "w_o": tiles(a["w_o"][0], KT),
        "w_up": tiles(a["w_up"][0], KT),
        "w_down": tiles(a["w_down"][0], NF),
    }
    nc = bacc.Bacc("TRN2", target_bir_lowering=False, num_devices=1)
    arrays, args = {}, []
    for name in _ARGS:
        v = np.ascontiguousarray(d[name])
        arrays["in_" + name] = v
        args.append(nc.dram_tensor("in_" + name, v.shape, mybir.dt.from_np(v.dtype), kind="ExternalInput").ap())
    for name, shape in _OUTS:
        args.append(nc.dram_tensor("out_" + name, shape, F32, kind="ExternalOutput").ap())
    build(nc, *args)
    res = run_bass_kernel_spmd(nc, [arrays], core_ids=[0]).results[0]
    o = {name: np.asarray(res["out_" + name]) for name, _ in _OUTS}
    y = o["yT"].transpose(2, 1, 0).reshape(T, D)
    k = o["kT"].transpose(2, 1, 0).reshape(T, WA)
    v = o["v"].transpose(1, 0, 2).reshape(SEQ, WA)
    tsh = o["tsh"].transpose(2, 1, 0).reshape(9, NPB * P)
    conv = o["conv"].transpose(2, 1, 0).reshape(9, 2, 2 * DFF)
    wp = o["wkvp"].reshape(2, HD, HP, HD).transpose(2, 0, 3, 1).reshape(1, 1, 8, HD, HD)
    ws = o["wkvs"].reshape(2, HD, HP, DB, HD).transpose(3, 2, 0, 4, 1).reshape(1, DB, 8, HD, HD)
    c = np.ascontiguousarray
    return (c(y[:SEQ].reshape(1, SEQ, D)), c(y[SEQ:].reshape(DB, DT, D)),
            c(k[:SEQ].reshape(1, 1, SEQ, 8, HD)), c(v.reshape(1, 1, SEQ, 8, HD)), c(wp),
            c(tsh[0:1].reshape(1, 1, -1)), c(conv[0:1].reshape(1, 1, 2, -1)),
            c(k[SEQ:].reshape(1, DB, DT, 8, HD)), c(o["vs"].reshape(1, DB, DT, 8, HD)), c(ws),
            c(tsh[1:].reshape(1, DB, -1)), c(conv[1:].reshape(1, DB, 2, -1)))
```
